# Optimizing a Trainium2 kernel written in Bass

```python
import jax, jax.numpy as jnp
from jax import lax
import numpy as np

D_MODEL = 1024
BATCH = 1
SEQ = 1024
DEPTH = 1
DEC_BATCH = 1
DEC_SEQ = 64
PAST_LEN = 256

CHUNK = 64
D_ATTN = D_MODEL // 2
SB_HEADS = 8
SB_HEAD_DIM = D_ATTN // SB_HEADS
SB_BLOCK = 128
D_POOL = D_MODEL - D_ATTN
POOL_WINDOWS = (2, 4, 8, 16)
N_POOL_GROUPS = len(POOL_WINDOWS)
POOL_GROUP = D_POOL // N_POOL_GROUPS
POOL_HIST = max(POOL_WINDOWS) - 1
D_IN = 3 * D_ATTN + D_POOL
N_KEYS = 128
N_EXPERTS = N_KEYS * N_KEYS
PEER_HEADS = 8
PEER_TOPK = 16
PEER_KEY_DIM = 256
KEY_HALF = PEER_KEY_DIM // 2
PEER_BLOCK = 256
EPS = 1e-6

kernel_name = 'hybrid_stickbreak_pool_peer_stream_step'

def _rms(x, g):
    xf = x.astype(jnp.float32)
    y = xf * lax.rsqrt(jnp.mean(xf * xf, axis=-1, keepdims=True) + EPS)
    return (y * g.astype(jnp.float32)).astype(x.dtype)

def _sb_block(q, qpos, k, v, kpos):
    z = jnp.einsum('bqhd,bkhd->bhqk', q, k).astype(jnp.float32) * (SB_HEAD_DIM ** -0.5)
    mask = kpos[None, :] < qpos[:, None]
    log_1mb = jnp.where(mask, jax.nn.log_sigmoid(-z), 0.0)
    after = lax.cumsum(log_1mb, axis=3, reverse=True) - log_1mb
    w = jnp.where(mask, jnp.exp(jax.nn.log_sigmoid(z) + after), 0.0)
    return jnp.einsum('bhqk,bkhd->bqhd', w.astype(v.dtype), v)

def _stick_breaking(q, k_all, v_all, offset):
    B, L, H, Dh = q.shape
    kpos = jnp.arange(k_all.shape[1])
    qpos = offset + jnp.arange(L)
    if L <= SB_BLOCK:
        return _sb_block(q, qpos, k_all, v_all, kpos)
    nb = L // SB_BLOCK
    qb = q.reshape(B, nb, SB_BLOCK, H, Dh).transpose(1, 0, 2, 3, 4)
    pb = qpos.reshape(nb, SB_BLOCK)
    ob = lax.map(lambda a: _sb_block(a[0], a[1], k_all, v_all, kpos), (qb, pb))
    return ob.transpose(1, 0, 2, 3, 4).reshape(B, L, H, Dh)

def _multiscale_pool(p_hist, p, offset, w_pool, pool_scale):
    B, L, _ = p.shape
    xp = jnp.concatenate([p_hist.astype(jnp.float32), p.astype(jnp.float32)], axis=1)
    cs = jnp.concatenate([jnp.zeros((B, 1, D_POOL), jnp.float32), jnp.cumsum(xp, axis=1)], axis=1)
    pos = offset + jnp.arange(L)
    end = cs[:, POOL_HIST + 1:POOL_HIST + 1 + L]
    outs = []
    for g, w in enumerate(POOL_WINDOWS):
        sl = slice(g * POOL_GROUP, (g + 1) * POOL_GROUP)
        start = cs[:, POOL_HIST + 1 - w:POOL_HIST + 1 - w + L, sl]
        cnt = jnp.minimum(pos + 1, w).astype(jnp.float32)[None, :, None]
        outs.append((end[..., sl] - start) / cnt)
    pooled = jnp.concatenate(outs, axis=-1) - p.astype(jnp.float32)
    mixed = jnp.einsum('blgc,gcd->blgd', pooled.reshape(B, L, N_POOL_GROUPS, POOL_GROUP),
                       w_pool.astype(jnp.float32)).reshape(B, L, D_POOL)
    return (mixed * pool_scale.astype(jnp.float32)).astype(p.dtype)

def _peer(h, w_query, sub_keys, u_tab, v_tab):
    B, L, D = h.shape
    T = B * L
    nb = -(-T // PEER_BLOCK)
    hp = jnp.pad(h.reshape(T, D), ((0, nb * PEER_BLOCK - T), (0, 0))).reshape(nb, PEER_BLOCK, D)

    def one(hb):
        q = (hb @ w_query).reshape(PEER_BLOCK, PEER_HEADS, 2, KEY_HALF)
        s1 = jnp.einsum('thd,hkd->thk', q[:, :, 0], sub_keys[0]).astype(jnp.float32)
        s2 = jnp.einsum('thd,hkd->thk', q[:, :, 1], sub_keys[1]).astype(jnp.float32)
        v1, i1 = lax.top_k(s1, PEER_TOPK)
        v2, i2 = lax.top_k(s2, PEER_TOPK)
        ncand = PEER_TOPK * PEER_TOPK
        cand = (v1[..., :, None] + v2[..., None, :]).reshape(PEER_BLOCK, PEER_HEADS, ncand)
        cidx = (i1[..., :, None] * N_KEYS + i2[..., None, :]).reshape(PEER_BLOCK, PEER_HEADS, ncand)
        best, sel = lax.top_k(cand, PEER_TOPK)
        idx = jnp.take_along_axis(cidx, sel, axis=-1)
        gate = jax.nn.softmax(best, axis=-1)
        ug = jnp.take(u_tab, idx, axis=0)
        vg = jnp.take(v_tab, idx, axis=0)
        act = jax.nn.gelu(jnp.einsum('td,thkd->thk', hb, ug).astype(jnp.float32), approximate=False)
        return jnp.einsum('thk,thkd->td', (gate * act).astype(hb.dtype), vg)

    return lax.map(one, hp).reshape(nb * PEER_BLOCK, D)[:T].reshape(B, L, D)

def _layer(x, c, k_hist, v_hist, p_hist, w_ada, b_ada, g_pre1, g_post1, g_pre2, g_post2,
           w_in, g_out_a, g_out_b, w_pool, pool_scale, w_out, w_query, sub_keys, u_experts, v_experts):
    B, L, _ = x.shape
    offset = k_hist.shape[1]
    mod = (jax.nn.silu(c) @ w_ada + b_ada).reshape(B, 6, D_MODEL)[:, :, None, :]
    sh1, sc1, gt1, sh2, sc2, gt2 = (mod[:, i] for i in range(6))
    h = _rms(x, g_pre1) * (1 + sc1) + sh1
    z = h @ w_in
    q, k, v, p = jnp.split(z, [D_ATTN, 2 * D_ATTN, 3 * D_ATTN], axis=-1)
    q = q.reshape(B, L, SB_HEADS, SB_HEAD_DIM)
    k = k.reshape(B, L, SB_HEADS, SB_HEAD_DIM)
    v = v.reshape(B, L, SB_HEADS, SB_HEAD_DIM)
    k_all = jnp.concatenate([k_hist.astype(k.dtype), k], axis=1)
    v_all = jnp.concatenate([v_hist.astype(v.dtype), v], axis=1)
    o_a = _stick_breaking(q, k_all, v_all, offset).reshape(B, L, D_ATTN)
    o_b = _multiscale_pool(p_hist, p, offset, w_pool, pool_scale)
    o = jnp.concatenate([_rms(o_a, g_out_a), _rms(o_b, g_out_b)], axis=-1) @ w_out
    x = x + gt1 * _rms(o, g_post1)
    h2 = _rms(x, g_pre2) * (1 + sc2) + sh2
    x = x + gt2 * _rms(_peer(h2, w_query, sub_keys, u_experts, v_experts), g_post2)
    p_state = jnp.concatenate([p_hist.astype(p.dtype), p], axis=1)[:, -POOL_HIST:]
    return x, k, v, p_state

def setup_inputs(seed: int = 0) -> dict:
    key = jax.random.key(seed)
    ks = jax.random.split(key, 24)
    n = lambda i, shape: jax.random.normal(ks[i], shape, jnp.float32)
    return {
        'x_prompt': n(0, (BATCH, SEQ, D_MODEL)),
        'x_sample': n(1, (DEC_BATCH, DEC_SEQ, D_MODEL)),
        'cache_k': n(2, (DEPTH, DEC_BATCH, PAST_LEN, SB_HEADS, SB_HEAD_DIM)),
        'cache_v': n(3, (DEPTH, DEC_BATCH, PAST_LEN, SB_HEADS, SB_HEAD_DIM)),
        'state_pool': n(4, (DEPTH, DEC_BATCH, POOL_HIST, D_POOL)),
        'c_prompt': n(5, (BATCH, D_MODEL)),
        'c_sample': n(6, (DEC_BATCH, D_MODEL)),
        'w_ada': n(7, (DEPTH, D_MODEL, 6 * D_MODEL)) * (0.5 * D_MODEL ** -0.5),
        'b_ada': n(8, (DEPTH, 6 * D_MODEL)) * 0.01,
        'g_pre1': 1.0 + 0.05 * n(9, (DEPTH, D_MODEL)),
        'g_post1': 1.0 + 0.05 * n(10, (DEPTH, D_MODEL)),
        'g_pre2': 1.0 + 0.05 * n(11, (DEPTH, D_MODEL)),
        'g_post2': 1.0 + 0.05 * n(12, (DEPTH, D_MODEL)),
        'w_in': n(13, (DEPTH, D_MODEL, D_IN)) * D_MODEL ** -0.5,
        'g_out_a': 1.0 + 0.05 * n(14, (DEPTH, D_ATTN)),
        'g_out_b': 1.0 + 0.05 * n(15, (DEPTH, D_POOL)),
        'w_pool': n(16, (DEPTH, N_POOL_GROUPS, POOL_GROUP, POOL_GROUP)) * POOL_GROUP ** -0.5,
        'pool_scale': 1.0 + 0.1 * n(17, (DEPTH, D_POOL)),
        'w_out': n(18, (DEPTH, D_MODEL, D_MODEL)) * D_MODEL ** -0.5,
        'w_query': n(19, (DEPTH, D_MODEL, PEER_HEADS * PEER_KEY_DIM)) * D_MODEL ** -0.5,
        'sub_keys': n(20, (DEPTH, 2, PEER_HEADS, N_KEYS, KEY_HALF)) * KEY_HALF ** -0.5,
        'u_experts': n(21, (DEPTH, N_EXPERTS, D_MODEL)) * D_MODEL ** -0.5,
        'v_experts': n(22, (DEPTH, N_EXPERTS, D_MODEL)) * D_MODEL ** -0.5,
    }

def reference(x_prompt, x_sample, cache_k, cache_v, state_pool, c_prompt, c_sample, w_ada, b_ada,
              g_pre1, g_post1, g_pre2, g_post2, w_in, g_out_a, g_out_b, w_pool, pool_scale, w_out,
              w_query, sub_keys, u_experts, v_experts):
    y_p, y_s = x_prompt, x_sample
    bp = x_prompt.shape[0]
    kp_l, vp_l, pp_l, ks_l, vs_l, ps_l = [], [], [], [], [], []
    for l in range(DEPTH):
        wts = (w_ada[l], b_ada[l], g_pre1[l], g_post1[l], g_pre2[l], g_post2[l], w_in[l],
               g_out_a[l], g_out_b[l], w_pool[l], pool_scale[l], w_out[l], w_query[l],
               sub_keys[l], u_experts[l], v_experts[l])
        empty_kv = jnp.zeros((bp, 0, SB_HEADS, SB_HEAD_DIM), y_p.dtype)
        empty_pool = jnp.zeros((bp, POOL_HIST, D_POOL), y_p.dtype)
        y_p, kp, vp, pp = _layer(y_p, c_prompt, empty_kv, empty_kv, empty_pool, *wts)
        y_s, ks_new, vs_new, ps = _layer(y_s, c_sample, cache_k[l], cache_v[l], state_pool[l], *wts)
        kp_l.append(kp); vp_l.append(vp); pp_l.append(pp)
        ks_l.append(ks_new); vs_l.append(vs_new); ps_l.append(ps)
    return (y_p, y_s, jnp.stack(kp_l), jnp.stack(vp_l), jnp.stack(pp_l),
            jnp.stack(ks_l), jnp.stack(vs_l), jnp.stack(ps_l))


_drawn_inputs = setup_inputs


def setup_inputs(seed=0):
    import zlib

    import numpy as np

    out = dict(_drawn_inputs(seed))
    spreads = {}
    factors = {'cache_k': 3.035, 'g_post2': 4.098}
    for name, (base, spread) in spreads.items():
        noise = np.random.default_rng([zlib.crc32(name.encode()), seed]).standard_normal(out[name].shape)
        drawn = base * np.exp(spread * noise) if base else spread * noise
        out[name] = __import__('jax').numpy.asarray(drawn.astype(out[name].dtype))
    for name, factor in factors.items():
        out[name] = (out[name] * factor).astype(out[name].dtype)
    return out
```

```python
from contextlib import ExitStack

import concourse.bass as bass
from concourse import mybir

ALU = mybir.AluOpType
ACT = mybir.ActivationFunctionType
F32 = mybir.dt.float32
U32 = mybir.dt.uint32
AX_X = mybir.AxisListType.X

P = 128
D = 1024
SEQ = 1024
DEC = 64
PAST = 256
HD = 64
DA = 512
DPOOL = 512
NMOD = 6
EPS = 1e-6
KC = D // P
FA = DA // P
WINDOWS = (2, 4, 8, 16)
HIST = 15
PAD = 16
TOK = SEQ + DEC
NT = SEQ // P
NEXP = 128 * 128
PH = 8
TOPK = 16
NKEY = 128
SLOTS = PH * TOPK
RING = 8
DIAGS = 4
LOWEST = -3.0e38

C_ID, C_NTRI, C_NONES, C_MASK, C_IOTA, C_INVC = 0, 128, 256, 384, 512, 528
C_END = 528 + 64
G_PRE1, G_OUT, G_POOL = 0, 8, 16
G_END = 20

RANGES = [(0, 512), (512, 512), (SEQ, DEC)]
TILES = [(P * t, P) for t in range(NT)] + [(SEQ, DEC)]


class Chain:

    def __init__(self, eng, sem):
        self.eng, self.sem, self.base, self.n = eng, sem, 0, 0

    def add(self, ins):
        ins.then_inc(self.sem, 1)
        self.n += 1

    def wait(self):
        self.eng.wait_ge(self.sem, self.base + self.n)

    def link(self, ins):
        self.add(ins)
        self.wait()

    def link_apart(self, ins, passed):
        self.link(ins)
        self.eng.sem_inc(passed, 1)


def build(nc, A):
    with ExitStack() as outer:
        def sem(name):
            return outer.enter_context(nc.semaphore(name))

        def dram(name, shape):
            return nc.dram_tensor(name, shape, F32).ap()

        def sbuf(stack, name, shape, dt=F32):
            return stack.enter_context(nc.sbuf_tensor(name, shape, dt))

        S = {
            "sem": sem,
            "mod_d": dram("mod_d", [2, NMOD * D]),
            "qT_d": dram("qT_d", [DA, TOK]),
            "kT_d": dram("kT_d", [DA, TOK]),
            "x1_d": dram("x1_d", [TOK, D]),
            "h2_d": dram("h2_d", [TOK, D]),
            "const": sbuf(outer, "const", [P, C_END]),
            "gains": sbuf(outer, "gains", [P, G_END]),
        }
        late = outer.enter_context(ExitStack())
        with nc.sbuf_tensor("oT", [P, KC, TOK], F32, side="right") as S["oT"]:
            with ExitStack() as early:
                S["w_in"] = sbuf(early, "w_in_sb", [P, KC, 4 * DA])
                S["w_in_full"] = sem("w_in_full")
                modulation(nc, A, S)
                projection(nc, A, S)
            attention(nc, A, S)
            S["w_q"] = sbuf(late, "w_q_sb", [P, KC, 2 * D])
            S["keys"] = sbuf(late, "keys_sb", [P, 2 * PH, NKEY])
            S["w_q_full"] = sem("w_q_full")
            output(nc, A, S)
        experts(nc, A, S)


def modulation(nc, A, S):
    sem = S["sem"]
    CH = 512
    NCH = NMOD * D // CH
    ADA = 4
    with ExitStack() as st:
        sb = lambda n, s, d=F32: st.enter_context(nc.sbuf_tensor(n, s, d))
        ada = [sb(f"ada{i}", [P, KC, CH]) for i in range(ADA)]
        c_sb = sb("c_sb", [P, KC * 2])
        ec = sb("ec", [P, KC * 2])
        silu = sb("silu", [P, KC * 2])
        bias = sb("bias", [2, NMOD * D])
        psum = [st.enter_context(nc.psum_tensor(f"ps_mod{i}", [P, CH], F32)) for i in range(2)]
        ada_full = [sem(f"ada_full{i}") for i in range(ADA)]
        c_in, b_in, small_in, c_exp, c_silu = (sem(x) for x in ("c_in", "b_in", "small_in", "c_exp", "c_silu"))
        dve_own, mm_done, mod_done, mod_out = (sem(x) for x in ("dve_own0", "mod_mm", "mod_done", "mod_out"))
        block = st.enter_context(nc.Block())

        @block.sync
        def _(sp):
            sp.dma_start(c_sb[:, :], A["cT"][:, :]).then_inc(c_in, 16)
            sp.dma_start(bias[:, :], A["b_ada"].broadcast_to([2, NMOD * D])).then_inc(b_in, 16)
            ada_v = A["w_ada"].rearrange("(k p) n -> p k n", p=P)
            with sp.Fori(0, NCH // ADA) as i:
                for j in range(ADA):
                    sp.wait_ge(mod_done, i * ADA + (j + 1))
                    sp.dma_start(ada[j][:, :, :], ada_v[:, :, bass.ds(i * (ADA * CH) + j * CH, CH)])\
                        .then_inc(ada_full[j], 16)
            sp.wait_ge(mod_done, NCH + ADA)
            sp.dma_start(S["mod_d"][:, :], bias[:, :]).then_inc(mod_out, 16)
            sp.wait_ge(mod_out, 16)

        @block.scalar
        def _(act):
            act.dma_start(S["const"][:, :], A["const"][:, :]).then_inc(small_in, 16)
            act.dma_start(S["gains"][:, :], A["gains"][:, :]).then_inc(small_in, 16)
            act.wait_ge(c_in, 16)
            nc.scalar.activation(ec[:, :], c_sb[:, :], ACT.Exp, scale=-1.0).then_inc(c_exp, 1)
            act.wait_ge(small_in, 32)
            act.wait_ge(mod_done, NCH + ADA - 2)
            w_v = A["w_in"].rearrange("(k p) n -> p k n", p=P)
            for k in range(KC):
                act.dma_start(S["w_in"][:, k, :], w_v[:, k, :]).then_inc(S["w_in_full"], 16)

        @block.vector
        def _(dve):
            own = Chain(dve, dve_own)
            dve.sem_inc(mod_done, ADA)
            dve.wait_ge(c_exp, 1)
            own.link(nc.vector.tensor_scalar_add(ec[:, :], ec[:, :], 1.0))
            own.link(nc.vector.reciprocal(silu[:, :], ec[:, :]))
            nc.vector.tensor_tensor(silu[:, :], silu[:, :], c_sb[:, :], ALU.mult).then_inc(c_silu, 1)
            dve.wait_ge(b_in, 16)
            with dve.Fori(0, NCH // 2) as i:
                for j in range(2):
                    dve.wait_ge(mm_done, i * 2 + (j + 1))
                    at = bass.ds(i * (2 * CH) + j * CH, CH)
                    nc.vector.tensor_tensor(bias[:, at], psum[j][0:2, :], bias[:, at], ALU.add)\
                        .then_inc(mod_done, 1)

        @block.tensor
        def _(pe):
            pe.wait_ge(c_silu, 1)
            with pe.Fori(0, NCH // ADA) as i:
                for j in range(ADA):
                    pe.wait_ge(ada_full[j], i * 16 + 16)
                    pe.wait_ge(mod_done, i * ADA + (j + ADA - 1))
                    for k in range(KC):
                        last = nc.tensor.matmul(psum[j % 2][0:2, :], silu[:, 2 * k:2 * k + 2], ada[j][:, k, :],
                                                start=(k == 0), stop=(k == KC - 1))
                    last.then_inc(mm_done, 1)


def rstd_steps(nc, own, mean_sq, start, power, y, t, to_act, from_act):
    to_act()
    from_act()
    own.link(nc.vector.tensor_tensor(t, y, y, ALU.mult))
    own.link(nc.vector.tensor_tensor(t, t, mean_sq, ALU.mult))
    own.link(nc.vector.tensor_scalar(t, t, -0.5, 1.5, ALU.mult, ALU.add))
    own.link(nc.vector.tensor_tensor(y, y, t, ALU.mult))


def projection(nc, A, S):
    sem = S["sem"]
    const, gains, w_in, oT = S["const"], S["gains"], S["w_in"], S["oT"]
    ident = const[:, C_ID:C_ID + P]
    NTILE = len(TILES)
    jobs = [(kind, f, r) for kind in "kqp" for f in range(FA) for r in range(len(RANGES))]
    jobs += [("v", t, None) for t in range(NTILE)]
    NB = 3
    with ExitStack() as st:
        sb = lambda n, s, d=F32: st.enter_context(nc.sbuf_tensor(n, s, d))
        ps = lambda n: st.enter_context(nc.psum_tensor(n, [P, 512], F32))
        x = [sb(f"x{i}", [P, D]) for i in range(2)]
        xn = [sb(f"xn{i}", [P, D]) for i in range(2)]
        hT = sb("hT", [P, KC, TOK])
        stage = [sb(f"stage{i}", [P, 512]) for i in range(NB)]
        krow = [sb(f"krow{i}", [P, 4, P]) for i in range(2)]
        pT = sb("pT", [P, FA, PAD + SEQ])
        pTs = sb("pTs", [P, FA, PAD + DEC])
        sums = [sb(f"sums{i}", [P, PAD + SEQ]) for i in range(2)]
        w_pool = sb("w_pool_sb", [P, FA, P])
        prow = [sb(f"prow{i}", [HIST, DPOOL]) for i in range(2)]
        mcol = sb("mcol", [P, 2, 2, KC])
        acol = sb("acol", [P, 2, KC])
        msq = sb("msq1", [P, NTILE])
        rs = sb("rs1", [P, NTILE])
        tmp = sb("tmp1", [P, NTILE])
        ps_t = [ps(f"ps_t{i}") for i in range(2)]
        ps_z = [ps(f"ps_z{i}") for i in range(NB)]
        ps_k = [ps(f"ps_k{i}") for i in range(2)]
        x_full = [sem(f"x_full{i}") for i in range(2)]
        mcol_in, pool_in = sem("mcol_in"), sem("pool_in")
        sq_done, msq_done, y0_done, xn_done = (sem(n) for n in ("sq_done1", "msq_done1", "y0_done1", "xn_done"))
        act_own, dve_own = sem("act_own1"), sem("dve_own1")
        tr_done, hT_done = sem("tr_done1"), sem("hT_done")
        z_done, z_read = sem("z_done"), sem("z_read")
        stage_out = [sem(f"stage_out{i}") for i in range(NB)]
        k_tr, k_read, krow_out = sem("k_tr"), sem("k_read"), [sem(f"krow_out{i}") for i in range(2)]
        hist_clear = sem("hist_clear")
        pooled_done, mix_done, mix_read = sem("pooled_done"), sem("mix_done"), sem("mix_read")
        p_tr, p_read, prow_out = sem("p_tr"), sem("p_read"), sem("prow_out")
        block = st.enter_context(nc.Block())

        n_k = FA * len(RANGES)
        last_p = 3 * n_k
        def stores_before(j, b):
            return sum(1 for m in range(j) if m % NB == b and jobs[m][0] != "p")

        @block.sync
        def _(sp):
            for s in range(2):
                for m in range(2):
                    sp.dma_start(mcol[:, s, m, :], S["mod_d"][s, m * D:(m + 1) * D].rearrange("(k p) -> p k", p=P),
                                 allow_slow_non_contiguous=True).then_inc(mcol_in, 16)
            for t, (t0, rows) in enumerate(TILES):
                if t >= 2:
                    sp.wait_ge(xn_done, t - 1)
                src = A["x_p"][t0:t0 + rows, :] if t < NT else A["x_s"][:, :]
                sp.dma_start(x[t % 2][0:rows, :], src).then_inc(x_full[t % 2], 16)
            for j, (kind, f, r) in enumerate(jobs):
                if kind == "p":
                    continue
                sp.wait_ge(z_read, j + 1)
                if kind == "v":
                    t0, rows = TILES[f]
                    dst = A["v_p"][t0:t0 + rows, :] if f < NT else A["v_s"][:, :]
                    src = stage[j % NB][0:rows, :]
                else:
                    c0, n = RANGES[r]
                    dst = S["qT_d" if kind == "q" else "kT_d"][f * P:(f + 1) * P, c0:c0 + n]
                    src = stage[j % NB][:, 0:n]
                sp.dma_start(dst, src).then_inc(stage_out[j % NB], 16)
                if kind == "k":
                    sp.wait_ge(k_read, j + 1)
                    if r < 2:
                        dst = A["k_p"][c0:c0 + n, f * P:(f + 1) * P].rearrange("(t p) c -> p t c", p=P)
                        sp.dma_start(dst, krow[j % 2][:, :, :]).then_inc(krow_out[j % 2], 16)
                    else:
                        sp.dma_start(A["k_s"][:, f * P:(f + 1) * P], krow[j % 2][0:DEC, 0, :])\
                            .then_inc(krow_out[j % 2], 16)
            sp.wait_ge(p_read, 2)
            sp.dma_start(A["pool_p"][:, :], prow[0][:, :]).then_inc(prow_out, 16)
            sp.dma_start(A["pool_s"][:, :], prow[1][:, :]).then_inc(prow_out, 16)
            sp.wait_ge(prow_out, 32)
            for b in range(NB):
                sp.wait_ge(stage_out[b], 16 * stores_before(len(jobs), b))
            for b in range(2):
                sp.wait_ge(krow_out[b], 16 * (n_k // 2))

        @block.scalar
        def _(act):
            own = Chain(act, act_own)
            act.dma_start(w_pool[:, :, :], A["w_pool"].rearrange("g c d -> c g d")).then_inc(pool_in, 16)
            act.wait_ge(hist_clear, 1)
            act.dma_start(pTs[:, :, PAD - HIST:PAD], A["histT"][:, :, :]).then_inc(pool_in, 16)
            for t, (_, rows) in enumerate(TILES):
                b = t % 2
                act.wait_ge(x_full[b], 16 * (t // 2 + 1))
                if t >= 2:
                    act.wait_ge(tr_done, 2 * (t - 1))
                nc.scalar.activation(xn[b][0:rows, :], x[b][0:rows, :], ACT.Square,
                                     accum_out=msq[0:rows, t:t + 1]).then_inc(sq_done, 1)
                act.wait_ge(msq_done, t + 1)
                own.link(nc.scalar.activation(rs[0:rows, t:t + 1], msq[0:rows, t:t + 1], ACT.Ln))
                nc.scalar.activation(rs[0:rows, t:t + 1], rs[0:rows, t:t + 1], ACT.Exp, scale=-0.5)\
                    .then_inc(y0_done, 1)
            for j, (kind, f, r) in enumerate(jobs):
                act.wait_ge(z_done, j + 1)
                z = ps_z[j % NB]
                if kind == "p":
                    c0, n = RANGES[r]
                    dst = pT[:, f, PAD + c0:PAD + c0 + n] if r < 2 else pTs[:, f, PAD:PAD + DEC]
                    nc.scalar.activation(dst, z[:, 0:n], ACT.Copy).then_inc(z_read, 1)
                    continue
                if stores_before(j, j % NB):
                    act.wait_ge(stage_out[j % NB], 16 * stores_before(j, j % NB))
                if kind == "k" and j >= NB:
                    act.wait_ge(k_tr, j - NB + 1)
                elif kind == "q":
                    act.wait_ge(k_tr, n_k)
                if kind == "v":
                    rows = TILES[f][1]
                    nc.scalar.activation(stage[j % NB][0:rows, :], z[0:rows, :], ACT.Copy).then_inc(z_read, 1)
                else:
                    n = RANGES[r][1]
                    nc.scalar.activation(stage[j % NB][:, 0:n], z[:, 0:n], ACT.Copy,
                                         scale=(HD ** -0.5 if kind == "q" else 1.0)).then_inc(z_read, 1)
            for m, (g, r) in enumerate((g, r) for g in range(FA) for r in range(len(RANGES))):
                c0, n = RANGES[r]
                act.wait_ge(mix_done, m + 1)
                nc.scalar.activation(oT[:, FA + g, c0:c0 + n], ps_k[m % 2][:, 0:n], ACT.Copy,
                                     scale=gains[:, G_POOL + g:G_POOL + g + 1]).then_inc(mix_read, 1)

        @block.vector
        def _(dve):
            own = Chain(dve, dve_own)
            nc.vector.memset(pTs[:, :, 0:PAD], 0.0).then_inc(hist_clear, 1)
            own.add(nc.vector.memset(pT[:, :, 0:PAD], 0.0))
            dve.wait_ge(mcol_in, 64)
            for s in range(2):
                own.link(nc.vector.tensor_scalar_add(acol[:, s, :], mcol[:, s, 1, :], 1.0))
                own.link(nc.vector.tensor_tensor(acol[:, s, :], acol[:, s, :], gains[:, G_PRE1:G_PRE1 + KC], ALU.mult))

            def finish_tile(t):
                rows, t0 = TILES[t][1], TILES[t][0]
                s = 0 if t < NT else 1
                for half in range(2):
                    dve.wait_ge(tr_done, 2 * t + half + 1)
                    for q in range(4):
                        k = 4 * half + q
                        last = nc.vector.tensor_scalar(hT[:, k, t0:t0 + rows], ps_t[half][:, q * P:q * P + rows],
                                                       acol[:, s, k:k + 1], mcol[:, s, 0, k:k + 1], ALU.mult, ALU.add)
                    last.then_inc(hT_done, 1)

            for t, (_, rows) in enumerate(TILES):
                col = slice(t, t + 1)
                dve.wait_ge(sq_done, t + 1)
                nc.vector.tensor_scalar(msq[0:rows, col], msq[0:rows, col], 1.0 / D, EPS, ALU.mult, ALU.add)\
                    .then_inc(msq_done, 1)
                if t:
                    finish_tile(t - 1)
                dve.wait_ge(msq_done, t + 1)
                rstd_steps(nc, own, msq[0:rows, col], None, None, rs[0:rows, col], tmp[0:rows, col],
                           lambda: None, lambda: dve.wait_ge(y0_done, t + 1))
                nc.vector.tensor_scalar(xn[t % 2][0:rows, :], x[t % 2][0:rows, :], rs[0:rows, col], None, ALU.mult)\
                    .then_inc(xn_done, 1)
            finish_tile(NTILE - 1)
            for j in range(n_k):
                r = jobs[j][2]
                dve.wait_ge(k_tr, j + 1)
                if j >= 2:
                    dve.wait_ge(krow_out[j % 2], 16 * (j // 2))
                if r < 2:
                    nc.vector.tensor_copy(krow[j % 2][:, :, :], ps_k[j % 2][:, :].rearrange("p (t c) -> p t c", t=4))\
                        .then_inc(k_read, 1)
                else:
                    nc.vector.tensor_copy(krow[j % 2][0:DEC, 0, :], ps_k[j % 2][0:DEC, 0:P]).then_inc(k_read, 1)
            for s in range(2):
                dve.wait_ge(p_tr, s + 1)
                nc.vector.tensor_copy(prow[s][:, :], ps_t[s][0:HIST, :]).then_inc(p_read, 1)
            dve.wait_ge(pool_in, 32)
            for g, w in enumerate(WINDOWS):
                for s, (src, n) in enumerate(((pT, SEQ), (pTs, DEC))):
                    full = PAD + n
                    at, cur = src[:, g, :], None
                    for level in range(g + 1):
                        step = 1 << level
                        lo = 2 * step - 1
                        new = sums[level % 2]
                        own.link(nc.vector.tensor_tensor(new[:, lo:full], at[:, lo:full], at[:, lo - step:full - step],
                                                         ALU.add))
                        at = new
                    src_g = src[:, g, PAD:full]
                    if s == 0:
                        inv = const[:, C_INVC + 16 * g:C_INVC + 16 * (g + 1)]
                        own.link(nc.vector.tensor_tensor(at[:, PAD:PAD + 16], at[:, PAD:PAD + 16], inv, ALU.mult))
                        own.link(nc.vector.tensor_tensor(src_g[:, 0:16], at[:, PAD:PAD + 16], src_g[:, 0:16],
                                                         ALU.subtract))
                        own.link(nc.vector.scalar_tensor_tensor(out=src_g[:, 16:n], in0=at[:, PAD + 16:full],
                                                                scalar=1.0 / w, in1=src_g[:, 16:n], op0=ALU.mult,
                                                                op1=ALU.subtract))
                    else:
                        own.link(nc.vector.scalar_tensor_tensor(out=src_g[:, :], in0=at[:, PAD:full], scalar=1.0 / w,
                                                                in1=src_g[:, :], op0=ALU.mult, op1=ALU.subtract))
                dve.sem_inc(pooled_done, 1)

        @block.tensor
        def _(pe):
            for t, (_, rows) in enumerate(TILES):
                pe.wait_ge(xn_done, t + 1)
                for half in range(2):
                    if t:
                        pe.wait_ge(hT_done, 2 * (t - 1) + half + 1)
                    for q in range(4):
                        k = 4 * half + q
                        last = nc.tensor.transpose(ps_t[half][:, q * P:q * P + rows], xn[t % 2][0:rows, k * P:(k + 1) * P],
                                                   ident[0:rows, 0:rows])
                    last.then_inc(tr_done, 1)
            pe.wait_ge(hT_done, 2 * NTILE)
            pe.wait_ge(S["w_in_full"], 16 * KC)

            def key_rows(j):
                n = RANGES[jobs[j][2]][1]
                pe.wait_ge(z_read, j + 1)
                if j >= 2:
                    pe.wait_ge(k_read, j - 1)
                for i in range(-(-n // P)):
                    m = min(P, n - i * P)
                    last = nc.tensor.transpose(ps_k[j % 2][0:m, i * P:(i + 1) * P], stage[j % NB][:, i * P:i * P + m],
                                               ident)
                last.then_inc(k_tr, 1)

            for j, (kind, f, r) in enumerate(jobs):
                if j >= NB:
                    pe.wait_ge(z_read, j - NB + 1)
                z = ps_z[j % NB]
                for k in range(KC):
                    if kind == "v":
                        t0, rows = TILES[f]
                        last = nc.tensor.matmul(z[0:rows, :], hT[:, k, t0:t0 + rows], w_in[:, k, 2 * DA:3 * DA],
                                                start=(k == 0), stop=(k == KC - 1))
                    else:
                        c0, n = RANGES[r]
                        w0 = {"q": 0, "k": DA, "p": 3 * DA}[kind] + f * P
                        last = nc.tensor.matmul(z[:, 0:n], w_in[:, k, w0:w0 + P], hT[:, k, c0:c0 + n],
                                                start=(k == 0), stop=(k == KC - 1))
                last.then_inc(z_done, 1)
                if 1 <= j <= n_k:
                    key_rows(j - 1)
                if j == last_p:
                    pe.wait_ge(z_read, last_p)
                    for s, (src, n) in enumerate(((pT, SEQ), (pTs, DEC))):
                        for g in range(FA):
                            last = nc.tensor.transpose(ps_t[s][0:HIST, g * P:(g + 1) * P],
                                                       src[:, g, PAD + n - HIST:PAD + n], ident)
                        last.then_inc(p_tr, 1)
            pe.wait_ge(pool_in, 32)
            m = 0
            for g in range(FA):
                pe.wait_ge(pooled_done, g + 1)
                for r, (c0, n) in enumerate(RANGES):
                    pe.wait_ge(mix_read, m - 1) if m >= 2 else pe.wait_ge(k_read, n_k)
                    src = pT[:, g, PAD + c0:PAD + c0 + n] if r < 2 else pTs[:, g, PAD:PAD + DEC]
                    nc.tensor.matmul(ps_k[m % 2][:, 0:n], w_pool[:, g, :], src, start=True, stop=True)\
                        .then_inc(mix_done, 1)
                    m += 1


def attention(nc, A, S):
    sem = S["sem"]
    const, oT = S["const"], S["oT"]
    ntri, nones = const[:, C_NTRI:C_NTRI + P], const[:, C_NONES:C_NONES + P]
    mask = const[:, C_MASK:C_MASK + P]
    NZ, NS, NR, AHEAD = 4, 4, 3, 2
    LEAD = 4
    units = []
    for qc in range(2):
        top = 4 * qc + 3
        for kb in range(top, -1, -1):
            c0 = max(0, kb * P - qc * 512)
            for h in range(2):
                units.append(dict(h=h, bank=qc, kb=kb, c0=c0, c1=512, first=kb == top, diag=kb >= 4 * qc,
                                  last=kb == 0, opens=kb == top and h == 0, closes=kb == 0 and h == 1))
    for kb in (2, 1, 0):
        units.append(dict(h=2, bank=2, kb=kb, c0=0, c1=P, first=kb == 2, diag=kb == 2, last=kb == 0,
                          opens=kb == 2, closes=kb == 0))
    NU = len(units)
    seen = {0: 0, 1: 0, 2: 0}
    for u in units:
        if u["first"]:
            seen[u["h"]] = 0
        u["par"] = seen[u["h"]] % NR
        seen[u["h"]] += 1
    ND = sum(u["diag"] for u in units)
    for m, u in enumerate(units):
        u["nd"] = sum(v["diag"] for v in units[:m])
    PAIRS = FA
    with ExitStack() as st:
        sb = lambda n, s, d=F32: st.enter_context(nc.sbuf_tensor(n, s, d))
        ps = lambda n: st.enter_context(nc.psum_tensor(n, [P, 512], F32))
        kT = [sb(f"kT{i}", [P, SEQ]) for i in range(2)]
        kTs = [sb(f"kTs{i}", [P, 3 * P]) for i in range(2)]
        qz = [sb(f"qz{i}", [P, 2, SEQ]) for i in range(2)]
        qzs = [sb(f"qzs{i}", [P, P]) for i in range(2)]
        vz = [sb(f"vz{i}", [P, 2, NT, P]) for i in range(2)]
        vzs = [sb(f"vzs{i}", [P, 2, 3, P]) for i in range(2)]
        lt = [sb(f"lt{i}", [P, 512]) for i in range(NS)]
        spt = [sb(f"spt{i}", [P, 512]) for i in range(NS)]
        wt = [sb(f"wt{i}", [P, 512]) for i in range(NS)]
        R = [[sb(f"R{h}{i}", [P, 512]) for i in range(NR)] for h in range(3)]
        ps_z = [ps(f"ps_s{i}") for i in range(NZ)]
        ps_o = [ps(f"ps_o{i}") for i in range(3)]
        cleared = sem("att_cleared")
        full = [sem(f"att_full{i}") for i in range(2)]
        z_done, l_done, sp_done, r_done, t_done, e_done, w_done, pv_done, o_read = (
            sem(n) for n in ("att_z", "att_l", "att_sp", "att_r", "att_t", "att_e", "att_w", "att_pv", "att_o"))
        act_own = sem("act_own2")
        dve_own = sem("dve_own2")
        NLOAD = 15
        block = st.enter_context(nc.Block())

        def seqs(i, b):
            return i * (2 * NU) + b * NU

        @block.sync
        def _(sp):
            sp.wait_ge(cleared, 1)

            def load(pair, b):
                f0 = pair * P

                def go(dst, src):
                    sp.dma_start(dst, src).then_inc(full[b], 16)

                rows = bass.ds(f0, P)
                go(kT[b][:, :], S["kT_d"][rows, 0:SEQ])
                go(kTs[b][:, 0:PAST], A["kpastT"][rows, :])
                go(kTs[b][:, PAST:PAST + DEC], S["kT_d"][rows, SEQ:TOK])
                for h in range(2):
                    hr = slice(h * HD, (h + 1) * HD)
                    hrow = bass.ds(f0 + h * HD, HD)
                    go(qz[b][hr, h, :], S["qT_d"][hrow, 0:SEQ])
                    go(qzs[b][hr, hr], S["qT_d"][hrow, SEQ:TOK])
                    for half in range(2):
                        part = slice(half * NT // 2, (half + 1) * NT // 2)
                        go(vz[b][:, h, part, hr],
                           A["v_p"][half * SEQ // 2:(half + 1) * SEQ // 2, hrow].rearrange("(t p) c -> p t c", p=P))
                    go(vzs[b][:, h, 0:2, hr], A["vpast"][:, hrow].rearrange("(t p) c -> p t c", p=P))
                    go(vzs[b][0:DEC, h, 2, hr], A["v_s"][:, hrow])

            load(0, 0)
            load(1, 1)
            for b in range(2):
                sp.wait_ge(pv_done, LEAD + (b + 1) * NU)
                load(2 + b, b)

        @block.gpsimd
        def _(pool):
            for b in range(2):
                nc.gpsimd.memset(kTs[b][:, :], 0.0)
                nc.gpsimd.memset(qz[b][:, :, :], 0.0)
                nc.gpsimd.memset(qzs[b][:, :], 0.0)
                nc.gpsimd.memset(vz[b][:, :, :, :], 0.0)
                last = nc.gpsimd.memset(vzs[b][:, :, :, :], 0.0)
            last.then_inc(cleared, 1)

        @block.tensor
        def _(pe):
            pe.sem_inc(t_done, LEAD)
            pe.sem_inc(pv_done, LEAD)
            with pe.Fori(0, PAIRS // 2) as i:
                for b in range(2):
                    n0 = seqs(i, b)
                    pe.wait_ge(full[b], i * (16 * NLOAD) + 16 * NLOAD)

                    def score(m):
                        u = units[m]
                        pe.wait_ge(e_done, n0 + (LEAD + m - NZ + 1))
                        z = ps_z[m % NZ]
                        if u["h"] == 2:
                            lhsT, rhs = kTs[b][:, u["kb"] * P:(u["kb"] + 1) * P], qzs[b][:, :]
                        else:
                            q0 = u["bank"] * 512 + u["c0"]
                            lhsT = kT[b][:, u["kb"] * P:(u["kb"] + 1) * P]
                            rhs = qz[b][:, u["h"], q0:(u["bank"] + 1) * 512]
                        nc.tensor.matmul(z[:, u["c0"]:u["c1"]], lhsT, rhs, start=True, stop=True,
                                         skip_group_check=True).then_inc(z_done, 1)

                    def after(m):
                        u = units[m]
                        z, c0, c1 = ps_z[m % NZ], u["c0"], u["c1"]
                        pe.wait_ge(sp_done, n0 + (LEAD + m + 1))
                        last = nc.tensor.matmul(z[:, c0:c1], ntri, spt[m % NS][:, c0:c1], start=False, stop=True,
                                                skip_group_check=True)
                        if not u["first"]:
                            lo = c0 + P if u["diag"] and u["h"] < 2 else c0
                            last = nc.tensor.matmul(z[:, lo:c1], nones, R[u["h"]][(u["par"] - 1) % NR][:, lo:c1],
                                                    start=False, stop=True, skip_group_check=True)
                        last.then_inc(t_done, 1)

                    def values(m):
                        u = units[m]
                        pe.wait_ge(e_done, n0 + (LEAD + m + 1))
                        if u["diag"]:
                            pe.wait_ge(w_done, i * (2 * ND) + (b * ND + u["nd"] + 1))
                        if u["opens"]:
                            pe.wait_ge(o_read, i * 6 + (3 * b + u["bank"] + 1))
                        o, c0, c1, w = ps_o[u["bank"]], u["c0"], u["c1"], wt[m % NS]
                        if u["h"] == 2:
                            for h in range(2):
                                last = nc.tensor.matmul(o[:, 0:DEC], vzs[b][:, h, u["kb"], :],
                                                        w[:, h * DEC:(h + 1) * DEC], start=u["opens"] and h == 0,
                                                        stop=u["closes"] and h == 1, skip_group_check=True)
                        else:
                            last = nc.tensor.matmul(o[:, c0:c1], vz[b][:, u["h"], u["kb"], :], w[:, c0:c1],
                                                    start=u["opens"], stop=u["closes"], skip_group_check=True)
                        last.then_inc(pv_done, 1)

                    for m in range(AHEAD):
                        score(m)
                    for m in range(NU):
                        if m + AHEAD < NU:
                            score(m + AHEAD)
                        after(m)
                        if m >= AHEAD:
                            values(m - AHEAD)
                    for m in range(NU - AHEAD, NU):
                        values(m)

        @block.scalar
        def _(act):
            own = Chain(act, act_own)
            PER = 2 * 2 * NU
            act.sem_inc(e_done, LEAD)
            with act.Fori(0, PAIRS // 2) as i:
                own.base, own.n = i * PER, 0
                for b in range(2):
                    n0 = seqs(i, b)

                    def logs(m):
                        u = units[m]
                        c = slice(u["c0"], u["c1"])
                        act.wait_ge(z_done, n0 + (m + 1))
                        act.wait_ge(sp_done, n0 + (LEAD + m - NS + 1))
                        own.link(nc.scalar.activation(lt[m % NS][:, c], ps_z[m % NZ][:, c], ACT.Abs))
                        own.link(nc.scalar.activation(lt[m % NS][:, c], lt[m % NS][:, c], ACT.Exp, scale=-1.0))
                        nc.scalar.activation(lt[m % NS][:, c], lt[m % NS][:, c], ACT.Ln, bias=1.0).then_inc(l_done, 1)

                    def weights(m):
                        u = units[m]
                        c = slice(u["c0"], u["c1"])
                        act.wait_ge(t_done, n0 + (LEAD + m + 1))
                        act.wait_ge(pv_done, n0 + (LEAD + m - NS + 1))
                        nc.scalar.activation(wt[m % NS][:, c], ps_z[m % NZ][:, c], ACT.Exp).then_inc(e_done, 1)

                    for m in range(AHEAD):
                        logs(m)
                    for m in range(NU):
                        if m + AHEAD < NU:
                            logs(m + AHEAD)
                        weights(m)
                assert own.n == PER

        @block.vector
        def _(dve):
            own = Chain(dve, dve_own)
            dve.sem_inc(o_read, 3)
            dve.sem_inc(sp_done, LEAD)
            PER = 2 * sum(1 + u["diag"] for u in units)
            with dve.Fori(0, PAIRS // 2) as i:
                own.base, own.n = i * PER, 0
                for b in range(2):
                    n0 = seqs(i, b)

                    def masked(tile, u):
                        if u["h"] == 2:
                            at = tile[:, 0:P].rearrange("p (h q) -> p h q", h=2)
                            by = mask[:, None, 0:DEC].broadcast_to([P, 2, DEC])
                        else:
                            at, by = tile[:, u["c0"]:u["c0"] + P], mask
                        return nc.vector.tensor_tensor(at, at, by, ALU.mult)

                    def softplus(m):
                        u = units[m]
                        c = slice(u["c0"], u["c1"])
                        dve.wait_ge(l_done, n0 + (m + 1))
                        dve.wait_ge(t_done, n0 + (LEAD + m - NS + 1))
                        op = nc.vector.scalar_tensor_tensor(out=spt[m % NS][:, c], in0=ps_z[m % NZ][:, c], scalar=0.0,
                                                            in1=lt[m % NS][:, c], op0=ALU.max, op1=ALU.add)
                        own.link(op)
                        if u["diag"]:
                            own.link(masked(spt[m % NS], u))
                        if u["h"] == 2 and not u["last"]:
                            dve.wait_ge(t_done, n0 + (LEAD + m - 1))
                        if not u["last"]:
                            new, old = R[u["h"]][u["par"]], R[u["h"]][(u["par"] - 1) % NR]
                            lo = u["c0"] + P if u["diag"] and u["h"] < 2 else u["c0"]
                            if u["first"]:
                                nc.vector.tensor_copy(new[:, c], spt[m % NS][:, c]).then_inc(r_done, 1)
                            else:
                                if lo > u["c0"]:
                                    nc.vector.tensor_copy(new[:, u["c0"]:lo], spt[m % NS][:, u["c0"]:lo])
                                nc.vector.tensor_tensor(new[:, lo:u["c1"]], old[:, lo:u["c1"]],
                                                        spt[m % NS][:, lo:u["c1"]], ALU.add).then_inc(r_done, 1)
                        else:
                            dve.sem_inc(r_done, 1)
                        dve.wait_ge(r_done, n0 + (m + 1))
                        dve.sem_inc(sp_done, 1)

                    def finish(m):
                        u = units[m]
                        if not u["diag"]:
                            return
                        dve.wait_ge(e_done, n0 + (LEAD + m + 1))
                        masked(wt[m % NS], u).then_inc(w_done, 1)

                    def read(m):
                        u = units[m]
                        if u["closes"]:
                            dve.wait_ge(pv_done, n0 + (LEAD + m + 1))
                            c0, n = RANGES[u["bank"]]
                            nc.vector.tensor_copy(oT[:, bass.ds(i * 2 + b, 1), c0:c0 + n],
                                                  ps_o[u["bank"]][:, None, 0:n]).then_inc(o_read, 1)

                    for m in range(AHEAD):
                        softplus(m)
                    for m in range(NU):
                        if m + AHEAD < NU:
                            softplus(m + AHEAD)
                        finish(m)
                        if m >= 4:
                            read(m - 4)
                    for m in range(NU - 4, NU):
                        read(m)
                assert own.n == PER, (own.n, PER)


def output(nc, A, S):
    sem = S["sem"]
    const, gains = S["const"], S["gains"]
    oT = S["oT"]
    NTILE = len(TILES)
    with ExitStack() as st:
        sb = lambda n, s, d=F32: st.enter_context(nc.sbuf_tensor(n, s, d))
        w_out = sb("w_out_sb", [P, KC, D])
        g1 = sb("g1", [P, D])
        a2 = sb("a2", [P, D])
        b2 = sb("b2", [P, D])
        gpost = sb("gpost", [P, D])
        gpre = sb("gpre", [P, D])
        xt = [sb(f"xo{i}", [P, D]) for i in range(2)]
        ot = sb("ot", [P, D])
        junk = sb("junk3", [P, D])
        h2 = [sb(f"h2o{i}", [P, D]) for i in range(2)]
        sq = sb("sq3", [P, KC, P])
        part = sb("part", [P, 512])
        msq = sb("msq3", [P, 4])
        rs = sb("rs3", [P, 4])
        tmp = sb("tmp3", [P, 4])
        ones = sb("ones3", [P, 1])
        ps_a = [st.enter_context(nc.psum_tensor(f"ps_a{i}", [P, 512], F32)) for i in range(3)]
        ps_b = [st.enter_context(nc.psum_tensor(f"ps_b{i}", [P, 512], F32)) for i in range(3)]
        ps_n = st.enter_context(nc.psum_tensor("ps_n", [P, 512], F32))
        w_full, vec_full, vec2_full = sem("w_out_full"), sem("vec_full"), sem("vec2_full")
        x_full = [sem(f"xo_full{i}") for i in range(2)]
        w_scaled, sq_done, n_done, ab_done, ab_read = (sem(n) for n in ("w_scaled", "sq_done3", "n_done", "ab_done",
                                                                        "ab_read"))
        ask, answer, sqr, act_own, dve_own = (sem(n) for n in ("ask3", "answer3", "sqr3", "act_own3", "dve_own3"))
        x1_done, h2_done, vec_used = sem("x1_done"), sem("h2_done"), sem("vec_used")
        rows_out = [sem(f"rows_out{i}") for i in range(2)]
        block = st.enter_context(nc.Block())

        def vectors(eng, s, done):
            for dst, m in ((g1, 2), (b2, 3), (a2, 4)):
                eng.dma_start(dst[:, :], S["mod_d"][s:s + 1, m * D:(m + 1) * D].broadcast_to([P, D])).then_inc(done, 16)

        def store(sp, t):
            t0, rows = TILES[t]
            sp.wait_ge(h2_done, t + 1)
            sp.dma_start(S["x1_d"][t0:t0 + rows, :], xt[t % 2][0:rows, :]).then_inc(rows_out[t % 2], 16)
            sp.dma_start(S["h2_d"][t0:t0 + rows, :], h2[t % 2][0:rows, :]).then_inc(rows_out[t % 2], 16)

        @block.sync
        def _(sp):
            w_v = A["w_out"].rearrange("(k p) n -> p k n", p=P)
            for k in range(KC):
                sp.dma_start(w_out[:, k, :], w_v[:, k, :]).then_inc(w_full, 16)
            sp.dma_start(gpost[:, :], A["rows"][0:1, :].broadcast_to([P, D])).then_inc(vec_full, 16)
            sp.dma_start(gpre[:, :], A["rows"][1:2, :].broadcast_to([P, D])).then_inc(vec_full, 16)
            vectors(sp, 0, vec_full)
            for t, (t0, rows) in enumerate(TILES):
                b = t % 2
                if t >= 2:
                    sp.wait_ge(rows_out[b], 32 * (t // 2))
                src = A["x_p"][t0:t0 + rows, :] if t < NT else A["x_s"][:, :]
                sp.dma_start(xt[b][0:rows, :], src).then_inc(x_full[b], 16)
                if t >= 1:
                    store(sp, t - 1)
                if t == NT:
                    sp.wait_ge(h2_done, NT)
                    vectors(sp, 1, vec2_full)
            store(sp, NT)
            sp.wait_ge(rows_out[0], 32 * 5)
            sp.wait_ge(rows_out[1], 32 * 4)

        @block.scalar
        def _(act):
            w_v = A["w_query"].rearrange("(k p) n -> p k n", p=P)
            for k in range(KC):
                act.dma_start(S["w_q"][:, k, :], w_v[:, k, :]).then_inc(S["w_q_full"], 16)
            act.dma_start(S["keys"][:, :, :], A["keysT"][:, :, :]).then_inc(S["w_q_full"], 16)
            own = Chain(act, act_own)
            asked = [0]

            def roots(rows, cols):
                asked[0] += 1
                act.wait_ge(ask, asked[0])
                own.link(nc.scalar.activation(rs[0:rows, cols], msq[0:rows, cols], ACT.Ln))
                nc.scalar.activation(rs[0:rows, cols], rs[0:rows, cols], ACT.Exp, scale=-0.5).then_inc(answer, 1)

            for t, (t0, rows) in enumerate(TILES):
                if t:
                    act.wait_ge(n_done, t)
                nc.scalar.activation(sq[:, :, 0:rows], oT[:, :, t0:t0 + rows], ACT.Square).then_inc(sq_done, 1)
                roots(rows, slice(0, 2))
                for m, (src, seen) in enumerate(((ot, ab_read), (xt[t % 2], x1_done))):
                    act.wait_ge(seen, 2 * (t + 1) if m == 0 else t + 1)
                    nc.scalar.activation(junk[0:rows, :], src[0:rows, :], ACT.Square,
                                         accum_out=msq[0:rows, 2 + m:3 + m]).then_inc(sqr, 1)
                    act.wait_ge(sqr, 2 * t + m + 1)
                    roots(rows, slice(2 + m, 3 + m))

        @block.vector
        def _(dve):
            own = Chain(dve, dve_own)
            own.add(nc.vector.memset(ones[:, :], 1.0))
            dve.wait_ge(w_full, 16 * KC)
            for k in range(KC):
                last = nc.vector.tensor_scalar(w_out[:, k, :], w_out[:, k, :], gains[:, G_OUT + k:G_OUT + k + 1], None,
                                               ALU.mult)
            own.wait()
            last.then_inc(w_scaled, 1)

            def prepare():
                own.link(nc.vector.tensor_tensor(g1[:, :], g1[:, :], gpost[:, :], ALU.mult))
                own.link(nc.vector.scalar_tensor_tensor(out=a2[:, :], in0=a2[:, :], scalar=1.0, in1=gpre[:, :],
                                                        op0=ALU.add, op1=ALU.mult))

            dve.wait_ge(vec_full, 16 * 5)
            prepare()
            asked = [0]

            def root(rows, cols, src, n):
                asked[0] += 1
                own.link(nc.vector.tensor_scalar(msq[0:rows, cols], src, 1.0 / n, EPS, ALU.mult, ALU.add))
                rstd_steps(nc, own, msq[0:rows, cols], None, None, rs[0:rows, cols], tmp[0:rows, cols],
                           lambda: dve.sem_inc(ask, 1), lambda: dve.wait_ge(answer, asked[0]))

            for t, (t0, rows) in enumerate(TILES):
                b = t % 2
                if t == NT:
                    dve.wait_ge(vec2_full, 48)
                    prepare()
                dve.wait_ge(n_done, t + 1)
                root(rows, slice(0, 2), ps_n[0:rows, 2 * t:2 * t + 2], DA)
                for half in range(2):
                    j = 2 * t + half
                    dve.wait_ge(ab_done, j + 1)
                    own.link(nc.vector.tensor_scalar(part[0:rows, :], ps_a[j % 3][0:rows, :], rs[0:rows, 0:1], None,
                                                     ALU.mult))
                    nc.vector.scalar_tensor_tensor(out=ot[0:rows, 512 * half:512 * (half + 1)], in0=ps_b[j % 3][0:rows, :],
                                                   scalar=rs[0:rows, 1:2], in1=part[0:rows, :], op0=ALU.mult,
                                                   op1=ALU.add).then_inc(ab_read, 1)
                    dve.wait_ge(ab_read, j + 1)
                dve.wait_ge(sqr, 2 * t + 1)
                root(rows, slice(2, 3), msq[0:rows, 2:3], D)
                own.link(nc.vector.scalar_tensor_tensor(out=ot[0:rows, :], in0=ot[0:rows, :], scalar=rs[0:rows, 2:3],
                                                        in1=g1[0:rows, :], op0=ALU.mult, op1=ALU.mult))
                dve.wait_ge(x_full[b], 16 * (t // 2 + 1))
                nc.vector.tensor_tensor(xt[b][0:rows, :], xt[b][0:rows, :], ot[0:rows, :], ALU.add).then_inc(x1_done, 1)
                dve.wait_ge(sqr, 2 * t + 2)
                root(rows, slice(3, 4), msq[0:rows, 3:4], D)
                if t >= 2:
                    dve.wait_ge(rows_out[b], 32 * (t // 2))
                dve.wait_ge(x1_done, t + 1)
                own.link(nc.vector.scalar_tensor_tensor(out=h2[b][0:rows, :], in0=xt[b][0:rows, :],
                                                        scalar=rs[0:rows, 3:4], in1=a2[0:rows, :], op0=ALU.mult,
                                                        op1=ALU.mult))
                nc.vector.tensor_tensor(h2[b][0:rows, :], h2[b][0:rows, :], b2[0:rows, :], ALU.add).then_inc(h2_done, 1)

        @block.tensor
        def _(pe):
            pe.wait_ge(w_scaled, 1)
            for t, (t0, rows) in enumerate(TILES):
                pe.wait_ge(sq_done, t + 1)
                for m in range(2):
                    for f in range(FA):
                        last = nc.tensor.matmul(ps_n[0:rows, 2 * t + m:2 * t + m + 1], sq[:, FA * m + f, 0:rows],
                                                ones[:, :], start=(f == 0), stop=(f == FA - 1), skip_group_check=True)
                last.then_inc(n_done, 1)
                for half in range(2):
                    j = 2 * t + half
                    if j >= 3:
                        pe.wait_ge(ab_read, j - 2)
                    for m, bank in enumerate((ps_a[j % 3], ps_b[j % 3])):
                        for f in range(FA):
                            last = nc.tensor.matmul(bank[0:rows, :], oT[:, FA * m + f, t0:t0 + rows],
                                                    w_out[:, FA * m + f, 512 * half:512 * (half + 1)],
                                                    start=(f == 0), stop=(f == FA - 1))
                    last.then_inc(ab_done, 1)


def experts(nc, A, S):
    sem = S["sem"]
    const = S["const"]
    ident, iota = const[:, C_ID:C_ID + P], const[:, C_IOTA:C_IOTA + TOPK]
    w_q, keys = S["w_q"], S["keys"]
    with ExitStack() as st:
        sb = lambda n, s, d=F32: st.enter_context(nc.sbuf_tensor(n, s, d))
        ps = lambda n, w=512: st.enter_context(nc.psum_tensor(n, [P, w], F32))
        urow = [sb(f"urow{i}", [P, D]) for i in range(RING)]
        vrow = [sb(f"vrow{i}", [P, D]) for i in range(RING)]
        diag = [sb(f"diag{i}", [P, P]) for i in range(DIAGS)]
        h2n = sb("h2n", [P, D])
        h2T = sb("h2T", [P, KC, P])
        x1 = sb("x1e", [P, D])
        y = sb("ye", [P, D])
        gpost = sb("gpost4", [P, D])
        g2 = [sb(f"g2_{i}", [P, D]) for i in range(2)]
        qTs = sb("qTs", [P, 2, P])
        srep = sb("srep", [P, 2, NKEY])
        v16 = sb("v16", [P, 2, TOPK])
        i16 = sb("i16", [P, 2, TOPK], U32)
        i16f = sb("i16f", [P, 2, TOPK])
        cand = sb("cand", [P, TOPK, TOPK])
        crep = sb("crep", [P, TOPK, TOPK])
        best = sb("best", [P, TOPK])
        sel = sb("sel", [P, TOPK], U32)
        selij = sb("selij", [P, 2, TOPK], U32)
        selijf = sb("selijf", [P, 2, TOPK])
        onehot = sb("onehot", [P, 2 * TOPK, TOPK])
        picked = sb("picked", [P, 2, TOPK])
        idxf = sb("idxf", [P, TOPK])
        idx = sb("idx", [P, SLOTS], U32)
        gexp = sb("gexp", [P, TOPK])
        gsum = sb("gsum", [P, 1])
        gate = sb("gate", [P, SLOTS])
        dots = [sb(f"dots{i}", [P, TOPK]) for i in range(2)]
        gelu = [sb(f"gelu{i}", [P, TOPK]) for i in range(2)]
        wgt = [sb(f"wgt{i}", [P, TOPK]) for i in range(2)]
        msq = sb("msq4", [P, 1])
        rs = sb("rs4", [P, 1])
        tmp = sb("tmp4", [P, 1])
        ps_y = st.enter_context(nc.psum_tensor("ps_y", [P, D], F32))
        ps_h = st.enter_context(nc.psum_tensor("ps_h", [P, D], F32))
        ps_q, ps_t = ps("ps_q"), ps("ps_tr4")
        ps_s = [ps(f"ps_s4{i}") for i in range(2)]

        u_full = [sem(f"u_full{i}") for i in range(RING)]
        v_full = [sem(f"v_full{i}") for i in range(RING)]
        (u_used, v_used, h2_in, x1_in, g2_in, h2_tr, h2T_done, h2_copied, q_done, q_ready, s_done, s_read, idx_ready,
         gate_ask, gate_exp, dots_done, gelu_done, w_ready, diag_ready, y_sq, y_ask, y_root, y_free, y_done,
         y_out) = (sem(n) for n in (
             "u_used", "v_used", "h2_in", "x1_in", "g2_in", "h2_tr", "h2T_done", "h2_copied", "q_done", "q_ready",
             "s_done", "s_read", "idx_ready", "gate_ask", "gate_exp", "dots_done", "gelu_done", "w_ready",
             "diag_ready", "y_sq", "y_ask", "y_root", "y_free", "y_done", "y_out"))
        act_own, dve_own = sem("act_own4"), sem("dve_own4")
        pool_passed, dve_passed = sem("pool_passed"), sem("dve_passed")
        block = st.enter_context(nc.Block())

        def run(eng, start, body):
            start()
            body(0, DEC, P, None)
            with eng.Fori(0, NT - 1) as i:
                body(i + 1, P, P, i)
            body(NT, P, 0, NT - 1)

        @block.sync
        def _(sp):
            for i in range(2):
                sp.dma_start(g2[i][:, :], S["mod_d"][i:i + 1, 5 * D:6 * D].broadcast_to([P, D])).then_inc(g2_in, 16)
            sp.dma_start(gpost[:, :], A["rows"][2:3, :].broadcast_to([P, D])).then_inc(g2_in, 16)

            def start():
                sp.dma_start(h2n[0:DEC, :], S["h2_d"][SEQ:TOK, :]).then_inc(h2_in, 16)

            def body(n, rows, nxt, tile):
                if nxt:
                    sp.wait_ge(h2_copied, n * 2 + 2)
                    sp.wait_ge(h2_tr, n * 2 + 2)
                    row0 = 0 if tile is None else tile * P + P
                    sp.dma_start(h2n[:, :], S["h2_d"][bass.ds(row0, P), :]).then_inc(h2_in, 16)
                row0 = SEQ if tile is None else tile * P
                if tile is not None:
                    sp.wait_ge(y_done, n)
                sp.dma_start(x1[0:rows, :], S["x1_d"][bass.ds(row0, rows), :]).then_inc(x1_in, 16)
                sp.wait_ge(y_done, n + 1)
                dst = A["y_s"][:, :] if tile is None else A["y_p"][bass.ds(row0, rows), :]
                sp.dma_start(dst, y[0:rows, :]).then_inc(y_out, 16)

            run(sp, start, body)
            sp.wait_ge(y_out, 16 * (NT + 1))

        @block.gpsimd
        def _(pool):
            def gather(table, ring, full, h, k, rows):
                nc.gpsimd.indirect_dma_start(
                    ring[(TOPK * h + k) % RING][0:rows, :], None, A[table][:, :],
                    bass.IndirectOffsetOnAxis(ap=idx[0:rows, TOPK * h + k:TOPK * h + k + 1], axis=0))\
                    .then_inc(full[k % RING], 16)

            def start():
                pool.wait_ge(idx_ready, 1)
                for k in range(TOPK):
                    if k >= RING:
                        pool.wait_ge(u_used, k - RING + 1)
                    gather("u_tab", urow, u_full, 0, k, DEC)

            def body(n, rows, nxt, tile):
                for h in range(PH):
                    ahead = h < PH - 1 or nxt
                    if ahead:
                        pool.wait_ge(idx_ready, n * PH + (h + 2))
                    for k in range(TOPK):
                        if ahead:
                            pool.wait_ge(u_used, n * SLOTS + (TOPK * (h + 1) + k - RING + 1))
                            pool.sem_inc(pool_passed, 1)
                            gather("u_tab", urow, u_full, (h + 1) % PH, k, rows if h < PH - 1 else nxt)
                        s = TOPK * h + k
                        if not (isinstance(n, int) and n == 0 and s < RING):
                            pool.wait_ge(v_used, n * SLOTS + (s - RING + 1))
                            pool.sem_inc(pool_passed, 1)
                        gather("v_tab", vrow, v_full, h, k, rows)

            run(pool, start, body)

        @block.scalar
        def _(act):
            own = Chain(act, act_own)

            def take_h2T(n, rows):
                for half in range(2):
                    act.wait_ge(h2_tr, n * 2 + (half + 1))
                    if half == 0 and not (isinstance(n, int) and n == 0):
                        act.wait_ge(q_done, n * PH)
                    nc.scalar.activation(h2T[:, 4 * half:4 * half + 4, 0:rows],
                                         ps_t[:, :].rearrange("p (k t) -> p k t", k=4)[:, :, 0:rows], ACT.Copy)\
                        .then_inc(h2T_done, 1)

            def take_q(n, h, rows):
                act.wait_ge(q_done, n * PH + (h + 1))
                if not (isinstance(n, int) and n == 0 and h == 0):
                    act.wait_ge(s_done, n * PH + h)
                nc.scalar.activation(qTs[:, :, 0:rows], ps_q[:, 0:2 * P].rearrange("p (k t) -> p k t", k=2)[:, :, 0:rows],
                                     ACT.Copy).then_inc(q_ready, 1)

            def copy_h2(n, rows, first=False):
                if first:
                    act.wait_ge(h2_in, 16)
                else:
                    act.wait_ge(u_used, n * SLOTS)
                    act.wait_ge(h2_in, n * 16 + 16)
                for half in range(2):
                    c = slice(512 * half, 512 * (half + 1))
                    nc.scalar.activation(ps_h[0:rows, c], h2n[0:rows, c], ACT.Copy).then_inc(h2_copied, 1)

            def exp_gate(n, h, rows):
                act.wait_ge(gate_ask, n * PH + (h + 1))
                nc.scalar.activation(gexp[0:rows, :], gexp[0:rows, :], ACT.Exp).then_inc(gate_exp, 1)

            def do_gelu(n, h, rows):
                act.wait_ge(dots_done, n * PH + (h + 1))
                nc.scalar.activation(gelu[h % 2][0:rows, :], dots[h % 2][0:rows, :], ACT.Gelu).then_inc(gelu_done, 1)

            def start():
                take_h2T(0, DEC)
                copy_h2(0, DEC, first=True)
                for h in range(PH):
                    take_q(0, h, DEC)
                    if h >= 1:
                        exp_gate(0, h - 1, DEC)
                do_gelu(0, 0, DEC)

            def body(n, rows, nxt, tile):
                for h in range(PH):
                    if h == 0 and nxt:
                        take_h2T(n + 1, nxt)
                    if h == PH - 1 and nxt:
                        copy_h2(n + 1, nxt)
                    act.wait_ge(w_ready, n * PH + (h + 1))
                    for k in range(TOPK):
                        s = TOPK * h + k
                        if not (isinstance(n, int) and n == 0 and s < DIAGS):
                            act.wait_ge(v_used, n * SLOTS + (s - DIAGS + 1))
                        nc.scalar.activation(diag[s % DIAGS][0:rows, 0:rows], ident[0:rows, 0:rows], ACT.Copy,
                                             scale=wgt[h % 2][0:rows, k:k + 1]).then_inc(diag_ready, 1)
                        if k == 3 and nxt:
                            take_q(n + 1, h, nxt)
                    if h == 0:
                        exp_gate(n, PH - 1, rows)
                    elif nxt:
                        exp_gate(n + 1, h - 1, nxt)
                    if h < PH - 1:
                        do_gelu(n, h + 1, rows)
                    elif nxt:
                        do_gelu(n + 1, 0, nxt)
                act.wait_ge(v_used, n * SLOTS + SLOTS)
                if tile is not None:
                    act.wait_ge(y_out, n * 16)
                nc.scalar.activation(y[0:rows, :], ps_y[0:rows, :], ACT.Square, accum_out=msq[0:rows, :])\
                    .then_inc(y_sq, 1)
                act.wait_ge(y_ask, n + 1)
                own.base, own.n = n, 0
                own.link(nc.scalar.activation(rs[0:rows, :], msq[0:rows, :], ACT.Ln))
                nc.scalar.activation(rs[0:rows, :], rs[0:rows, :], ACT.Exp, scale=-0.5).then_inc(y_root, 1)

            run(act, start, body)

        @block.vector
        def _(dve):
            own = Chain(dve, dve_own)
            dve.wait_ge(g2_in, 48)
            for i in range(2):
                own.link(nc.vector.tensor_tensor(g2[i][:, :], g2[i][:, :], gpost[:, :], ALU.mult))

            def top16(values, src, rep, index):
                own.link_apart(nc.vector.max(values[:, 0:8], src), dve_passed)
                own.add(nc.vector.max_index(index[:, 0:8], values[:, 0:8], src))
                own.link_apart(nc.vector.match_replace(rep, values[:, 0:8], src, LOWEST), dve_passed)
                own.link_apart(nc.vector.max(values[:, 8:16], rep), dve_passed)
                own.link_apart(nc.vector.max_index(index[:, 8:16], values[:, 8:16], rep), dve_passed)

            def search(n, h, rows):
                r = slice(0, rows)
                s = ps_s[h % 2]
                dve.wait_ge(s_done, n * PH + (h + 1))
                dve.sem_inc(dve_passed, 1)
                for side in range(2):
                    top16(v16[r, side, :], s[r, side * P:(side + 1) * P], srep[r, side, :], i16[r, side, :])
                dve.sem_inc(s_read, 1)
                own.add(nc.vector.tensor_copy(i16f[r, :, :], i16[r, :, :]))
                own.link_apart(nc.vector.tensor_tensor(cand[r, :, :], v16[r, 0, :, None].broadcast_to([rows, TOPK, TOPK]),
                                                       v16[r, 1, None, :].broadcast_to([rows, TOPK, TOPK]), ALU.add),
                               dve_passed)
                flat = cand[r, :, :].rearrange("p a b -> p (a b)")
                top16(best[r, :], flat, crep[r, :, :].rearrange("p a b -> p (a b)"), sel[r, :])
                nc.vector.tensor_scalar(gexp[r, :], best[r, :], best[r, 0:1], None, ALU.subtract).then_inc(gate_ask, 1)
                own.add(nc.vector.tensor_scalar(selij[r, 0, :], sel[r, :], 4, None, ALU.logical_shift_right))
                own.link(nc.vector.tensor_scalar(selij[r, 1, :], sel[r, :], TOPK - 1, None, ALU.bitwise_and))
                own.link(nc.vector.tensor_copy(selijf[r, :, :], selij[r, :, :]))
                own.link(nc.vector.tensor_tensor(
                    onehot[r, :, :], selijf[r, :, :].rearrange("p s k -> p (s k)")[:, :, None]
                    .broadcast_to([rows, 2 * TOPK, TOPK]),
                    iota[r, None, :].broadcast_to([rows, 2 * TOPK, TOPK]), ALU.is_equal))
                for side in range(2):
                    at = onehot[r, side * TOPK:(side + 1) * TOPK, :]
                    own.link(nc.vector.tensor_tensor(at, at, i16f[r, side, None, :].broadcast_to([rows, TOPK, TOPK]),
                                                     ALU.mult))
                own.link(nc.vector.tensor_reduce(picked[r, :, :].rearrange("p s k -> p (s k)"), onehot[r, :, :],
                                                 AX_X, ALU.add))
                own.link(nc.vector.scalar_tensor_tensor(out=idxf[r, :], in0=picked[r, 0, :], scalar=float(NKEY),
                                                        in1=picked[r, 1, :], op0=ALU.mult, op1=ALU.add))
                if not (isinstance(n, int) and n == 0):
                    dve.wait_ge(v_used, (n - 1) * SLOTS + TOPK * (h + 1))
                nc.vector.tensor_copy(idx[r, TOPK * h:TOPK * (h + 1)], idxf[r, :]).then_inc(idx_ready, 1)
                dve.wait_ge(gate_exp, n * PH + (h + 1))
                own.link(nc.vector.tensor_reduce(gsum[r, :], gexp[r, :], AX_X, ALU.add))
                own.link(nc.vector.reciprocal(gsum[r, :], gsum[r, :]))
                own.link(nc.vector.tensor_scalar(gate[r, TOPK * h:TOPK * (h + 1)], gexp[r, :], gsum[r, 0:1], None,
                                                 ALU.mult))

            def products(n, h, rows):
                if isinstance(n, int) and n == 0 and h == 0:
                    dve.wait_ge(h2_copied, 2)
                elif h == 0:
                    dve.wait_ge(h2_copied, n * 2 + 2)
                if not (isinstance(n, int) and n == 0 and h < 2):
                    dve.wait_ge(gelu_done, n * PH + (h - 1))
                for k in range(TOPK):
                    s = TOPK * h + k
                    dve.wait_ge(u_full[s % RING], n * (16 * SLOTS // RING) + 16 * (s // RING + 1))
                    last = nc.vector.tensor_tensor_reduce(out=urow[s % RING][0:rows, :], in0=urow[s % RING][0:rows, :],
                                                          in1=ps_h[0:rows, :], scale=1.0, scalar=0.0, op0=ALU.mult,
                                                          op1=ALU.add, accum_out=dots[h % 2][0:rows, k:k + 1])
                    last.then_inc(u_used, 1)
                dve.wait_ge(u_used, n * SLOTS + TOPK * (h + 1))
                dve.sem_inc(dots_done, 1)

            def weights(n, h, rows):
                dve.wait_ge(gelu_done, n * PH + (h + 1))
                if not (isinstance(n, int) and n == 0 and h < 2):
                    dve.wait_ge(diag_ready, n * SLOTS + TOPK * (h - 1))
                nc.vector.tensor_tensor(wgt[h % 2][0:rows, :], gate[0:rows, TOPK * h:TOPK * (h + 1)],
                                        gelu[h % 2][0:rows, :], ALU.mult).then_inc(w_ready, 1)

            SEARCH = 28

            def start():
                for h in range(PH - 1):
                    search(0, h, DEC)
                products(0, 0, DEC)
                weights(0, 0, DEC)

            ahead = 2 + (PH - 1) * SEARCH
            per = PH * SEARCH + 5

            def body(n, rows, nxt, tile):
                own.base, own.n = n * per + ahead, 0
                for h in range(PH):
                    if h < PH - 1:
                        products(n, h + 1, rows)
                    elif nxt:
                        products(n + 1, 0, nxt)
                    if h == 0:
                        search(n, PH - 1, rows)
                    elif nxt:
                        search(n + 1, h - 1, nxt)
                    if h < PH - 1:
                        weights(n, h + 1, rows)
                    elif nxt:
                        weights(n + 1, 0, nxt)
                r = slice(0, rows)
                dve.wait_ge(y_sq, n + 1)
                own.link(nc.vector.tensor_scalar(msq[r, :], msq[r, :], 1.0 / D, EPS, ALU.mult, ALU.add))
                rstd_steps(nc, own, msq[r, :], None, None, rs[r, :], tmp[r, :], lambda: dve.sem_inc(y_ask, 1),
                           lambda: dve.wait_ge(y_root, n + 1))
                if tile is not None:
                    dve.wait_ge(y_out, n * 16)
                nc.vector.scalar_tensor_tensor(out=y[r, :], in0=ps_y[r, :], scalar=rs[r, 0:1],
                                               in1=g2[1 if tile is None else 0][r, :], op0=ALU.mult,
                                               op1=ALU.mult).then_inc(y_free, 1)
                dve.wait_ge(y_free, n + 1)
                dve.wait_ge(x1_in, n * 16 + 16)
                nc.vector.tensor_tensor(y[r, :], y[r, :], x1[r, :], ALU.add).then_inc(y_done, 1)
                if nxt:
                    assert own.n == per, (own.n, per)

            run(dve, start, body)

        @block.tensor
        def _(pe):
            pe.wait_ge(S["w_q_full"], 16 * (KC + 1))

            def transposes(n, rows):
                pe.wait_ge(h2_in, n * 16 + 16)
                for half in range(2):
                    if half or not (isinstance(n, int) and n == 0):
                        pe.wait_ge(h2T_done, n * 2 + half)
                    for q in range(4):
                        k = 4 * half + q
                        last = nc.tensor.transpose(ps_t[:, q * P:q * P + rows], h2n[0:rows, k * P:(k + 1) * P],
                                                   ident[0:rows, 0:rows])
                    last.then_inc(h2_tr, 1)
                pe.wait_ge(h2T_done, n * 2 + 2)

            def queries(n, h, rows):
                if not (isinstance(n, int) and n == 0 and h == 0):
                    pe.wait_ge(q_ready, n * PH + h)
                for side in range(2):
                    c = 2 * h + side
                    for k in range(KC):
                        last = nc.tensor.matmul(ps_q[:, side * P:side * P + rows], w_q[:, k, c * P:(c + 1) * P],
                                                h2T[:, k, 0:rows], start=(k == 0), stop=(k == KC - 1),
                                                skip_group_check=True)
                last.then_inc(q_done, 1)

            def scores(n, h, rows):
                pe.wait_ge(q_ready, n * PH + (h + 1))
                if not (isinstance(n, int) and n == 0 and h < 2):
                    pe.wait_ge(s_read, n * PH + (h - 1))
                for side in range(2):
                    last = nc.tensor.matmul(ps_s[h % 2][0:rows, side * P:(side + 1) * P], qTs[:, side, 0:rows],
                                            keys[:, 2 * h + side, :], start=True, stop=True, skip_group_check=True)
                last.then_inc(s_done, 1)

            def add_row(n, h, k, rows):
                s = TOPK * h + k
                pe.wait_ge(v_full[s % RING], n * (16 * SLOTS // RING) + 16 * (s // RING + 1))
                pe.wait_ge(diag_ready, n * SLOTS + (s + 1))
                for half in range(2):
                    c = slice(512 * half, 512 * (half + 1))
                    last = nc.tensor.matmul(ps_y[0:rows, c], diag[s % DIAGS][0:rows, 0:rows], vrow[s % RING][0:rows, c],
                                            start=(s == 0), stop=(s == SLOTS - 1))
                last.then_inc(v_used, 1)

            def start():
                transposes(0, DEC)
                for h in range(PH):
                    queries(0, h, DEC)
                    scores(0, h, DEC)

            def body(n, rows, nxt, tile):
                for h in range(PH):
                    if nxt:
                        if h == 0:
                            transposes(n + 1, nxt)
                        queries(n + 1, h, nxt)
                    if h == 0 and tile is not None:
                        pe.wait_ge(y_free, n)
                    for k in range(TOPK):
                        add_row(n, h, k, rows)
                        if k == TOPK // 2 - 1 and nxt:
                            scores(n + 1, h, nxt)

            run(pe, start, body)


def constants():
    import numpy as np

    c = np.zeros((P, C_END), np.float32)
    i = np.arange(P)
    c[:, C_ID:C_ID + P] = np.eye(P)
    c[:, C_NTRI:C_NTRI + P] = -(i[:, None] >= i[None, :]).astype(np.float32)
    c[:, C_NONES:C_NONES + P] = -1.0
    c[:, C_MASK:C_MASK + P] = i[:, None] < i[None, :]
    c[:, C_IOTA:C_IOTA + TOPK] = np.arange(TOPK)
    for g, w in enumerate(WINDOWS):
        c[:, C_INVC + 16 * g:C_INVC + 16 * (g + 1)] = 1.0 / np.minimum(np.arange(16) + 1, w)
    return c


_OUTS = [("y_p", (SEQ, D)), ("y_s", (DEC, D)), ("k_p", (SEQ, DA)), ("v_p", (SEQ, DA)), ("pool_p", (HIST, DPOOL)),
         ("k_s", (DEC, DA)), ("v_s", (DEC, DA)), ("pool_s", (HIST, DPOOL))]


def kernel(x_prompt, x_sample, cache_k, cache_v, state_pool, c_prompt, c_sample, w_ada, b_ada, g_pre1, g_post1,
           g_pre2, g_post2, w_in, g_out_a, g_out_b, w_pool, pool_scale, w_out, w_query, sub_keys, u_experts, v_experts):
    import numpy as np
    import concourse.bacc as bacc
    from concourse.bass_utils import run_bass_kernel_spmd

    a = lambda v: np.ascontiguousarray(np.asarray(v))
    col = lambda v: np.asarray(v).reshape(-1, P).T
    ins = {
        "x_p": a(x_prompt)[0], "x_s": a(x_sample)[0],
        "cT": a(np.stack([np.asarray(c_prompt)[0], np.asarray(c_sample)[0]]).reshape(2, KC, P).transpose(2, 1, 0)
                .reshape(P, 2 * KC)),
        "w_ada": a(w_ada)[0], "b_ada": a(b_ada),
        "gains": a(np.concatenate([col(g_pre1), col(g_out_a), col(g_out_b), col(pool_scale)], axis=1)),
        "rows": a(np.concatenate([np.asarray(g_post1), np.asarray(g_pre2), np.asarray(g_post2)])),
        "w_in": a(w_in)[0], "w_pool": a(w_pool)[0], "w_out": a(w_out)[0], "w_query": a(w_query)[0],
        "keysT": a(np.asarray(sub_keys)[0].transpose(3, 1, 0, 2).reshape(P, 2 * PH, NKEY)),
        "kpastT": a(np.asarray(cache_k)[0, 0].reshape(PAST, DA).T), "vpast": a(cache_v)[0, 0].reshape(PAST, DA),
        "histT": a(np.asarray(state_pool)[0, 0].reshape(HIST, FA, P).transpose(2, 1, 0)),
        "u_tab": a(u_experts)[0], "v_tab": a(v_experts)[0],
        "const": constants(),
    }
    nc = bacc.Bacc("TRN2", target_bir_lowering=False, num_devices=1)
    A, arrays = {}, {}
    for name, v in ins.items():
        arrays[f"in_{name}"] = np.ascontiguousarray(v)
        A[name] = nc.dram_tensor(f"in_{name}", v.shape, mybir.dt.from_np(v.dtype), kind="ExternalInput").ap()
    for name, shape in _OUTS:
        A[name] = nc.dram_tensor(f"out_{name}", shape, F32, kind="ExternalOutput").ap()
    build(nc, A)
    r = run_bass_kernel_spmd(nc, [arrays], core_ids=[0]).results[0]
    y_p, y_s, k_p, v_p, pool_p, k_s, v_s, pool_s = (r[f"out_{name}"] for name, _ in _OUTS)
    kv = lambda t, n: t.reshape(1, 1, n, DA // HD, HD)
    return (y_p[None], y_s[None], kv(k_p, SEQ), kv(v_p, SEQ), pool_p[None, None], kv(k_s, DEC), kv(v_s, DEC),
            pool_s[None, None])
```

```python
from contextlib import ExitStack

import concourse.bass as bass
from concourse import mybir

ALU = mybir.AluOpType
ACT = mybir.ActivationFunctionType
F32 = mybir.dt.float32
U32 = mybir.dt.uint32
AX_X = mybir.AxisListType.X

P = 128
D = 1024
SEQ = 1024
DEC = 64
PAST = 256
HD = 64
DA = 512
DPOOL = 512
NMOD = 6
EPS = 1e-6
KC = D // P
FA = DA // P
WINDOWS = (2, 4, 8, 16)
HIST = 15
PAD = 16
TOK = SEQ + DEC
NT = SEQ // P
NEXP = 128 * 128
PH = 8
TOPK = 16
NKEY = 128
SLOTS = PH * TOPK
RING = 8
DIAGS = 4
LOWEST = -3.0e38
LOG_EXP = "natural_log_exp_and_others"

C_ID, C_NTRI, C_NONES, C_MASK, C_IOTA, C_INVC = 0, 128, 256, 384, 512, 528
C_END = 528 + 64
G_PRE1, G_OUT, G_POOL = 0, 8, 16
G_END = 20

RANGES = [(0, 512), (512, 512), (SEQ, DEC)]
TILES = [(P * t, P) for t in range(NT)] + [(SEQ, DEC)]


class Chain:

    def __init__(self, eng, sem):
        self.eng, self.sem, self.base, self.n = eng, sem, 0, 0

    def add(self, ins):
        ins.then_inc(self.sem, 1)
        self.n += 1

    def wait(self):
        self.eng.wait_ge(self.sem, self.base + self.n)

    def link(self, ins):
        self.add(ins)
        self.wait()

    def link_apart(self, ins, passed):
        self.link(ins)
        self.eng.sem_inc(passed, 1)


def build(nc, A):
    with ExitStack() as outer:
        def sem(name):
            return outer.enter_context(nc.semaphore(name))

        def dram(name, shape):
            return nc.dram_tensor(name, shape, F32).ap()

        def sbuf(stack, name, shape, dt=F32):
            return stack.enter_context(nc.sbuf_tensor(name, shape, dt))

        S = {
            "sem": sem,
            "mod_d": dram("mod_d", [2, NMOD * D]),
            "qT_d": dram("qT_d", [DA, TOK]),
            "kT_d": dram("kT_d", [DA, TOK]),
            "x1_d": dram("x1_d", [TOK, D]),
            "h2_d": dram("h2_d", [TOK, D]),
            "const": sbuf(outer, "const", [P, C_END]),
            "gains": sbuf(outer, "gains", [P, G_END]),
        }
        late = outer.enter_context(ExitStack())
        with ExitStack() as right:
            with ExitStack() as early:
                S["w_in"] = sbuf(early, "w_in_sb", [P, KC, 4 * DA])
                S["hT"] = sbuf(early, "hT", [P, KC, TOK])
                S["acol"] = sbuf(early, "acol", [P, 2, KC])
                S["bcol"] = sbuf(early, "bcol", [P, 2, KC])
                S["w_in_full"] = sem("w_in_full")
                modulation(nc, A, S)
                S["oT"] = right.enter_context(nc.sbuf_tensor("oT", [P, KC, TOK], F32, side="right"))
                projection(nc, A, S)
            S["w_out"] = right.enter_context(nc.sbuf_tensor("w_out_sb", [P, KC, D], F32, side="right"))
            for name in ("g1", "a2", "b2", "gpost", "gpre"):
                S[name] = right.enter_context(nc.sbuf_tensor(name, [P, D], F32, side="right"))
            S["w_out_full"], S["w_scaled"] = sem("w_out_full"), sem("w_scaled")
            attention(nc, A, S)
            S["w_q"] = sbuf(late, "w_q_sb", [P, KC, 2 * D])
            S["keys"] = sbuf(late, "keys_sb", [P, 2 * PH, NKEY])
            S["w_q_full"] = sem("w_q_full")
            output(nc, A, S)
        experts(nc, A, S)


def modulation(nc, A, S):
    sem = S["sem"]
    hT, acol, bcol, gains = S["hT"], S["acol"], S["bcol"], S["gains"]
    ident = S["const"][:, C_ID:C_ID + P]
    CH = 512
    NCH = NMOD * D // CH
    ADA = 4
    FIRST = 2 * D // CH
    NTILE = len(TILES)
    with ExitStack() as st:
        sb = lambda n, s, d=F32: st.enter_context(nc.sbuf_tensor(n, s, d))
        ada = [sb(f"ada{i}", [P, KC, CH]) for i in range(ADA)]
        c_sb = sb("c_sb", [P, KC * 2])
        ec = sb("ec", [P, KC * 2])
        silu = sb("silu", [P, KC * 2])
        mod = sb("mod", [2, NMOD * D])
        x = [sb(f"x{i}", [P, D]) for i in range(2)]
        xn = [sb(f"xn{i}", [P, D]) for i in range(2)]
        scol = sb("scol", [P, 2, KC])
        msq = sb("msq1", [P, NTILE])
        rs = sb("rs1", [P, NTILE])
        tmp = sb("tmp1", [P, NTILE])
        psum = [st.enter_context(nc.psum_tensor(f"ps_mod{i}", [P, CH], F32)) for i in range(2)]
        ps_t = [st.enter_context(nc.psum_tensor(f"ps_t{i}", [P, 512], F32)) for i in range(4)]
        ada_full = [sem(f"ada_full{i}") for i in range(ADA)]
        c_in, b_in, gains_in, const_in, c_exp, c_silu = (
            sem(x) for x in ("c_in", "b_in", "gains_in", "const_in", "c_exp", "c_silu"))
        mm_done, mod_done, mod1_out, mod_out, col_in = (
            sem(x) for x in ("mod_mm", "mod_done", "mod1_out", "mod_out", "col_in"))
        x_full = [sem(f"x_full{i}") for i in range(2)]
        sq_done, msq_done, y0_done, xn_done = (sem(n) for n in ("sq_done1", "msq_done1", "y0_done1", "xn_done"))
        act_own, dve_own = sem("act_own0"), sem("dve_own0")
        tr_done, hT_done = sem("tr_done1"), sem("hT_done")
        block = st.enter_context(nc.Block())

        @block.sync
        def _(sp):
            sp.dma_start(c_sb[:, :], A["cT"][:, :]).then_inc(c_in, 16)
            sp.dma_start(mod[:, :], A["b_ada"].broadcast_to([2, NMOD * D])).then_inc(b_in, 16)
            ada_v = A["w_ada"].rearrange("(k p) n -> p k n", p=P)
            with sp.Fori(0, NCH // ADA) as i:
                for j in range(ADA):
                    sp.wait_ge(mod_done, i * ADA + (j + 1))
                    sp.dma_start(ada[j][:, :, :], ada_v[:, :, bass.ds(i * (ADA * CH) + j * CH, CH)])\
                        .then_inc(ada_full[j], 16)
            w_v = A["w_in"].rearrange("(k p) n -> p k n", p=P)
            for k in range(KC):
                sp.dma_start(S["w_in"][:, k, :], w_v[:, k, :]).then_inc(S["w_in_full"], 16)
            sp.wait_ge(mod_done, NCH + ADA)
            sp.dma_start(S["mod_d"][:, 2 * D:], mod[:, 2 * D:]).then_inc(mod_out, 16)
            sp.wait_ge(mod_out, 16)

        @block.gpsimd
        def _(pool):
            pool.wait_ge(mod_done, FIRST + ADA)
            pool.dma_start(S["mod_d"][:, 0:2 * D], mod[:, 0:2 * D]).then_inc(mod1_out, 16)
            pool.wait_ge(mod1_out, 16)
            for s in range(2):
                for m, dst in enumerate((bcol, scol)):
                    pool.dma_start(dst[:, s, :], S["mod_d"][s, m * D:(m + 1) * D].rearrange("(k p) -> p k", p=P),
                                   allow_slow_non_contiguous=True).then_inc(col_in, 16)

        @block.scalar
        def _(act):
            own = Chain(act, act_own)
            act.preload_act_table_set(LOG_EXP)
            act.dma_start(S["const"][:, :], A["const"][:, :]).then_inc(const_in, 16)
            act.dma_start(S["gains"][:, :], A["gains"][:, :]).then_inc(gains_in, 16)

            def load(t):
                t0, rows = TILES[t]
                src = A["x_p"][t0:t0 + rows, :] if t < NT else A["x_s"][:, :]
                act.dma_start(x[t % 2][0:rows, :], src).then_inc(x_full[t % 2], 16)

            load(0)
            load(1)
            act.wait_ge(c_in, 16)
            nc.scalar.activation(ec[:, :], c_sb[:, :], ACT.Exp, scale=-1.0).then_inc(c_exp, 1)
            for t, (_, rows) in enumerate(TILES):
                b = t % 2
                act.wait_ge(x_full[b], 16 * (t // 2 + 1))
                if t >= 2:
                    act.wait_ge(tr_done, 2 * (t - 1))
                nc.scalar.activation(xn[b][0:rows, :], x[b][0:rows, :], ACT.Square,
                                     accum_out=msq[0:rows, t:t + 1]).then_inc(sq_done, 1)
                act.wait_ge(msq_done, t + 1)
                own.link(nc.scalar.activation(rs[0:rows, t:t + 1], msq[0:rows, t:t + 1], ACT.Ln))
                nc.scalar.activation(rs[0:rows, t:t + 1], rs[0:rows, t:t + 1], ACT.Exp, scale=-0.5)\
                    .then_inc(y0_done, 1)
                if t + 2 < NTILE:
                    act.wait_ge(xn_done, t + 1)
                    load(t + 2)

        @block.vector
        def _(dve):
            own = Chain(dve, dve_own)
            dve.sem_inc(mod_done, ADA)
            dve.wait_ge(c_exp, 1)
            own.link(nc.vector.tensor_scalar_add(ec[:, :], ec[:, :], 1.0))
            own.link(nc.vector.reciprocal(silu[:, :], ec[:, :]))
            nc.vector.tensor_tensor(silu[:, :], silu[:, :], c_sb[:, :], ALU.mult).then_inc(c_silu, 1)

            def finish_tile(t):
                t0, rows = TILES[t]
                for half in range(2):
                    dve.wait_ge(tr_done, 2 * t + half + 1)
                    bank = ps_t[2 * (t % 2) + half]
                    nc.vector.tensor_copy(hT[:, 4 * half:4 * half + 4, t0:t0 + rows],
                                          bank[:, :].rearrange("p (k t) -> p k t", k=4)[:, :, 0:rows])\
                        .then_inc(hT_done, 1)

            for t, (_, rows) in enumerate(TILES):
                col = slice(t, t + 1)
                dve.wait_ge(sq_done, t + 1)
                nc.vector.tensor_scalar(msq[0:rows, col], msq[0:rows, col], 1.0 / D, EPS, ALU.mult, ALU.add)\
                    .then_inc(msq_done, 1)
                if t:
                    finish_tile(t - 1)
                dve.wait_ge(msq_done, t + 1)
                rstd_steps(own, nc, msq[0:rows, col], rs[0:rows, col], tmp[0:rows, col],
                           lambda: None, lambda: dve.wait_ge(y0_done, t + 1))
                nc.vector.tensor_scalar(xn[t % 2][0:rows, :], x[t % 2][0:rows, :], rs[0:rows, col], None, ALU.mult)\
                    .then_inc(xn_done, 1)
            finish_tile(NTILE - 1)
            dve.wait_ge(b_in, 16)
            with dve.Fori(0, NCH // 2) as i:
                for j in range(2):
                    dve.wait_ge(mm_done, i * 2 + (j + 1))
                    at = bass.ds(i * (2 * CH) + j * CH, CH)
                    nc.vector.tensor_tensor(mod[:, at], psum[j][0:2, :], mod[:, at], ALU.add)\
                        .then_inc(mod_done, 1)
            dve.wait_ge(col_in, 64)
            dve.wait_ge(gains_in, 16)
            for s in range(2):
                own.link(nc.vector.tensor_scalar_add(acol[:, s, :], scol[:, s, :], 1.0))
                own.link(nc.vector.tensor_tensor(acol[:, s, :], acol[:, s, :], gains[:, G_PRE1:G_PRE1 + KC], ALU.mult))

        @block.tensor
        def _(pe):
            pe.wait_ge(const_in, 16)
            for t, (_, rows) in enumerate(TILES):
                pe.wait_ge(xn_done, t + 1)
                for half in range(2):
                    if t >= 2:
                        pe.wait_ge(hT_done, 2 * (t - 2) + half + 1)
                    for q in range(4):
                        k = 4 * half + q
                        last = nc.tensor.transpose(ps_t[2 * (t % 2) + half][:, q * P:q * P + rows],
                                                   xn[t % 2][0:rows, k * P:(k + 1) * P], ident[0:rows, 0:rows])
                    last.then_inc(tr_done, 1)
            pe.wait_ge(c_silu, 1)
            with pe.Fori(0, NCH // ADA) as i:
                for j in range(ADA):
                    pe.wait_ge(ada_full[j], i * 16 + 16)
                    pe.wait_ge(mod_done, i * ADA + (j + ADA - 1))
                    for k in range(KC):
                        last = nc.tensor.matmul(psum[j % 2][0:2, :], silu[:, 2 * k:2 * k + 2], ada[j][:, k, :],
                                                start=(k == 0), stop=(k == KC - 1))
                    last.then_inc(mm_done, 1)


def rstd_steps(own, nc, mean_sq, y, t, to_act, from_act):
    to_act()
    from_act()
    own.link(nc.vector.tensor_tensor(t, y, y, ALU.mult))
    own.link(nc.vector.tensor_tensor(t, t, mean_sq, ALU.mult))
    own.link(nc.vector.tensor_scalar(t, t, -0.5, 1.5, ALU.mult, ALU.add))
    own.link(nc.vector.tensor_tensor(y, y, t, ALU.mult))


def projection(nc, A, S):
    sem = S["sem"]
    const, gains, w_in, oT = S["const"], S["gains"], S["w_in"], S["oT"]
    hT, acol, bcol = S["hT"], S["acol"], S["bcol"]
    ident = const[:, C_ID:C_ID + P]
    NTILE = len(TILES)
    jobs = [(kind, f, r) for kind in "kqp" for f in range(FA) for r in range(len(RANGES))]
    jobs += [("v", t, None) for t in range(NTILE)]
    NB = 3
    with ExitStack() as st:
        sb = lambda n, s, d=F32: st.enter_context(nc.sbuf_tensor(n, s, d))
        ps = lambda n: st.enter_context(nc.psum_tensor(n, [P, 512], F32))
        stage = [sb(f"stage{i}", [P, 512]) for i in range(NB)]
        krow = [sb(f"krow{i}", [P, 4, P]) for i in range(2)]
        pT = sb("pT", [P, FA, PAD + SEQ])
        pTs = sb("pTs", [P, FA, PAD + DEC])
        sums = [sb(f"sums{i}", [P, PAD + SEQ]) for i in range(2)]
        w_pool = sb("w_pool_sb", [P, FA, P])
        prow = [sb(f"prow{i}", [HIST, DPOOL]) for i in range(2)]
        ps_t = [ps(f"ps_p{i}") for i in range(2)]
        ps_z = [ps(f"ps_z{i}") for i in range(NB)]
        ps_k = [ps(f"ps_k{i}") for i in range(2)]
        pool_in, dve_own, h_done = sem("pool_in"), sem("dve_own1"), sem("h_done")
        z_done, z_read = sem("z_done"), sem("z_read")
        stage_out = [sem(f"stage_out{i}") for i in range(NB)]
        k_tr, k_read, krow_out = sem("k_tr"), sem("k_read"), [sem(f"krow_out{i}") for i in range(2)]
        hist_clear = sem("hist_clear")
        pooled_done, mix_done, mix_read = sem("pooled_done"), sem("mix_done"), sem("mix_read")
        p_tr, p_read, prow_out = sem("p_tr"), sem("p_read"), sem("prow_out")
        block = st.enter_context(nc.Block())

        n_k = FA * len(RANGES)
        last_p = 3 * n_k
        def stores_before(j, b):
            return sum(1 for m in range(j) if m % NB == b and jobs[m][0] != "p")

        @block.sync
        def _(sp):
            for j, (kind, f, r) in enumerate(jobs):
                if kind == "p":
                    continue
                sp.wait_ge(z_read, j + 1)
                if kind == "v":
                    t0, rows = TILES[f]
                    dst = A["v_p"][t0:t0 + rows, :] if f < NT else A["v_s"][:, :]
                    src = stage[j % NB][0:rows, :]
                else:
                    c0, n = RANGES[r]
                    dst = S["qT_d" if kind == "q" else "kT_d"][f * P:(f + 1) * P, c0:c0 + n]
                    src = stage[j % NB][:, 0:n]
                sp.dma_start(dst, src).then_inc(stage_out[j % NB], 16)
                if kind == "k":
                    sp.wait_ge(k_read, j + 1)
                    if r < 2:
                        dst = A["k_p"][c0:c0 + n, f * P:(f + 1) * P].rearrange("(t p) c -> p t c", p=P)
                        sp.dma_start(dst, krow[j % 2][:, :, :]).then_inc(krow_out[j % 2], 16)
                    else:
                        sp.dma_start(A["k_s"][:, f * P:(f + 1) * P], krow[j % 2][0:DEC, 0, :])\
                            .then_inc(krow_out[j % 2], 16)
            sp.wait_ge(p_read, 2)
            sp.dma_start(A["pool_p"][:, :], prow[0][:, :]).then_inc(prow_out, 16)
            sp.dma_start(A["pool_s"][:, :], prow[1][:, :]).then_inc(prow_out, 16)
            sp.wait_ge(prow_out, 32)
            for b in range(NB):
                sp.wait_ge(stage_out[b], 16 * stores_before(len(jobs), b))
            for b in range(2):
                sp.wait_ge(krow_out[b], 16 * (n_k // 2))

        @block.scalar
        def _(act):
            act.dma_start(w_pool[:, :, :], A["w_pool"].rearrange("g c d -> c g d")).then_inc(pool_in, 16)
            act.wait_ge(hist_clear, 1)
            act.dma_start(pTs[:, :, PAD - HIST:PAD], A["histT"][:, :, :]).then_inc(pool_in, 16)
            for j, (kind, f, r) in enumerate(jobs):
                act.wait_ge(z_done, j + 1)
                z = ps_z[j % NB]
                if kind == "p":
                    c0, n = RANGES[r]
                    dst = pT[:, f, PAD + c0:PAD + c0 + n] if r < 2 else pTs[:, f, PAD:PAD + DEC]
                    nc.scalar.activation(dst, z[:, 0:n], ACT.Copy).then_inc(z_read, 1)
                    continue
                if stores_before(j, j % NB):
                    act.wait_ge(stage_out[j % NB], 16 * stores_before(j, j % NB))
                if kind == "k" and j >= NB:
                    act.wait_ge(k_tr, j - NB + 1)
                elif kind == "q":
                    act.wait_ge(k_tr, n_k)
                if kind == "v":
                    rows = TILES[f][1]
                    nc.scalar.activation(stage[j % NB][0:rows, :], z[0:rows, :], ACT.Copy).then_inc(z_read, 1)
                else:
                    n = RANGES[r][1]
                    nc.scalar.activation(stage[j % NB][:, 0:n], z[:, 0:n], ACT.Copy,
                                         scale=(HD ** -0.5 if kind == "q" else 1.0)).then_inc(z_read, 1)
            for m, (g, r) in enumerate((g, r) for g in range(FA) for r in range(len(RANGES))):
                c0, n = RANGES[r]
                act.wait_ge(mix_done, m + 1)
                nc.scalar.activation(oT[:, FA + g, c0:c0 + n], ps_k[m % 2][:, 0:n], ACT.Copy,
                                     scale=gains[:, G_POOL + g:G_POOL + g + 1]).then_inc(mix_read, 1)

        @block.vector
        def _(dve):
            own = Chain(dve, dve_own)
            for k in range(KC):
                for s, (c0, n) in enumerate(((0, SEQ), (SEQ, DEC))):
                    last = nc.vector.tensor_scalar(hT[:, k, c0:c0 + n], hT[:, k, c0:c0 + n], acol[:, s, k:k + 1],
                                                   bcol[:, s, k:k + 1], ALU.mult, ALU.add)
                last.then_inc(h_done, 1)
            nc.vector.memset(pTs[:, :, 0:PAD], 0.0).then_inc(hist_clear, 1)
            own.add(nc.vector.memset(pT[:, :, 0:PAD], 0.0))
            for j in range(n_k):
                r = jobs[j][2]
                dve.wait_ge(k_tr, j + 1)
                if j >= 2:
                    dve.wait_ge(krow_out[j % 2], 16 * (j // 2))
                if r < 2:
                    nc.vector.tensor_copy(krow[j % 2][:, :, :], ps_k[j % 2][:, :].rearrange("p (t c) -> p t c", t=4))\
                        .then_inc(k_read, 1)
                else:
                    nc.vector.tensor_copy(krow[j % 2][0:DEC, 0, :], ps_k[j % 2][0:DEC, 0:P]).then_inc(k_read, 1)
            for s in range(2):
                dve.wait_ge(p_tr, s + 1)
                nc.vector.tensor_copy(prow[s][:, :], ps_t[s][0:HIST, :]).then_inc(p_read, 1)
            dve.wait_ge(pool_in, 32)
            for g, w in enumerate(WINDOWS):
                for s, (src, n) in enumerate(((pT, SEQ), (pTs, DEC))):
                    full = PAD + n
                    at, cur = src[:, g, :], None
                    for level in range(g + 1):
                        step = 1 << level
                        lo = 2 * step - 1
                        new = sums[level % 2]
                        own.link(nc.vector.tensor_tensor(new[:, lo:full], at[:, lo:full], at[:, lo - step:full - step],
                                                         ALU.add))
                        at = new
                    src_g = src[:, g, PAD:full]
                    if s == 0:
                        inv = const[:, C_INVC + 16 * g:C_INVC + 16 * (g + 1)]
                        own.link(nc.vector.tensor_tensor(at[:, PAD:PAD + 16], at[:, PAD:PAD + 16], inv, ALU.mult))
                        own.link(nc.vector.tensor_tensor(src_g[:, 0:16], at[:, PAD:PAD + 16], src_g[:, 0:16],
                                                         ALU.subtract))
                        own.link(nc.vector.scalar_tensor_tensor(out=src_g[:, 16:n], in0=at[:, PAD + 16:full],
                                                                scalar=1.0 / w, in1=src_g[:, 16:n], op0=ALU.mult,
                                                                op1=ALU.subtract))
                    else:
                        own.link(nc.vector.scalar_tensor_tensor(out=src_g[:, :], in0=at[:, PAD:full], scalar=1.0 / w,
                                                                in1=src_g[:, :], op0=ALU.mult, op1=ALU.subtract))
                dve.sem_inc(pooled_done, 1)

        @block.tensor
        def _(pe):
            def key_rows(j):
                n = RANGES[jobs[j][2]][1]
                pe.wait_ge(z_read, j + 1)
                if j >= 2:
                    pe.wait_ge(k_read, j - 1)
                for i in range(-(-n // P)):
                    m = min(P, n - i * P)
                    last = nc.tensor.transpose(ps_k[j % 2][0:m, i * P:(i + 1) * P], stage[j % NB][:, i * P:i * P + m],
                                               ident)
                last.then_inc(k_tr, 1)

            for j, (kind, f, r) in enumerate(jobs):
                if j >= NB:
                    pe.wait_ge(z_read, j - NB + 1)
                z = ps_z[j % NB]
                for k in range(KC):
                    if j == 0:
                        pe.wait_ge(h_done, k + 1)
                        if k == 0:
                            pe.wait_ge(S["w_in_full"], 16 * KC)
                    if kind == "v":
                        t0, rows = TILES[f]
                        last = nc.tensor.matmul(z[0:rows, :], hT[:, k, t0:t0 + rows], w_in[:, k, 2 * DA:3 * DA],
                                                start=(k == 0), stop=(k == KC - 1))
                    else:
                        c0, n = RANGES[r]
                        w0 = {"q": 0, "k": DA, "p": 3 * DA}[kind] + f * P
                        last = nc.tensor.matmul(z[:, 0:n], w_in[:, k, w0:w0 + P], hT[:, k, c0:c0 + n],
                                                start=(k == 0), stop=(k == KC - 1))
                last.then_inc(z_done, 1)
                if 1 <= j <= n_k:
                    key_rows(j - 1)
                if j == last_p:
                    pe.wait_ge(z_read, last_p)
                    for s, (src, n) in enumerate(((pT, SEQ), (pTs, DEC))):
                        for g in range(FA):
                            last = nc.tensor.transpose(ps_t[s][0:HIST, g * P:(g + 1) * P],
                                                       src[:, g, PAD + n - HIST:PAD + n], ident)
                        last.then_inc(p_tr, 1)
            pe.wait_ge(pool_in, 32)
            m = 0
            for g in range(FA):
                pe.wait_ge(pooled_done, g + 1)
                for r, (c0, n) in enumerate(RANGES):
                    pe.wait_ge(mix_read, m - 1) if m >= 2 else pe.wait_ge(k_read, n_k)
                    src = pT[:, g, PAD + c0:PAD + c0 + n] if r < 2 else pTs[:, g, PAD:PAD + DEC]
                    nc.tensor.matmul(ps_k[m % 2][:, 0:n], w_pool[:, g, :], src, start=True, stop=True)\
                        .then_inc(mix_done, 1)
                    m += 1


def attention(nc, A, S):
    sem = S["sem"]
    const, oT = S["const"], S["oT"]
    ntri, nones = const[:, C_NTRI:C_NTRI + P], const[:, C_NONES:C_NONES + P]
    mask = const[:, C_MASK:C_MASK + P]
    NZ, NS, NR, AHEAD = 4, 4, 3, 2
    LEAD = 4
    units = []
    for qc in range(2):
        top = 4 * qc + 3
        for kb in range(top, -1, -1):
            c0 = max(0, kb * P - qc * 512)
            for h in range(2):
                units.append(dict(h=h, bank=qc, kb=kb, c0=c0, c1=512, first=kb == top, diag=kb >= 4 * qc,
                                  last=kb == 0, opens=kb == top and h == 0, closes=kb == 0 and h == 1))
    for kb in (2, 1, 0):
        units.append(dict(h=2, bank=2, kb=kb, c0=0, c1=P, first=kb == 2, diag=kb == 2, last=kb == 0,
                          opens=kb == 2, closes=kb == 0))
    NU = len(units)
    seen = {0: 0, 1: 0, 2: 0}
    for u in units:
        if u["first"]:
            seen[u["h"]] = 0
        u["par"] = seen[u["h"]] % NR
        seen[u["h"]] += 1
    ND = sum(u["diag"] for u in units)
    for m, u in enumerate(units):
        u["nd"] = sum(v["diag"] for v in units[:m])
    PAIRS = FA
    with ExitStack() as st:
        sb = lambda n, s, d=F32: st.enter_context(nc.sbuf_tensor(n, s, d))
        ps = lambda n: st.enter_context(nc.psum_tensor(n, [P, 512], F32))
        kT = [sb(f"kT{i}", [P, SEQ]) for i in range(2)]
        kTs = [sb(f"kTs{i}", [P, 3 * P]) for i in range(2)]
        qz = [sb(f"qz{i}", [P, 2, SEQ]) for i in range(2)]
        qzs = [sb(f"qzs{i}", [P, P]) for i in range(2)]
        vz = [sb(f"vz{i}", [P, 2, NT, P]) for i in range(2)]
        vzs = [sb(f"vzs{i}", [P, 2, 3, P]) for i in range(2)]
        lt = [sb(f"lt{i}", [P, 512]) for i in range(NS)]
        spt = [sb(f"spt{i}", [P, 512]) for i in range(NS)]
        wt = [sb(f"wt{i}", [P, 512]) for i in range(NS)]
        R = [[sb(f"R{h}{i}", [P, 512]) for i in range(NR)] for h in range(3)]
        ps_z = [ps(f"ps_s{i}") for i in range(NZ)]
        ps_o = [ps(f"ps_o{i}") for i in range(3)]
        cleared = sem("att_cleared")
        full = [sem(f"att_full{i}") for i in range(2)]
        z_done, l_done, sp_done, r_done, t_done, e_done, w_done, pv_done, o_read = (
            sem(n) for n in ("att_z", "att_l", "att_sp", "att_r", "att_t", "att_e", "att_w", "att_pv", "att_o"))
        act_own = sem("act_own2")
        dve_own = sem("dve_own2")
        NLOAD = 15
        block = st.enter_context(nc.Block())

        def seqs(i, b):
            return i * (2 * NU) + b * NU

        @block.sync
        def _(sp):
            sp.wait_ge(cleared, 1)

            def load(pair, b):
                f0 = pair * P

                def go(dst, src):
                    sp.dma_start(dst, src).then_inc(full[b], 16)

                rows = bass.ds(f0, P)
                go(kT[b][:, :], S["kT_d"][rows, 0:SEQ])
                go(kTs[b][:, 0:PAST], A["kpastT"][rows, :])
                go(kTs[b][:, PAST:PAST + DEC], S["kT_d"][rows, SEQ:TOK])
                for h in range(2):
                    hr = slice(h * HD, (h + 1) * HD)
                    hrow = bass.ds(f0 + h * HD, HD)
                    go(qz[b][hr, h, :], S["qT_d"][hrow, 0:SEQ])
                    go(qzs[b][hr, hr], S["qT_d"][hrow, SEQ:TOK])
                    for half in range(2):
                        part = slice(half * NT // 2, (half + 1) * NT // 2)
                        go(vz[b][:, h, part, hr],
                           A["v_p"][half * SEQ // 2:(half + 1) * SEQ // 2, hrow].rearrange("(t p) c -> p t c", p=P))
                    go(vzs[b][:, h, 0:2, hr], A["vpast"][:, hrow].rearrange("(t p) c -> p t c", p=P))
                    go(vzs[b][0:DEC, h, 2, hr], A["v_s"][:, hrow])

            load(0, 0)
            load(1, 1)
            w_v = A["w_out"].rearrange("(k p) n -> p k n", p=P)
            for k in range(KC):
                sp.dma_start(S["w_out"][:, k, :], w_v[:, k, :]).then_inc(S["w_out_full"], 16)
            sp.dma_start(S["gpost"][:, :], A["rows"][0:1, :].broadcast_to([P, D])).then_inc(S["w_out_full"], 16)
            sp.dma_start(S["gpre"][:, :], A["rows"][1:2, :].broadcast_to([P, D])).then_inc(S["w_out_full"], 16)
            gate_vectors(sp, S, 0, S["w_out_full"])
            for b in range(2):
                sp.wait_ge(pv_done, LEAD + (b + 1) * NU)
                load(2 + b, b)

        @block.gpsimd
        def _(pool):
            for b in range(2):
                nc.gpsimd.memset(kTs[b][:, :], 0.0)
                nc.gpsimd.memset(qz[b][:, :, :], 0.0)
                nc.gpsimd.memset(qzs[b][:, :], 0.0)
                nc.gpsimd.memset(vz[b][:, :, :, :], 0.0)
                last = nc.gpsimd.memset(vzs[b][:, :, :, :], 0.0)
            last.then_inc(cleared, 1)

        @block.tensor
        def _(pe):
            pe.sem_inc(t_done, LEAD)
            pe.sem_inc(pv_done, LEAD)
            with pe.Fori(0, PAIRS // 2) as i:
                for b in range(2):
                    n0 = seqs(i, b)
                    pe.wait_ge(full[b], i * (16 * NLOAD) + 16 * NLOAD)

                    def score(m):
                        u = units[m]
                        pe.wait_ge(e_done, n0 + (LEAD + m - NZ + 1))
                        z = ps_z[m % NZ]
                        if u["h"] == 2:
                            lhsT, rhs = kTs[b][:, u["kb"] * P:(u["kb"] + 1) * P], qzs[b][:, :]
                        else:
                            q0 = u["bank"] * 512 + u["c0"]
                            lhsT = kT[b][:, u["kb"] * P:(u["kb"] + 1) * P]
                            rhs = qz[b][:, u["h"], q0:(u["bank"] + 1) * 512]
                        nc.tensor.matmul(z[:, u["c0"]:u["c1"]], lhsT, rhs, start=True, stop=True,
                                         skip_group_check=True).then_inc(z_done, 1)

                    def after(m):
                        u = units[m]
                        z, c0, c1 = ps_z[m % NZ], u["c0"], u["c1"]
                        pe.wait_ge(sp_done, n0 + (LEAD + m + 1))
                        last = nc.tensor.matmul(z[:, c0:c1], ntri, spt[m % NS][:, c0:c1], start=False, stop=True,
                                                skip_group_check=True)
                        if not u["first"]:
                            lo = c0 + P if u["diag"] and u["h"] < 2 else c0
                            last = nc.tensor.matmul(z[:, lo:c1], nones, R[u["h"]][(u["par"] - 1) % NR][:, lo:c1],
                                                    start=False, stop=True, skip_group_check=True)
                        last.then_inc(t_done, 1)

                    def values(m):
                        u = units[m]
                        pe.wait_ge(e_done, n0 + (LEAD + m + 1))
                        if u["diag"]:
                            pe.wait_ge(w_done, i * (2 * ND) + (b * ND + u["nd"] + 1))
                        if u["opens"]:
                            pe.wait_ge(o_read, i * 6 + (3 * b + u["bank"] + 1))
                        o, c0, c1, w = ps_o[u["bank"]], u["c0"], u["c1"], wt[m % NS]
                        if u["h"] == 2:
                            for h in range(2):
                                last = nc.tensor.matmul(o[:, 0:DEC], vzs[b][:, h, u["kb"], :],
                                                        w[:, h * DEC:(h + 1) * DEC], start=u["opens"] and h == 0,
                                                        stop=u["closes"] and h == 1, skip_group_check=True)
                        else:
                            last = nc.tensor.matmul(o[:, c0:c1], vz[b][:, u["h"], u["kb"], :], w[:, c0:c1],
                                                    start=u["opens"], stop=u["closes"], skip_group_check=True)
                        last.then_inc(pv_done, 1)

                    for m in range(AHEAD):
                        score(m)
                    for m in range(NU):
                        if m + AHEAD < NU:
                            score(m + AHEAD)
                        after(m)
                        if m >= AHEAD:
                            values(m - AHEAD)
                    for m in range(NU - AHEAD, NU):
                        values(m)

        @block.scalar
        def _(act):
            own = Chain(act, act_own)
            PER = 2 * 2 * NU
            act.preload_act_table_set(LOG_EXP)
            act.sem_inc(e_done, LEAD)
            with act.Fori(0, PAIRS // 2) as i:
                own.base, own.n = i * PER, 0
                for b in range(2):
                    n0 = seqs(i, b)

                    def logs(m):
                        u = units[m]
                        c = slice(u["c0"], u["c1"])
                        act.wait_ge(z_done, n0 + (m + 1))
                        act.wait_ge(sp_done, n0 + (LEAD + m - NS + 1))
                        own.link(nc.scalar.activation(lt[m % NS][:, c], ps_z[m % NZ][:, c], ACT.Abs))
                        own.link(nc.scalar.activation(lt[m % NS][:, c], lt[m % NS][:, c], ACT.Exp, scale=-1.0))
                        nc.scalar.activation(lt[m % NS][:, c], lt[m % NS][:, c], ACT.Ln, bias=1.0).then_inc(l_done, 1)

                    def weights(m):
                        u = units[m]
                        c = slice(u["c0"], u["c1"])
                        act.wait_ge(t_done, n0 + (LEAD + m + 1))
                        act.wait_ge(pv_done, n0 + (LEAD + m - NS + 1))
                        nc.scalar.activation(wt[m % NS][:, c], ps_z[m % NZ][:, c], ACT.Exp).then_inc(e_done, 1)

                    for m in range(AHEAD):
                        logs(m)
                    for m in range(NU):
                        if m + AHEAD < NU:
                            logs(m + AHEAD)
                        weights(m)
                assert own.n == PER

        @block.vector
        def _(dve):
            own = Chain(dve, dve_own)
            dve.sem_inc(o_read, 3)
            dve.sem_inc(sp_done, LEAD)
            PER = 2 * sum(1 + u["diag"] for u in units)
            with dve.Fori(0, PAIRS // 2) as i:
                own.base, own.n = i * PER, 0
                for b in range(2):
                    n0 = seqs(i, b)

                    def masked(tile, u):
                        if u["h"] == 2:
                            at = tile[:, 0:P].rearrange("p (h q) -> p h q", h=2)
                            by = mask[:, None, 0:DEC].broadcast_to([P, 2, DEC])
                        else:
                            at, by = tile[:, u["c0"]:u["c0"] + P], mask
                        return nc.vector.tensor_tensor(at, at, by, ALU.mult)

                    def softplus(m):
                        u = units[m]
                        c = slice(u["c0"], u["c1"])
                        dve.wait_ge(l_done, n0 + (m + 1))
                        dve.wait_ge(t_done, n0 + (LEAD + m - NS + 1))
                        op = nc.vector.scalar_tensor_tensor(out=spt[m % NS][:, c], in0=ps_z[m % NZ][:, c], scalar=0.0,
                                                            in1=lt[m % NS][:, c], op0=ALU.max, op1=ALU.add)
                        own.link(op)
                        if u["diag"]:
                            own.link(masked(spt[m % NS], u))
                        if u["h"] == 2 and not u["last"]:
                            dve.wait_ge(t_done, n0 + (LEAD + m - 1))
                        if not u["last"]:
                            new, old = R[u["h"]][u["par"]], R[u["h"]][(u["par"] - 1) % NR]
                            lo = u["c0"] + P if u["diag"] and u["h"] < 2 else u["c0"]
                            if u["first"]:
                                nc.vector.tensor_copy(new[:, c], spt[m % NS][:, c]).then_inc(r_done, 1)
                            else:
                                if lo > u["c0"]:
                                    nc.vector.tensor_copy(new[:, u["c0"]:lo], spt[m % NS][:, u["c0"]:lo])
                                nc.vector.tensor_tensor(new[:, lo:u["c1"]], old[:, lo:u["c1"]],
                                                        spt[m % NS][:, lo:u["c1"]], ALU.add).then_inc(r_done, 1)
                        else:
                            dve.sem_inc(r_done, 1)
                        dve.wait_ge(r_done, n0 + (m + 1))
                        dve.sem_inc(sp_done, 1)

                    def finish(m):
                        u = units[m]
                        if not u["diag"]:
                            return
                        dve.wait_ge(e_done, n0 + (LEAD + m + 1))
                        masked(wt[m % NS], u).then_inc(w_done, 1)

                    def read(m):
                        u = units[m]
                        if u["closes"]:
                            dve.wait_ge(pv_done, n0 + (LEAD + m + 1))
                            c0, n = RANGES[u["bank"]]
                            nc.vector.tensor_copy(oT[:, bass.ds(i * 2 + b, 1), c0:c0 + n],
                                                  ps_o[u["bank"]][:, None, 0:n]).then_inc(o_read, 1)

                    for m in range(AHEAD):
                        softplus(m)
                    for m in range(NU):
                        if m + AHEAD < NU:
                            softplus(m + AHEAD)
                        finish(m)
                        if m >= 4:
                            read(m - 4)
                    for m in range(NU - 4, NU):
                        read(m)
                assert own.n == PER, (own.n, PER)


def gate_vectors(eng, S, s, done):
    for dst, m in (("g1", 2), ("b2", 3), ("a2", 4)):
        eng.dma_start(S[dst][:, :], S["mod_d"][s:s + 1, m * D:(m + 1) * D].broadcast_to([P, D])).then_inc(done, 16)


def output(nc, A, S):
    sem = S["sem"]
    const, gains = S["const"], S["gains"]
    oT, w_out, g1, a2, b2, gpost, gpre = (S[n] for n in ("oT", "w_out", "g1", "a2", "b2", "gpost", "gpre"))
    NTILE = len(TILES)
    NX = 3
    with ExitStack() as st:
        sb = lambda n, s, d=F32: st.enter_context(nc.sbuf_tensor(n, s, d))
        xt = [sb(f"xo{i}", [P, D]) for i in range(NX)]
        ot = [sb(f"ot{i}", [P, D]) for i in range(2)]
        junk = sb("junk3", [P, D])
        h2 = [sb(f"h2o{i}", [P, D]) for i in range(2)]
        sq = sb("sq3", [P, KC, P])
        part = sb("part", [P, 512])
        msq = sb("msq3", [P, NTILE, 4])
        rs = sb("rs3", [P, NTILE, 4])
        tmp = sb("tmp3", [P, 2])
        ones = sb("ones3", [P, 1])
        ps_a = [st.enter_context(nc.psum_tensor(f"ps_a{i}", [P, 512], F32)) for i in range(3)]
        ps_b = [st.enter_context(nc.psum_tensor(f"ps_b{i}", [P, 512], F32)) for i in range(3)]
        ps_n = st.enter_context(nc.psum_tensor("ps_n", [P, 512], F32))
        vec2_full = sem("vec2_full")
        x_full = [sem(f"xo_full{i}") for i in range(NX)]
        sq_done, n_done, ab_done, ab_read = (sem(n) for n in ("sq_done3", "n_done", "ab_done", "ab_read"))
        ask, answer, o_sq, x1_sq, act_own, dve_own = (
            sem(n) for n in ("ask3", "answer3", "o_sq", "x1_sq", "act_own3", "dve_own3"))
        x1_done, h2_done = sem("x1_done"), sem("h2_done")
        x1_out = [sem(f"x1_out{i}") for i in range(NX)]
        h2_out = [sem(f"h2_out{i}") for i in range(2)]
        block = st.enter_context(nc.Block())
        w_scaled = S["w_scaled"]

        def stages(t):
            pairs = [(m, t - m) for m in range(3) if 0 <= t - m < NTILE]
            return pairs if t <= NT else pairs[::-1]

        def load(eng, t):
            t0, rows = TILES[t]
            src = A["x_p"][t0:t0 + rows, :] if t < NT else A["x_s"][:, :]
            eng.dma_start(xt[t % NX][0:rows, :], src).then_inc(x_full[t % NX], 16)

        @block.sync
        def _(sp):
            for t in range(NX):
                load(sp, t)
            for t, (t0, rows) in enumerate(TILES):
                sp.wait_ge(h2_done, t + 1)
                sp.dma_start(S["x1_d"][t0:t0 + rows, :], xt[t % NX][0:rows, :]).then_inc(x1_out[t % NX], 16)
                sp.dma_start(S["h2_d"][t0:t0 + rows, :], h2[t % 2][0:rows, :]).then_inc(h2_out[t % 2], 16)
                if t + NX < NTILE:
                    sp.wait_ge(x1_out[t % NX], 16 * (t // NX + 1))
                    load(sp, t + NX)
                if t == NT - 1:
                    gate_vectors(sp, S, 1, vec2_full)
            for b in range(NX):
                sp.wait_ge(x1_out[b], 16 * (NTILE // NX))
            sp.wait_ge(h2_out[0], 16 * 5)
            sp.wait_ge(h2_out[1], 16 * 4)

        @block.scalar
        def _(act):
            act.preload_act_table_set(LOG_EXP)
            w_v = A["w_query"].rearrange("(k p) n -> p k n", p=P)
            for k in range(KC):
                act.dma_start(S["w_q"][:, k, :], w_v[:, k, :]).then_inc(S["w_q_full"], 16)
            act.dma_start(S["keys"][:, :, :], A["keysT"][:, :, :]).then_inc(S["w_q_full"], 16)
            own = Chain(act, act_own)
            asked = [0]

            def roots(rows, t, cols):
                asked[0] += 1
                act.wait_ge(ask, asked[0])
                own.link(nc.scalar.activation(rs[0:rows, t, cols], msq[0:rows, t, cols], ACT.Ln))
                nc.scalar.activation(rs[0:rows, t, cols], rs[0:rows, t, cols], ACT.Exp, scale=-0.5).then_inc(answer, 1)

            def squares(t):
                t0, rows = TILES[t]
                if t:
                    act.wait_ge(n_done, t)
                nc.scalar.activation(sq[:, :, 0:rows], oT[:, :, t0:t0 + rows], ACT.Square).then_inc(sq_done, 1)

            squares(0)
            for step in range(NTILE + 2):
                for m, t in stages(step):
                    rows = TILES[t][1]
                    if m == 0:
                        roots(rows, t, slice(0, 2))
                        if t + 1 < NTILE:
                            squares(t + 1)
                        act.wait_ge(ab_read, 2 * (t + 1))
                        nc.scalar.activation(junk[0:rows, :], ot[t % 2][0:rows, :], ACT.Square,
                                             accum_out=msq[0:rows, t, 2:3]).then_inc(o_sq, 1)
                    elif m == 1:
                        roots(rows, t, slice(2, 3))
                        act.wait_ge(x1_done, t + 1)
                        nc.scalar.activation(junk[0:rows, :], xt[t % NX][0:rows, :], ACT.Square,
                                             accum_out=msq[0:rows, t, 3:4]).then_inc(x1_sq, 1)
                    else:
                        roots(rows, t, slice(3, 4))

        @block.vector
        def _(dve):
            own = Chain(dve, dve_own)
            own.add(nc.vector.memset(ones[:, :], 1.0))
            dve.wait_ge(S["w_out_full"], 16 * (KC + 5))
            for k in range(KC):
                own.add(nc.vector.tensor_scalar(w_out[:, k, :], w_out[:, k, :], gains[:, G_OUT + k:G_OUT + k + 1], None,
                                                ALU.mult))
            own.wait()
            dve.sem_inc(w_scaled, 1)

            def prepare():
                own.link(nc.vector.tensor_tensor(g1[:, :], g1[:, :], gpost[:, :], ALU.mult))
                own.link(nc.vector.scalar_tensor_tensor(out=a2[:, :], in0=a2[:, :], scalar=1.0, in1=gpre[:, :],
                                                        op0=ALU.add, op1=ALU.mult))

            prepare()
            asked = [0]

            def root(rows, t, cols, src, n):
                asked[0] += 1
                own.link(nc.vector.tensor_scalar(msq[0:rows, t, cols], src, 1.0 / n, EPS, ALU.mult, ALU.add))
                rstd_steps(own, nc, msq[0:rows, t, cols], rs[0:rows, t, cols],
                           tmp[0:rows, 0:cols.stop - cols.start],
                           lambda: dve.sem_inc(ask, 1), lambda: dve.wait_ge(answer, asked[0]))

            def product(t, rows):
                dve.wait_ge(n_done, t + 1)
                root(rows, t, slice(0, 2), ps_n[0:rows, 2 * t:2 * t + 2], DA)
                for half in range(2):
                    j = 2 * t + half
                    dve.wait_ge(ab_done, j + 1)
                    own.link(nc.vector.tensor_scalar(part[0:rows, :], ps_a[j % 3][0:rows, :], rs[0:rows, t, 0:1], None,
                                                     ALU.mult))
                    nc.vector.scalar_tensor_tensor(out=ot[t % 2][0:rows, 512 * half:512 * (half + 1)],
                                                   in0=ps_b[j % 3][0:rows, :], scalar=rs[0:rows, t, 1:2],
                                                   in1=part[0:rows, :], op0=ALU.mult, op1=ALU.add).then_inc(ab_read, 1)
                    dve.wait_ge(ab_read, j + 1)

            def residual(t, rows):
                if t == NT:
                    dve.wait_ge(vec2_full, 48)
                    prepare()
                dve.wait_ge(o_sq, t + 1)
                root(rows, t, slice(2, 3), msq[0:rows, t, 2:3], D)
                o = ot[t % 2][0:rows, :]
                own.link(nc.vector.scalar_tensor_tensor(out=o, in0=o, scalar=rs[0:rows, t, 2:3],
                                                        in1=g1[0:rows, :], op0=ALU.mult, op1=ALU.mult))
                dve.wait_ge(x_full[t % NX], 16 * (t // NX + 1))
                nc.vector.tensor_tensor(xt[t % NX][0:rows, :], xt[t % NX][0:rows, :], o, ALU.add).then_inc(x1_done, 1)

            def second(t, rows):
                dve.wait_ge(x1_sq, t + 1)
                root(rows, t, slice(3, 4), msq[0:rows, t, 3:4], D)
                if t >= 2:
                    dve.wait_ge(h2_out[t % 2], 16 * (t // 2))
                own.link(nc.vector.scalar_tensor_tensor(out=h2[t % 2][0:rows, :], in0=xt[t % NX][0:rows, :],
                                                        scalar=rs[0:rows, t, 3:4], in1=a2[0:rows, :], op0=ALU.mult,
                                                        op1=ALU.mult))
                nc.vector.tensor_tensor(h2[t % 2][0:rows, :], h2[t % 2][0:rows, :], b2[0:rows, :], ALU.add)\
                    .then_inc(h2_done, 1)

            for step in range(NTILE + 2):
                for m, t in stages(step):
                    (product, residual, second)[m](t, TILES[t][1])

        @block.tensor
        def _(pe):
            pe.wait_ge(w_scaled, 1)
            for t, (t0, rows) in enumerate(TILES):
                pe.wait_ge(sq_done, t + 1)
                for m in range(2):
                    for f in range(FA):
                        last = nc.tensor.matmul(ps_n[0:rows, 2 * t + m:2 * t + m + 1], sq[:, FA * m + f, 0:rows],
                                                ones[:, :], start=(f == 0), stop=(f == FA - 1), skip_group_check=True)
                last.then_inc(n_done, 1)
                for half in range(2):
                    j = 2 * t + half
                    if j >= 3:
                        pe.wait_ge(ab_read, j - 2)
                    for m, bank in enumerate((ps_a[j % 3], ps_b[j % 3])):
                        for f in range(FA):
                            last = nc.tensor.matmul(bank[0:rows, :], oT[:, FA * m + f, t0:t0 + rows],
                                                    w_out[:, FA * m + f, 512 * half:512 * (half + 1)],
                                                    start=(f == 0), stop=(f == FA - 1))
                    last.then_inc(ab_done, 1)


def experts(nc, A, S):
    sem = S["sem"]
    const = S["const"]
    ident, iota = const[:, C_ID:C_ID + P], const[:, C_IOTA:C_IOTA + TOPK]
    w_q, keys = S["w_q"], S["keys"]
    with ExitStack() as st:
        sb = lambda n, s, d=F32: st.enter_context(nc.sbuf_tensor(n, s, d))
        ps = lambda n, w=512: st.enter_context(nc.psum_tensor(n, [P, w], F32))
        urow = [sb(f"urow{i}", [P, D]) for i in range(RING)]
        vrow = [sb(f"vrow{i}", [P, D]) for i in range(RING)]
        diag = [sb(f"diag{i}", [P, P]) for i in range(DIAGS)]
        h2n = sb("h2n", [P, D])
        h2T = sb("h2T", [P, KC, P])
        x1 = sb("x1e", [P, D])
        y = sb("ye", [P, D])
        gpost = sb("gpost4", [P, D])
        g2 = [sb(f"g2_{i}", [P, D]) for i in range(2)]
        qTs = sb("qTs", [P, 2, P])
        srep = sb("srep", [P, 2, NKEY])
        v16 = sb("v16", [P, 2, TOPK])
        i16 = sb("i16", [P, 2, TOPK], U32)
        i16f = sb("i16f", [P, 2, TOPK])
        cand = sb("cand", [P, TOPK, TOPK])
        crep = sb("crep", [P, TOPK, TOPK])
        best = sb("best", [P, TOPK])
        sel = sb("sel", [P, TOPK], U32)
        selij = sb("selij", [P, 2, TOPK], U32)
        selijf = sb("selijf", [P, 2, TOPK])
        onehot = sb("onehot", [P, 2 * TOPK, TOPK])
        picked = sb("picked", [P, 2, TOPK])
        idxf = sb("idxf", [P, TOPK])
        idx = sb("idx", [P, SLOTS], U32)
        gexp = sb("gexp", [P, TOPK])
        gsum = sb("gsum", [P, 1])
        gate = sb("gate", [P, SLOTS])
        dots = [sb(f"dots{i}", [P, TOPK]) for i in range(2)]
        gelu = [sb(f"gelu{i}", [P, TOPK]) for i in range(2)]
        wgt = [sb(f"wgt{i}", [P, TOPK]) for i in range(2)]
        msq = sb("msq4", [P, 1])
        rs = sb("rs4", [P, 1])
        tmp = sb("tmp4", [P, 1])
        ps_y = st.enter_context(nc.psum_tensor("ps_y", [P, D], F32))
        ps_h = st.enter_context(nc.psum_tensor("ps_h", [P, D], F32))
        ps_q, ps_t = ps("ps_q"), ps("ps_tr4")
        ps_s = [ps(f"ps_s4{i}") for i in range(2)]

        u_full = [sem(f"u_full{i}") for i in range(RING)]
        v_full = [sem(f"v_full{i}") for i in range(RING)]
        (u_used, v_used, h2_in, x1_in, g2_in, h2_tr, h2T_done, h2_copied, q_done, q_ready, s_done, s_read, idx_ready,
         gate_ask, gate_exp, dots_done, gelu_done, w_ready, diag_ready, y_sq, y_ask, y_root, y_free, y_done,
         y_out) = (sem(n) for n in (
             "u_used", "v_used", "h2_in", "x1_in", "g2_in", "h2_tr", "h2T_done", "h2_copied", "q_done", "q_ready",
             "s_done", "s_read", "idx_ready", "gate_ask", "gate_exp", "dots_done", "gelu_done", "w_ready",
             "diag_ready", "y_sq", "y_ask", "y_root", "y_free", "y_done", "y_out"))
        act_own, dve_own = sem("act_own4"), sem("dve_own4")
        pool_passed, dve_passed = sem("pool_passed"), sem("dve_passed")
        block = st.enter_context(nc.Block())

        def run(eng, start, body):
            start()
            body(0, DEC, P, None)
            with eng.Fori(0, NT - 1) as i:
                body(i + 1, P, P, i)
            body(NT, P, 0, NT - 1)

        @block.sync
        def _(sp):
            for i in range(2):
                sp.dma_start(g2[i][:, :], S["mod_d"][i:i + 1, 5 * D:6 * D].broadcast_to([P, D])).then_inc(g2_in, 16)
            sp.dma_start(gpost[:, :], A["rows"][2:3, :].broadcast_to([P, D])).then_inc(g2_in, 16)

            def start():
                sp.dma_start(h2n[0:DEC, :], S["h2_d"][SEQ:TOK, :]).then_inc(h2_in, 16)

            def body(n, rows, nxt, tile):
                if nxt:
                    sp.wait_ge(h2_copied, n * 2 + 2)
                    sp.wait_ge(h2_tr, n * 2 + 2)
                    row0 = 0 if tile is None else tile * P + P
                    sp.dma_start(h2n[:, :], S["h2_d"][bass.ds(row0, P), :]).then_inc(h2_in, 16)
                row0 = SEQ if tile is None else tile * P
                if tile is not None:
                    sp.wait_ge(y_done, n)
                sp.dma_start(x1[0:rows, :], S["x1_d"][bass.ds(row0, rows), :]).then_inc(x1_in, 16)
                sp.wait_ge(y_done, n + 1)
                dst = A["y_s"][:, :] if tile is None else A["y_p"][bass.ds(row0, rows), :]
                sp.dma_start(dst, y[0:rows, :]).then_inc(y_out, 16)

            run(sp, start, body)
            sp.wait_ge(y_out, 16 * (NT + 1))

        @block.gpsimd
        def _(pool):
            def gather(table, ring, full, h, k, rows):
                nc.gpsimd.indirect_dma_start(
                    ring[(TOPK * h + k) % RING][0:rows, :], None, A[table][:, :],
                    bass.IndirectOffsetOnAxis(ap=idx[0:rows, TOPK * h + k:TOPK * h + k + 1], axis=0))\
                    .then_inc(full[k % RING], 16)

            def start():
                pool.wait_ge(idx_ready, 1)
                for k in range(TOPK):
                    if k >= RING:
                        pool.wait_ge(u_used, k - RING + 1)
                    gather("u_tab", urow, u_full, 0, k, DEC)

            def body(n, rows, nxt, tile):
                for h in range(PH):
                    ahead = h < PH - 1 or nxt
                    if ahead:
                        pool.wait_ge(idx_ready, n * PH + (h + 2))
                    for k in range(TOPK):
                        if ahead:
                            pool.wait_ge(u_used, n * SLOTS + (TOPK * (h + 1) + k - RING + 1))
                            pool.sem_inc(pool_passed, 1)
                            gather("u_tab", urow, u_full, (h + 1) % PH, k, rows if h < PH - 1 else nxt)
                        s = TOPK * h + k
                        if not (isinstance(n, int) and n == 0 and s < RING):
                            pool.wait_ge(v_used, n * SLOTS + (s - RING + 1))
                            pool.sem_inc(pool_passed, 1)
                        gather("v_tab", vrow, v_full, h, k, rows)

            run(pool, start, body)

        @block.scalar
        def _(act):
            own = Chain(act, act_own)

            def take_h2T(n, rows):
                for half in range(2):
                    act.wait_ge(h2_tr, n * 2 + (half + 1))
                    if half == 0 and not (isinstance(n, int) and n == 0):
                        act.wait_ge(q_done, n * PH)
                    nc.scalar.activation(h2T[:, 4 * half:4 * half + 4, 0:rows],
                                         ps_t[:, :].rearrange("p (k t) -> p k t", k=4)[:, :, 0:rows], ACT.Copy)\
                        .then_inc(h2T_done, 1)

            def take_q(n, h, rows):
                act.wait_ge(q_done, n * PH + (h + 1))
                if not (isinstance(n, int) and n == 0 and h == 0):
                    act.wait_ge(s_done, n * PH + h)
                nc.scalar.activation(qTs[:, :, 0:rows], ps_q[:, 0:2 * P].rearrange("p (k t) -> p k t", k=2)[:, :, 0:rows],
                                     ACT.Copy).then_inc(q_ready, 1)

            def copy_h2(n, rows, first=False):
                if first:
                    act.wait_ge(h2_in, 16)
                else:
                    act.wait_ge(u_used, n * SLOTS)
                    act.wait_ge(h2_in, n * 16 + 16)
                for half in range(2):
                    c = slice(512 * half, 512 * (half + 1))
                    nc.scalar.activation(ps_h[0:rows, c], h2n[0:rows, c], ACT.Copy).then_inc(h2_copied, 1)

            def exp_gate(n, h, rows):
                act.wait_ge(gate_ask, n * PH + (h + 1))
                nc.scalar.activation(gexp[0:rows, :], gexp[0:rows, :], ACT.Exp).then_inc(gate_exp, 1)

            def do_gelu(n, h, rows):
                act.wait_ge(dots_done, n * PH + (h + 1))
                nc.scalar.activation(gelu[h % 2][0:rows, :], dots[h % 2][0:rows, :], ACT.Gelu).then_inc(gelu_done, 1)

            def start():
                take_h2T(0, DEC)
                copy_h2(0, DEC, first=True)
                for h in range(PH):
                    take_q(0, h, DEC)
                    if h >= 1:
                        exp_gate(0, h - 1, DEC)
                do_gelu(0, 0, DEC)

            def body(n, rows, nxt, tile):
                for h in range(PH):
                    if h == 0 and nxt:
                        take_h2T(n + 1, nxt)
                    if h == PH - 1 and nxt:
                        copy_h2(n + 1, nxt)
                    act.wait_ge(w_ready, n * PH + (h + 1))
                    for k in range(TOPK):
                        s = TOPK * h + k
                        if not (isinstance(n, int) and n == 0 and s < DIAGS):
                            act.wait_ge(v_used, n * SLOTS + (s - DIAGS + 1))
                        nc.scalar.activation(diag[s % DIAGS][0:rows, 0:rows], ident[0:rows, 0:rows], ACT.Copy,
                                             scale=wgt[h % 2][0:rows, k:k + 1]).then_inc(diag_ready, 1)
                        if k == 3 and nxt:
                            take_q(n + 1, h, nxt)
                    if h == 0:
                        exp_gate(n, PH - 1, rows)
                    elif nxt:
                        exp_gate(n + 1, h - 1, nxt)
                    if h < PH - 1:
                        do_gelu(n, h + 1, rows)
                    elif nxt:
                        do_gelu(n + 1, 0, nxt)
                act.wait_ge(v_used, n * SLOTS + SLOTS)
                if tile is not None:
                    act.wait_ge(y_out, n * 16)
                nc.scalar.activation(y[0:rows, :], ps_y[0:rows, :], ACT.Square, accum_out=msq[0:rows, :])\
                    .then_inc(y_sq, 1)
                act.preload_act_table_set(LOG_EXP)
                act.wait_ge(y_ask, n + 1)
                own.base, own.n = n, 0
                own.link(nc.scalar.activation(rs[0:rows, :], msq[0:rows, :], ACT.Ln))
                nc.scalar.activation(rs[0:rows, :], rs[0:rows, :], ACT.Exp, scale=-0.5).then_inc(y_root, 1)

            run(act, start, body)

        @block.vector
        def _(dve):
            own = Chain(dve, dve_own)
            dve.wait_ge(g2_in, 48)
            for i in range(2):
                own.link(nc.vector.tensor_tensor(g2[i][:, :], g2[i][:, :], gpost[:, :], ALU.mult))

            def top16(values, src, rep, index):
                own.link_apart(nc.vector.max(values[:, 0:8], src), dve_passed)
                own.add(nc.vector.max_index(index[:, 0:8], values[:, 0:8], src))
                own.link_apart(nc.vector.match_replace(rep, values[:, 0:8], src, LOWEST), dve_passed)
                own.link_apart(nc.vector.max(values[:, 8:16], rep), dve_passed)
                own.link_apart(nc.vector.max_index(index[:, 8:16], values[:, 8:16], rep), dve_passed)

            def search(n, h, rows):
                r = slice(0, rows)
                s = ps_s[h % 2]
                dve.wait_ge(s_done, n * PH + (h + 1))
                dve.sem_inc(dve_passed, 1)
                for side in range(2):
                    top16(v16[r, side, :], s[r, side * P:(side + 1) * P], srep[r, side, :], i16[r, side, :])
                dve.sem_inc(s_read, 1)
                own.add(nc.vector.tensor_copy(i16f[r, :, :], i16[r, :, :]))
                own.link_apart(nc.vector.tensor_tensor(cand[r, :, :], v16[r, 0, :, None].broadcast_to([rows, TOPK, TOPK]),
                                                       v16[r, 1, None, :].broadcast_to([rows, TOPK, TOPK]), ALU.add),
                               dve_passed)
                flat = cand[r, :, :].rearrange("p a b -> p (a b)")
                top16(best[r, :], flat, crep[r, :, :].rearrange("p a b -> p (a b)"), sel[r, :])
                nc.vector.tensor_scalar(gexp[r, :], best[r, :], best[r, 0:1], None, ALU.subtract).then_inc(gate_ask, 1)
                own.add(nc.vector.tensor_scalar(selij[r, 0, :], sel[r, :], 4, None, ALU.logical_shift_right))
                own.link(nc.vector.tensor_scalar(selij[r, 1, :], sel[r, :], TOPK - 1, None, ALU.bitwise_and))
                own.link(nc.vector.tensor_copy(selijf[r, :, :], selij[r, :, :]))
                own.link(nc.vector.tensor_tensor(
                    onehot[r, :, :], selijf[r, :, :].rearrange("p s k -> p (s k)")[:, :, None]
                    .broadcast_to([rows, 2 * TOPK, TOPK]),
                    iota[r, None, :].broadcast_to([rows, 2 * TOPK, TOPK]), ALU.is_equal))
                for side in range(2):
                    at = onehot[r, side * TOPK:(side + 1) * TOPK, :]
                    own.link(nc.vector.tensor_tensor(at, at, i16f[r, side, None, :].broadcast_to([rows, TOPK, TOPK]),
                                                     ALU.mult))
                own.link(nc.vector.tensor_reduce(picked[r, :, :].rearrange("p s k -> p (s k)"), onehot[r, :, :],
                                                 AX_X, ALU.add))
                own.link(nc.vector.scalar_tensor_tensor(out=idxf[r, :], in0=picked[r, 0, :], scalar=float(NKEY),
                                                        in1=picked[r, 1, :], op0=ALU.mult, op1=ALU.add))
                if not (isinstance(n, int) and n == 0):
                    dve.wait_ge(v_used, (n - 1) * SLOTS + TOPK * (h + 1))
                nc.vector.tensor_copy(idx[r, TOPK * h:TOPK * (h + 1)], idxf[r, :]).then_inc(idx_ready, 1)
                dve.wait_ge(gate_exp, n * PH + (h + 1))
                own.link(nc.vector.tensor_reduce(gsum[r, :], gexp[r, :], AX_X, ALU.add))
                own.link(nc.vector.reciprocal(gsum[r, :], gsum[r, :]))
                own.link(nc.vector.tensor_scalar(gate[r, TOPK * h:TOPK * (h + 1)], gexp[r, :], gsum[r, 0:1], None,
                                                 ALU.mult))

            def products(n, h, rows):
                if isinstance(n, int) and n == 0 and h == 0:
                    dve.wait_ge(h2_copied, 2)
                elif h == 0:
                    dve.wait_ge(h2_copied, n * 2 + 2)
                if not (isinstance(n, int) and n == 0 and h < 2):
                    dve.wait_ge(gelu_done, n * PH + (h - 1))
                for k in range(TOPK):
                    s = TOPK * h + k
                    dve.wait_ge(u_full[s % RING], n * (16 * SLOTS // RING) + 16 * (s // RING + 1))
                    last = nc.vector.tensor_tensor_reduce(out=urow[s % RING][0:rows, :], in0=urow[s % RING][0:rows, :],
                                                          in1=ps_h[0:rows, :], scale=1.0, scalar=0.0, op0=ALU.mult,
                                                          op1=ALU.add, accum_out=dots[h % 2][0:rows, k:k + 1])
                    last.then_inc(u_used, 1)
                dve.wait_ge(u_used, n * SLOTS + TOPK * (h + 1))
                dve.sem_inc(dots_done, 1)

            def weights(n, h, rows):
                dve.wait_ge(gelu_done, n * PH + (h + 1))
                if not (isinstance(n, int) and n == 0 and h < 2):
                    dve.wait_ge(diag_ready, n * SLOTS + TOPK * (h - 1))
                nc.vector.tensor_tensor(wgt[h % 2][0:rows, :], gate[0:rows, TOPK * h:TOPK * (h + 1)],
                                        gelu[h % 2][0:rows, :], ALU.mult).then_inc(w_ready, 1)

            SEARCH = 28

            def start():
                for h in range(PH - 1):
                    search(0, h, DEC)
                products(0, 0, DEC)
                weights(0, 0, DEC)

            ahead = 2 + (PH - 1) * SEARCH
            per = PH * SEARCH + 5

            def body(n, rows, nxt, tile):
                own.base, own.n = n * per + ahead, 0
                for h in range(PH):
                    if h < PH - 1:
                        products(n, h + 1, rows)
                    elif nxt:
                        products(n + 1, 0, nxt)
                    if h == 0:
                        search(n, PH - 1, rows)
                    elif nxt:
                        search(n + 1, h - 1, nxt)
                    if h < PH - 1:
                        weights(n, h + 1, rows)
                    elif nxt:
                        weights(n + 1, 0, nxt)
                r = slice(0, rows)
                dve.wait_ge(y_sq, n + 1)
                own.link(nc.vector.tensor_scalar(msq[r, :], msq[r, :], 1.0 / D, EPS, ALU.mult, ALU.add))
                rstd_steps(own, nc, msq[r, :], rs[r, :], tmp[r, :], lambda: dve.sem_inc(y_ask, 1),
                           lambda: dve.wait_ge(y_root, n + 1))
                if tile is not None:
                    dve.wait_ge(y_out, n * 16)
                nc.vector.scalar_tensor_tensor(out=y[r, :], in0=ps_y[r, :], scalar=rs[r, 0:1],
                                               in1=g2[1 if tile is None else 0][r, :], op0=ALU.mult,
                                               op1=ALU.mult).then_inc(y_free, 1)
                dve.wait_ge(y_free, n + 1)
                dve.wait_ge(x1_in, n * 16 + 16)
                nc.vector.tensor_tensor(y[r, :], y[r, :], x1[r, :], ALU.add).then_inc(y_done, 1)
                if nxt:
                    assert own.n == per, (own.n, per)

            run(dve, start, body)

        @block.tensor
        def _(pe):
            pe.wait_ge(S["w_q_full"], 16 * (KC + 1))

            def transposes(n, rows):
                pe.wait_ge(h2_in, n * 16 + 16)
                for half in range(2):
                    if half or not (isinstance(n, int) and n == 0):
                        pe.wait_ge(h2T_done, n * 2 + half)
                    for q in range(4):
                        k = 4 * half + q
                        last = nc.tensor.transpose(ps_t[:, q * P:q * P + rows], h2n[0:rows, k * P:(k + 1) * P],
                                                   ident[0:rows, 0:rows])
                    last.then_inc(h2_tr, 1)
                pe.wait_ge(h2T_done, n * 2 + 2)

            def queries(n, h, rows):
                if not (isinstance(n, int) and n == 0 and h == 0):
                    pe.wait_ge(q_ready, n * PH + h)
                for side in range(2):
                    c = 2 * h + side
                    for k in range(KC):
                        last = nc.tensor.matmul(ps_q[:, side * P:side * P + rows], w_q[:, k, c * P:(c + 1) * P],
                                                h2T[:, k, 0:rows], start=(k == 0), stop=(k == KC - 1),
                                                skip_group_check=True)
                last.then_inc(q_done, 1)

            def scores(n, h, rows):
                pe.wait_ge(q_ready, n * PH + (h + 1))
                if not (isinstance(n, int) and n == 0 and h < 2):
                    pe.wait_ge(s_read, n * PH + (h - 1))
                for side in range(2):
                    last = nc.tensor.matmul(ps_s[h % 2][0:rows, side * P:(side + 1) * P], qTs[:, side, 0:rows],
                                            keys[:, 2 * h + side, :], start=True, stop=True, skip_group_check=True)
                last.then_inc(s_done, 1)

            def add_row(n, h, k, rows):
                s = TOPK * h + k
                pe.wait_ge(v_full[s % RING], n * (16 * SLOTS // RING) + 16 * (s // RING + 1))
                pe.wait_ge(diag_ready, n * SLOTS + (s + 1))
                for half in range(2):
                    c = slice(512 * half, 512 * (half + 1))
                    last = nc.tensor.matmul(ps_y[0:rows, c], diag[s % DIAGS][0:rows, 0:rows], vrow[s % RING][0:rows, c],
                                            start=(s == 0), stop=(s == SLOTS - 1))
                last.then_inc(v_used, 1)

            def start():
                transposes(0, DEC)
                for h in range(PH):
                    queries(0, h, DEC)
                    scores(0, h, DEC)

            def body(n, rows, nxt, tile):
                for h in range(PH):
                    if nxt:
                        if h == 0:
                            transposes(n + 1, nxt)
                        queries(n + 1, h, nxt)
                    if h == 0 and tile is not None:
                        pe.wait_ge(y_free, n)
                    for k in range(TOPK):
                        add_row(n, h, k, rows)
                        if k == TOPK // 2 - 1 and nxt:
                            scores(n + 1, h, nxt)

            run(pe, start, body)


def constants():
    import numpy as np

    c = np.zeros((P, C_END), np.float32)
    i = np.arange(P)
    c[:, C_ID:C_ID + P] = np.eye(P)
    c[:, C_NTRI:C_NTRI + P] = -(i[:, None] >= i[None, :]).astype(np.float32)
    c[:, C_NONES:C_NONES + P] = -1.0
    c[:, C_MASK:C_MASK + P] = i[:, None] < i[None, :]
    c[:, C_IOTA:C_IOTA + TOPK] = np.arange(TOPK)
    for g, w in enumerate(WINDOWS):
        c[:, C_INVC + 16 * g:C_INVC + 16 * (g + 1)] = 1.0 / np.minimum(np.arange(16) + 1, w)
    return c


_OUTS = [("y_p", (SEQ, D)), ("y_s", (DEC, D)), ("k_p", (SEQ, DA)), ("v_p", (SEQ, DA)), ("pool_p", (HIST, DPOOL)),
         ("k_s", (DEC, DA)), ("v_s", (DEC, DA)), ("pool_s", (HIST, DPOOL))]


def kernel(x_prompt, x_sample, cache_k, cache_v, state_pool, c_prompt, c_sample, w_ada, b_ada, g_pre1, g_post1,
           g_pre2, g_post2, w_in, g_out_a, g_out_b, w_pool, pool_scale, w_out, w_query, sub_keys, u_experts, v_experts):
    import numpy as np
    import concourse.bacc as bacc
    from concourse.bass_utils import run_bass_kernel_spmd

    a = lambda v: np.ascontiguousarray(np.asarray(v))
    col = lambda v: np.asarray(v).reshape(-1, P).T
    ins = {
        "x_p": a(x_prompt)[0], "x_s": a(x_sample)[0],
        "cT": a(np.stack([np.asarray(c_prompt)[0], np.asarray(c_sample)[0]]).reshape(2, KC, P).transpose(2, 1, 0)
                .reshape(P, 2 * KC)),
        "w_ada": a(w_ada)[0], "b_ada": a(b_ada),
        "gains": a(np.concatenate([col(g_pre1), col(g_out_a), col(g_out_b), col(pool_scale)], axis=1)),
        "rows": a(np.concatenate([np.asarray(g_post1), np.asarray(g_pre2), np.asarray(g_post2)])),
        "w_in": a(w_in)[0], "w_pool": a(w_pool)[0], "w_out": a(w_out)[0], "w_query": a(w_query)[0],
        "keysT": a(np.asarray(sub_keys)[0].transpose(3, 1, 0, 2).reshape(P, 2 * PH, NKEY)),
        "kpastT": a(np.asarray(cache_k)[0, 0].reshape(PAST, DA).T), "vpast": a(cache_v)[0, 0].reshape(PAST, DA),
        "histT": a(np.asarray(state_pool)[0, 0].reshape(HIST, FA, P).transpose(2, 1, 0)),
        "u_tab": a(u_experts)[0], "v_tab": a(v_experts)[0],
        "const": constants(),
    }
    nc = bacc.Bacc("TRN2", target_bir_lowering=False, num_devices=1)
    A, arrays = {}, {}
    for name, v in ins.items():
        arrays[f"in_{name}"] = np.ascontiguousarray(v)
        A[name] = nc.dram_tensor(f"in_{name}", v.shape, mybir.dt.from_np(v.dtype), kind="ExternalInput").ap()
    for name, shape in _OUTS:
        A[name] = nc.dram_tensor(f"out_{name}", shape, F32, kind="ExternalOutput").ap()
    build(nc, A)
    r = run_bass_kernel_spmd(nc, [arrays], core_ids=[0]).results[0]
    y_p, y_s, k_p, v_p, pool_p, k_s, v_s, pool_s = (r[f"out_{name}"] for name, _ in _OUTS)
    kv = lambda t, n: t.reshape(1, 1, n, DA // HD, HD)
    return (y_p[None], y_s[None], kv(k_p, SEQ), kv(v_p, SEQ), pool_p[None, None], kv(k_s, DEC), kv(v_s, DEC),
            pool_s[None, None])
```

```python
from contextlib import ExitStack

import concourse.bass as bass
from concourse import mybir

ALU = mybir.AluOpType
ACT = mybir.ActivationFunctionType
F32 = mybir.dt.float32
U32 = mybir.dt.uint32
AX_X = mybir.AxisListType.X

P = 128
D = 1024
SEQ = 1024
DEC = 64
PAST = 256
HD = 64
DA = 512
DPOOL = 512
NMOD = 6
EPS = 1e-6
KC = D // P
FA = DA // P
WINDOWS = (2, 4, 8, 16)
HIST = 15
PAD = 16
TOK = SEQ + DEC
NT = SEQ // P
NEXP = 128 * 128
PH = 8
TOPK = 16
NKEY = 128
SLOTS = PH * TOPK
RING = 8
DIAGS = 4
LOWEST = -3.0e38
LOG_EXP = "natural_log_exp_and_others"

C_ID, C_NTRI, C_NONES, C_MASK, C_IOTA, C_INVC = 0, 128, 256, 384, 512, 528
C_FOLD = 528 + 64
C_EPS = C_FOLD + 64
C_END = C_EPS + 1
G_PRE1, G_OUT, G_POOL = 0, 8, 16
G_END = 20

RANGES = [(0, 512), (512, 512), (SEQ, DEC)]
TILES = [(P * t, P) for t in range(NT)] + [(SEQ, DEC)]


class Chain:

    def __init__(self, eng, sem):
        self.eng, self.sem, self.base, self.n = eng, sem, 0, 0

    def add(self, ins):
        ins.then_inc(self.sem, 1)
        self.n += 1

    def wait(self):
        self.eng.wait_ge(self.sem, self.base + self.n)

    def link(self, ins):
        self.add(ins)
        self.wait()

    def link_apart(self, ins, passed):
        self.add(ins)
        self.pass_apart(passed)

    def pass_apart(self, passed):
        self.wait()
        if not isinstance(self.base, int):
            self.eng.sem_inc(passed, 1)


def build(nc, A):
    with ExitStack() as outer:
        def sem(name):
            return outer.enter_context(nc.semaphore(name))

        def dram(name, shape):
            return nc.dram_tensor(name, shape, F32).ap()

        def sbuf(stack, name, shape, dt=F32):
            return stack.enter_context(nc.sbuf_tensor(name, shape, dt))

        S = {
            "sem": sem,
            "mod_d": dram("mod_d", [2, NMOD * D]),
            "qT_d": dram("qT_d", [DA, TOK]),
            "kT_d": dram("kT_d", [DA, TOK]),
            "x1_d": dram("x1_d", [TOK, D]),
            "h2_d": dram("h2_d", [TOK, D]),
            "const": sbuf(outer, "const", [P, C_END]),
            "gains": sbuf(outer, "gains", [P, G_END]),
        }
        late = outer.enter_context(ExitStack())
        with ExitStack() as right:
            with ExitStack() as early:
                S["w_in"] = sbuf(early, "w_in_sb", [P, KC, 4 * DA])
                S["hT"] = sbuf(early, "hT", [P, KC, TOK])
                S["acol"] = sbuf(early, "acol", [P, 2, KC])
                S["bcol"] = sbuf(early, "bcol", [P, 2, KC])
                S["w_in_full"] = sem("w_in_full")
                modulation(nc, A, S)
                S["oT"] = right.enter_context(nc.sbuf_tensor("oT", [P, KC, TOK], F32, side="right"))
                projection(nc, A, S)
            S["aux"] = sbuf(late, "aux", [P, 3 * D])
            S["w_out"] = right.enter_context(nc.sbuf_tensor("w_out_sb", [P, KC, D], F32, side="right"))
            for m, name in enumerate(("g1", "a2", "b2")):
                S[name] = [right.enter_context(nc.sbuf_tensor(name, [P, D], F32, side="right")),
                           S["aux"][:, m * D:(m + 1) * D]]
            S["w_out_full"], S["prepared"] = sem("w_out_full"), sem("prepared")
            with ExitStack() as gains_only:
                for name in ("gpost", "gpre"):
                    S[name] = gains_only.enter_context(nc.sbuf_tensor(name, [P, D], F32, side="right"))
                attention(nc, A, S)
            S["w_q"] = sbuf(late, "w_q_sb", [P, KC, 2 * D])
            S["keys"] = sbuf(late, "keys_sb", [P, 2 * PH, NKEY])
            S["w_q_full"] = sem("w_q_full")
            S["find"] = Find(nc, S, late)
            output(nc, A, S)
        experts(nc, A, S)


def modulation(nc, A, S):
    sem = S["sem"]
    hT, acol, bcol, gains = S["hT"], S["acol"], S["bcol"], S["gains"]
    ident, eps = S["const"][:, C_ID:C_ID + P], S["const"][:, C_EPS:C_EPS + 1]
    CH = 512
    NCH = NMOD * D // CH
    ADA = 4
    FIRST = 2 * D // CH
    NTILE = len(TILES)
    with ExitStack() as st:
        sb = lambda n, s, d=F32: st.enter_context(nc.sbuf_tensor(n, s, d))
        ada = [sb(f"ada{i}", [P, KC, CH]) for i in range(ADA)]
        c_sb = sb("c_sb", [P, KC * 2])
        ec = sb("ec", [P, KC * 2])
        silu = sb("silu", [P, KC * 2])
        mod = sb("mod", [2, NMOD * D])
        x = [sb(f"x{i}", [P, D]) for i in range(2)]
        xn = [sb(f"xn{i}", [P, D]) for i in range(2)]
        scol = sb("scol", [P, 2, KC])
        msq = sb("msq1", [P, NTILE])
        rs = sb("rs1", [P, NTILE])
        tmp = sb("tmp1", [P, NTILE])
        psum = [st.enter_context(nc.psum_tensor(f"ps_mod{i}", [P, CH], F32)) for i in range(2)]
        ps_t = [st.enter_context(nc.psum_tensor(f"ps_t{i}", [P, 512], F32)) for i in range(4)]
        ada_full = [sem(f"ada_full{i}") for i in range(ADA)]
        c_in, b_in, gains_in, const_in, c_exp, c_silu = (
            sem(x) for x in ("c_in", "b_in", "gains_in", "const_in", "c_exp", "c_silu"))
        mm_done, mod_done, mod1_out, mod_out, col_in = (
            sem(x) for x in ("mod_mm", "mod_done", "mod1_out", "mod_out", "col_in"))
        x_full = [sem(f"x_full{i}") for i in range(2)]
        y0_done, xn_done = sem("y0_done1"), sem("xn_done")
        act_own, dve_own = sem("act_own0"), sem("dve_own0")
        tr_done, hT_done = sem("tr_done1"), sem("hT_done")
        block = st.enter_context(nc.Block())

        @block.sync
        def _(sp):
            sp.dma_start(c_sb[:, :], A["cT"][:, :]).then_inc(c_in, 16)
            sp.dma_start(mod[:, :], A["b_ada"].broadcast_to([2, NMOD * D])).then_inc(b_in, 16)
            ada_v = A["w_ada"].rearrange("(k p) n -> p k n", p=P)
            with sp.Fori(0, NCH // ADA) as i:
                for j in range(ADA):
                    sp.wait_ge(mod_done, i * ADA + (j + 1))
                    sp.dma_start(ada[j][:, :, :], ada_v[:, :, bass.ds(i * (ADA * CH) + j * CH, CH)])\
                        .then_inc(ada_full[j], 16)
            w_v = A["w_in"].rearrange("(k p) n -> p k n", p=P)
            for k in range(KC):
                sp.dma_start(S["w_in"][:, k, :], w_v[:, k, :]).then_inc(S["w_in_full"], 16)
            sp.wait_ge(mod_done, NCH + ADA)
            sp.dma_start(S["mod_d"][:, 2 * D:], mod[:, 2 * D:]).then_inc(mod_out, 16)
            sp.wait_ge(mod_out, 16)

        @block.gpsimd
        def _(pool):
            pool.wait_ge(mod_done, FIRST + ADA)
            pool.dma_start(S["mod_d"][:, 0:2 * D], mod[:, 0:2 * D]).then_inc(mod1_out, 16)
            pool.wait_ge(mod1_out, 16)
            for s in range(2):
                for m, dst in enumerate((bcol, scol)):
                    pool.dma_start(dst[:, s, :], S["mod_d"][s, m * D:(m + 1) * D].rearrange("(k p) -> p k", p=P),
                                   allow_slow_non_contiguous=True).then_inc(col_in, 16)

        @block.scalar
        def _(act):
            own = Chain(act, act_own)
            act.preload_act_table_set(LOG_EXP)
            act.dma_start(S["const"][:, :], A["const"][:, :]).then_inc(const_in, 16)
            act.dma_start(S["gains"][:, :], A["gains"][:, :]).then_inc(gains_in, 16)

            def load(t):
                t0, rows = TILES[t]
                src = A["x_p"][t0:t0 + rows, :] if t < NT else A["x_s"][:, :]
                act.dma_start(x[t % 2][0:rows, :], src).then_inc(x_full[t % 2], 16)

            load(0)
            load(1)
            act.wait_ge(c_in, 16)
            nc.scalar.activation(ec[:, :], c_sb[:, :], ACT.Exp, scale=-1.0).then_inc(c_exp, 1)
            for t, (_, rows) in enumerate(TILES):
                b = t % 2
                act.wait_ge(x_full[b], 16 * (t // 2 + 1))
                if t >= 2:
                    act.wait_ge(tr_done, 2 * (t - 1))
                own.link(nc.scalar.activation(xn[b][0:rows, :], x[b][0:rows, :], ACT.Square,
                                              accum_out=msq[0:rows, t:t + 1]))
                if t == 0:
                    act.wait_ge(const_in, 16)
                own.link(nc.scalar.activation(rs[0:rows, t:t + 1], msq[0:rows, t:t + 1], ACT.Ln, scale=1.0 / D,
                                              bias=eps[0:rows, :]))
                nc.scalar.activation(rs[0:rows, t:t + 1], rs[0:rows, t:t + 1], ACT.Exp, scale=-0.5)\
                    .then_inc(y0_done, 1)
                if t + 2 < NTILE:
                    act.wait_ge(xn_done, t + 1)
                    load(t + 2)

        @block.vector
        def _(dve):
            own = Chain(dve, dve_own)
            dve.sem_inc(mod_done, ADA)
            dve.wait_ge(c_exp, 1)
            own.link(nc.vector.tensor_scalar_add(ec[:, :], ec[:, :], 1.0))
            own.link(nc.vector.reciprocal(silu[:, :], ec[:, :]))
            nc.vector.tensor_tensor(silu[:, :], silu[:, :], c_sb[:, :], ALU.mult).then_inc(c_silu, 1)

            def finish_tile(t):
                t0, rows = TILES[t]
                for half in range(2):
                    dve.wait_ge(tr_done, 2 * t + half + 1)
                    bank = ps_t[2 * (t % 2) + half]
                    nc.vector.tensor_copy(hT[:, 4 * half:4 * half + 4, t0:t0 + rows],
                                          bank[:, :].rearrange("p (k t) -> p k t", k=4)[:, :, 0:rows])\
                        .then_inc(hT_done, 1)

            def normalise(t):
                rows, col = TILES[t][1], slice(t, t + 1)
                dve.wait_ge(y0_done, t + 1)
                own.link(nc.vector.tensor_scalar(msq[0:rows, col], msq[0:rows, col], 1.0 / D, EPS, ALU.mult, ALU.add))
                newton(own, nc, msq[0:rows, col], rs[0:rows, col], tmp[0:rows, col])
                nc.vector.tensor_scalar(xn[t % 2][0:rows, :], x[t % 2][0:rows, :], rs[0:rows, col], None, ALU.mult)\
                    .then_inc(xn_done, 1)

            normalise(0)
            dve.wait_ge(b_in, 16)
            for c in range(NCH):
                if c + 1 < NTILE:
                    normalise(c + 1)
                dve.wait_ge(mm_done, c + 1)
                at = slice(c * CH, (c + 1) * CH)
                nc.vector.tensor_tensor(mod[:, at], psum[c % 2][0:2, :], mod[:, at], ALU.add).then_inc(mod_done, 1)
                if c < NTILE:
                    finish_tile(c)
            dve.wait_ge(col_in, 64)
            dve.wait_ge(gains_in, 16)
            for s in range(2):
                own.link(nc.vector.tensor_scalar_add(acol[:, s, :], scol[:, s, :], 1.0))
                own.link(nc.vector.tensor_tensor(acol[:, s, :], acol[:, s, :], gains[:, G_PRE1:G_PRE1 + KC], ALU.mult))

        @block.tensor
        def _(pe):
            def transposes(t):
                rows = TILES[t][1]
                pe.wait_ge(xn_done, t + 1)
                for half in range(2):
                    if t >= 2:
                        pe.wait_ge(hT_done, 2 * (t - 2) + half + 1)
                    for q in range(4):
                        k = 4 * half + q
                        last = nc.tensor.transpose(ps_t[2 * (t % 2) + half][:, q * P:q * P + rows],
                                                   xn[t % 2][0:rows, k * P:(k + 1) * P], ident[0:rows, 0:rows])
                    last.then_inc(tr_done, 1)

            pe.wait_ge(c_silu, 1)
            pe.wait_ge(const_in, 16)
            for c in range(NCH):
                pe.wait_ge(ada_full[c % ADA], 16 * (c // ADA + 1))
                pe.wait_ge(mod_done, ADA + c - 1)
                for k in range(KC):
                    last = nc.tensor.matmul(psum[c % 2][0:2, :], silu[:, 2 * k:2 * k + 2], ada[c % ADA][:, k, :],
                                            start=(k == 0), stop=(k == KC - 1))
                last.then_inc(mm_done, 1)
                if c < NTILE:
                    transposes(c)


def newton(own, nc, mean_sq, y, t):
    own.add(nc.vector.scalar_tensor_tensor(out=t, in0=y, scalar=mean_sq, in1=y, op0=ALU.mult, op1=ALU.mult))
    own.wait()
    own.link(nc.vector.tensor_scalar(t, t, -0.5, 1.5, ALU.mult, ALU.add))
    own.link(nc.vector.tensor_tensor(y, y, t, ALU.mult))


def projection(nc, A, S):
    sem = S["sem"]
    const, gains, w_in, oT = S["const"], S["gains"], S["w_in"], S["oT"]
    hT, acol, bcol = S["hT"], S["acol"], S["bcol"]
    ident = const[:, C_ID:C_ID + P]
    NTILE = len(TILES)
    jobs = [(kind, f, r) for kind in "kqp" for f in range(FA) for r in range(len(RANGES))]
    jobs += [("v", t, None) for t in range(NTILE)]
    NB = 3
    with ExitStack() as st:
        sb = lambda n, s, d=F32: st.enter_context(nc.sbuf_tensor(n, s, d))
        ps = lambda n: st.enter_context(nc.psum_tensor(n, [P, 512], F32))
        stage = [sb(f"stage{i}", [P, 512]) for i in range(NB)]
        krow = [sb(f"krow{i}", [P, 4, P]) for i in range(2)]
        pT = sb("pT", [P, FA, PAD + SEQ])
        pTs = sb("pTs", [P, FA, PAD + DEC])
        sums = [sb(f"sums{i}", [P, PAD + SEQ]) for i in range(2)]
        w_pool = sb("w_pool_sb", [P, FA, P])
        prow = [sb(f"prow{i}", [HIST, DPOOL]) for i in range(2)]
        ps_t = [ps(f"ps_p{i}") for i in range(2)]
        ps_z = [ps(f"ps_z{i}") for i in range(NB)]
        ps_k = [ps(f"ps_k{i}") for i in range(2)]
        pool_in, dve_own, h_done = sem("pool_in"), sem("dve_own1"), sem("h_done")
        z_done, z_read = sem("z_done"), sem("z_read")
        stage_out = [sem(f"stage_out{i}") for i in range(NB)]
        k_tr, k_read, krow_out = sem("k_tr"), sem("k_read"), [sem(f"krow_out{i}") for i in range(2)]
        hist_clear = sem("hist_clear")
        pooled_done, mix_done, mix_read = sem("pooled_done"), sem("mix_done"), sem("mix_read")
        p_tr, p_read, prow_out = sem("p_tr"), sem("p_read"), sem("prow_out")
        block = st.enter_context(nc.Block())

        n_k = FA * len(RANGES)
        last_p = 3 * n_k
        def stores_before(j, b):
            return sum(1 for m in range(j) if m % NB == b and jobs[m][0] != "p")

        @block.sync
        def _(sp):
            for j, (kind, f, r) in enumerate(jobs):
                if kind == "p":
                    continue
                sp.wait_ge(z_read, j + 1)
                if kind == "v":
                    t0, rows = TILES[f]
                    dst = A["v_p"][t0:t0 + rows, :] if f < NT else A["v_s"][:, :]
                    src = stage[j % NB][0:rows, :]
                else:
                    c0, n = RANGES[r]
                    dst = S["qT_d" if kind == "q" else "kT_d"][f * P:(f + 1) * P, c0:c0 + n]
                    src = stage[j % NB][:, 0:n]
                sp.dma_start(dst, src).then_inc(stage_out[j % NB], 16)
                if kind == "k":
                    sp.wait_ge(k_read, j + 1)
                    if r < 2:
                        dst = A["k_p"][c0:c0 + n, f * P:(f + 1) * P].rearrange("(t p) c -> p t c", p=P)
                        sp.dma_start(dst, krow[j % 2][:, :, :]).then_inc(krow_out[j % 2], 16)
                    else:
                        sp.dma_start(A["k_s"][:, f * P:(f + 1) * P], krow[j % 2][0:DEC, 0, :])\
                            .then_inc(krow_out[j % 2], 16)
            sp.wait_ge(p_read, 2)
            sp.dma_start(A["pool_p"][:, :], prow[0][:, :]).then_inc(prow_out, 16)
            sp.dma_start(A["pool_s"][:, :], prow[1][:, :]).then_inc(prow_out, 16)
            sp.wait_ge(prow_out, 32)
            for b in range(NB):
                sp.wait_ge(stage_out[b], 16 * stores_before(len(jobs), b))
            for b in range(2):
                sp.wait_ge(krow_out[b], 16 * (n_k // 2))

        @block.scalar
        def _(act):
            act.dma_start(w_pool[:, :, :], A["w_pool"].rearrange("g c d -> c g d")).then_inc(pool_in, 16)
            act.wait_ge(hist_clear, 1)
            act.dma_start(pTs[:, :, PAD - HIST:PAD], A["histT"][:, :, :]).then_inc(pool_in, 16)
            for j, (kind, f, r) in enumerate(jobs):
                act.wait_ge(z_done, j + 1)
                z = ps_z[j % NB]
                if kind == "p":
                    c0, n = RANGES[r]
                    dst = pT[:, f, PAD + c0:PAD + c0 + n] if r < 2 else pTs[:, f, PAD:PAD + DEC]
                    nc.scalar.activation(dst, z[:, 0:n], ACT.Copy).then_inc(z_read, 1)
                    continue
                if stores_before(j, j % NB):
                    act.wait_ge(stage_out[j % NB], 16 * stores_before(j, j % NB))
                if kind == "k" and j >= NB:
                    act.wait_ge(k_tr, j - NB + 1)
                elif kind == "q":
                    act.wait_ge(k_tr, n_k)
                if kind == "v":
                    rows = TILES[f][1]
                    nc.scalar.activation(stage[j % NB][0:rows, :], z[0:rows, :], ACT.Copy).then_inc(z_read, 1)
                else:
                    n = RANGES[r][1]
                    nc.scalar.activation(stage[j % NB][:, 0:n], z[:, 0:n], ACT.Copy,
                                         scale=(HD ** -0.5 if kind == "q" else 1.0)).then_inc(z_read, 1)
            for m, (g, r) in enumerate((g, r) for g in range(FA) for r in range(len(RANGES))):
                c0, n = RANGES[r]
                act.wait_ge(mix_done, m + 1)
                nc.scalar.activation(oT[:, FA + g, c0:c0 + n], ps_k[m % 2][:, 0:n], ACT.Copy,
                                     scale=gains[:, G_POOL + g:G_POOL + g + 1]).then_inc(mix_read, 1)

        @block.vector
        def _(dve):
            own = Chain(dve, dve_own)
            for k in range(KC):
                for s, (c0, n) in enumerate(((0, SEQ), (SEQ, DEC))):
                    last = nc.vector.tensor_scalar(hT[:, k, c0:c0 + n], hT[:, k, c0:c0 + n], acol[:, s, k:k + 1],
                                                   bcol[:, s, k:k + 1], ALU.mult, ALU.add)
                last.then_inc(h_done, 1)
            nc.vector.memset(pTs[:, :, 0:PAD], 0.0).then_inc(hist_clear, 1)
            own.add(nc.vector.memset(pT[:, :, 0:PAD], 0.0))
            for j in range(n_k):
                r = jobs[j][2]
                dve.wait_ge(k_tr, j + 1)
                if j >= 2:
                    dve.wait_ge(krow_out[j % 2], 16 * (j // 2))
                if r < 2:
                    nc.vector.tensor_copy(krow[j % 2][:, :, :], ps_k[j % 2][:, :].rearrange("p (t c) -> p t c", t=4))\
                        .then_inc(k_read, 1)
                else:
                    nc.vector.tensor_copy(krow[j % 2][0:DEC, 0, :], ps_k[j % 2][0:DEC, 0:P]).then_inc(k_read, 1)
            for s in range(2):
                dve.wait_ge(p_tr, s + 1)
                nc.vector.tensor_copy(prow[s][:, :], ps_t[s][0:HIST, :]).then_inc(p_read, 1)
            dve.wait_ge(pool_in, 32)
            for g, w in enumerate(WINDOWS):
                for s, (src, n) in enumerate(((pT, SEQ), (pTs, DEC))):
                    full = PAD + n
                    at, cur = src[:, g, :], None
                    for level in range(g + 1):
                        step = 1 << level
                        lo = 2 * step - 1
                        new = sums[level % 2]
                        own.link(nc.vector.tensor_tensor(new[:, lo:full], at[:, lo:full], at[:, lo - step:full - step],
                                                         ALU.add))
                        at = new
                    src_g = src[:, g, PAD:full]
                    if s == 0:
                        inv = const[:, C_INVC + 16 * g:C_INVC + 16 * (g + 1)]
                        own.link(nc.vector.tensor_tensor(at[:, PAD:PAD + 16], at[:, PAD:PAD + 16], inv, ALU.mult))
                        own.link(nc.vector.tensor_tensor(src_g[:, 0:16], at[:, PAD:PAD + 16], src_g[:, 0:16],
                                                         ALU.subtract))
                        own.link(nc.vector.scalar_tensor_tensor(out=src_g[:, 16:n], in0=at[:, PAD + 16:full],
                                                                scalar=1.0 / w, in1=src_g[:, 16:n], op0=ALU.mult,
                                                                op1=ALU.subtract))
                    else:
                        own.link(nc.vector.scalar_tensor_tensor(out=src_g[:, :], in0=at[:, PAD:full], scalar=1.0 / w,
                                                                in1=src_g[:, :], op0=ALU.mult, op1=ALU.subtract))
                dve.sem_inc(pooled_done, 1)

        @block.tensor
        def _(pe):
            def key_rows(j):
                n = RANGES[jobs[j][2]][1]
                pe.wait_ge(z_read, j + 1)
                if j >= 2:
                    pe.wait_ge(k_read, j - 1)
                for i in range(-(-n // P)):
                    m = min(P, n - i * P)
                    last = nc.tensor.transpose(ps_k[j % 2][0:m, i * P:(i + 1) * P], stage[j % NB][:, i * P:i * P + m],
                                               ident)
                last.then_inc(k_tr, 1)

            for j, (kind, f, r) in enumerate(jobs):
                if j >= NB:
                    pe.wait_ge(z_read, j - NB + 1)
                z = ps_z[j % NB]
                for k in range(KC):
                    if j == 0:
                        pe.wait_ge(h_done, k + 1)
                        if k == 0:
                            pe.wait_ge(S["w_in_full"], 16 * KC)
                    if kind == "v":
                        t0, rows = TILES[f]
                        last = nc.tensor.matmul(z[0:rows, :], hT[:, k, t0:t0 + rows], w_in[:, k, 2 * DA:3 * DA],
                                                start=(k == 0), stop=(k == KC - 1))
                    else:
                        c0, n = RANGES[r]
                        w0 = {"q": 0, "k": DA, "p": 3 * DA}[kind] + f * P
                        last = nc.tensor.matmul(z[:, 0:n], w_in[:, k, w0:w0 + P], hT[:, k, c0:c0 + n],
                                                start=(k == 0), stop=(k == KC - 1))
                last.then_inc(z_done, 1)
                if 1 <= j <= n_k:
                    key_rows(j - 1)
                if j == last_p:
                    pe.wait_ge(z_read, last_p)
                    for s, (src, n) in enumerate(((pT, SEQ), (pTs, DEC))):
                        for g in range(FA):
                            last = nc.tensor.transpose(ps_t[s][0:HIST, g * P:(g + 1) * P],
                                                       src[:, g, PAD + n - HIST:PAD + n], ident)
                        last.then_inc(p_tr, 1)
            pe.wait_ge(pool_in, 32)
            m = 0
            for g in range(FA):
                pe.wait_ge(pooled_done, g + 1)
                for r, (c0, n) in enumerate(RANGES):
                    pe.wait_ge(mix_read, m - 1) if m >= 2 else pe.wait_ge(k_read, n_k)
                    src = pT[:, g, PAD + c0:PAD + c0 + n] if r < 2 else pTs[:, g, PAD:PAD + DEC]
                    nc.tensor.matmul(ps_k[m % 2][:, 0:n], w_pool[:, g, :], src, start=True, stop=True)\
                        .then_inc(mix_done, 1)
                    m += 1


def attention(nc, A, S):
    sem = S["sem"]
    const, oT = S["const"], S["oT"]
    ntri, nones = const[:, C_NTRI:C_NTRI + P], const[:, C_NONES:C_NONES + P]
    mask = const[:, C_MASK:C_MASK + P]
    NZ, NS, NR, AHEAD = 4, 4, 3, 2
    LEAD = 4
    units = []
    for qc in range(2):
        top = 4 * qc + 3
        for kb in range(top, -1, -1):
            c0 = max(0, kb * P - qc * 512)
            for h in range(2):
                units.append(dict(h=h, bank=qc, kb=kb, c0=c0, c1=512, first=kb == top, diag=kb >= 4 * qc,
                                  last=kb == 0, opens=kb == top and h == 0, closes=kb == 0 and h == 1))
    for kb in (2, 1, 0):
        units.append(dict(h=2, bank=2, kb=kb, c0=0, c1=P, first=kb == 2, diag=kb == 2, last=kb == 0,
                          opens=kb == 2, closes=kb == 0))
    NU = len(units)
    seen = {0: 0, 1: 0, 2: 0}
    for u in units:
        if u["first"]:
            seen[u["h"]] = 0
        u["par"] = seen[u["h"]] % NR
        seen[u["h"]] += 1
    ND = sum(u["diag"] for u in units)
    for m, u in enumerate(units):
        u["nd"] = sum(v["diag"] for v in units[:m])
    PAIRS = FA
    with ExitStack() as st:
        sb = lambda n, s, d=F32: st.enter_context(nc.sbuf_tensor(n, s, d))
        ps = lambda n: st.enter_context(nc.psum_tensor(n, [P, 512], F32))
        kT = [sb(f"kT{i}", [P, SEQ]) for i in range(2)]
        kTs = [sb(f"kTs{i}", [P, 3 * P]) for i in range(2)]
        qz = [sb(f"qz{i}", [P, 2, SEQ]) for i in range(2)]
        qzs = [sb(f"qzs{i}", [P, P]) for i in range(2)]
        vz = [sb(f"vz{i}", [P, 2, NT, P]) for i in range(2)]
        vzs = [sb(f"vzs{i}", [P, 2, 3, P]) for i in range(2)]
        lt = [sb(f"lt{i}", [P, 512]) for i in range(NS)]
        spt = [sb(f"spt{i}", [P, 512]) for i in range(NS)]
        wt = [sb(f"wt{i}", [P, 512]) for i in range(NS)]
        R = [[sb(f"R{h}{i}", [P, 512]) for i in range(NR)] for h in range(3)]
        ps_z = [ps(f"ps_s{i}") for i in range(NZ)]
        ps_o = [ps(f"ps_o{i}") for i in range(3)]
        cleared = sem("att_cleared")
        full = [sem(f"att_full{i}") for i in range(2)]
        z_done, l_done, sp_done, r_done, t_done, e_done, w_done, pv_done, o_read = (
            sem(n) for n in ("att_z", "att_l", "att_sp", "att_r", "att_t", "att_e", "att_w", "att_pv", "att_o"))
        act_own = sem("act_own2")
        dve_own = sem("dve_own2")
        NLOAD = 15
        block = st.enter_context(nc.Block())

        def seqs(i, b):
            return i * (2 * NU) + b * NU

        @block.sync
        def _(sp):
            sp.wait_ge(cleared, 1)

            def load(pair, b):
                f0 = pair * P

                def go(dst, src):
                    sp.dma_start(dst, src).then_inc(full[b], 16)

                rows = bass.ds(f0, P)
                go(kT[b][:, :], S["kT_d"][rows, 0:SEQ])
                go(kTs[b][:, 0:PAST], A["kpastT"][rows, :])
                go(kTs[b][:, PAST:PAST + DEC], S["kT_d"][rows, SEQ:TOK])
                for h in range(2):
                    hr = slice(h * HD, (h + 1) * HD)
                    hrow = bass.ds(f0 + h * HD, HD)
                    go(qz[b][hr, h, :], S["qT_d"][hrow, 0:SEQ])
                    go(qzs[b][hr, hr], S["qT_d"][hrow, SEQ:TOK])
                    for half in range(2):
                        part = slice(half * NT // 2, (half + 1) * NT // 2)
                        go(vz[b][:, h, part, hr],
                           A["v_p"][half * SEQ // 2:(half + 1) * SEQ // 2, hrow].rearrange("(t p) c -> p t c", p=P))
                    go(vzs[b][:, h, 0:2, hr], A["vpast"][:, hrow].rearrange("(t p) c -> p t c", p=P))
                    go(vzs[b][0:DEC, h, 2, hr], A["v_s"][:, hrow])

            load(0, 0)
            load(1, 1)
            w_v = A["w_out"].rearrange("(k p) n -> p k n", p=P)
            for k in range(KC):
                sp.dma_start(S["w_out"][:, k, :], w_v[:, k, :]).then_inc(S["w_out_full"], 16)
            sp.dma_start(S["gpost"][:, :], A["rows"][0:1, :].broadcast_to([P, D])).then_inc(S["w_out_full"], 16)
            sp.dma_start(S["gpre"][:, :], A["rows"][1:2, :].broadcast_to([P, D])).then_inc(S["w_out_full"], 16)
            for s in range(2):
                for dst, m in (("g1", 2), ("b2", 3), ("a2", 4)):
                    sp.dma_start(S[dst][s][:, :], S["mod_d"][s:s + 1, m * D:(m + 1) * D].broadcast_to([P, D]))\
                        .then_inc(S["w_out_full"], 16)
            for b in range(2):
                sp.wait_ge(pv_done, LEAD + (b + 1) * NU)
                load(2 + b, b)

        @block.gpsimd
        def _(pool):
            for b in range(2):
                nc.gpsimd.memset(kTs[b][:, :], 0.0)
                nc.gpsimd.memset(qz[b][:, :, :], 0.0)
                nc.gpsimd.memset(qzs[b][:, :], 0.0)
                nc.gpsimd.memset(vz[b][:, :, :, :], 0.0)
                last = nc.gpsimd.memset(vzs[b][:, :, :, :], 0.0)
            last.then_inc(cleared, 1)
            prepared = S["prepared"]
            pool.wait_ge(S["w_out_full"], 16 * (KC + 2 + 6))
            for k in range(KC):
                gain = S["gains"][:, G_OUT + k:G_OUT + k + 1]
                nc.gpsimd.tensor_scalar(S["w_out"][:, k, :], S["w_out"][:, k, :], gain, None, ALU.mult)\
                    .then_inc(prepared, 1)
            for s in range(2):
                g1, a2 = S["g1"][s], S["a2"][s]
                nc.gpsimd.tensor_tensor(g1[:, :], g1[:, :], S["gpost"][:, :], ALU.mult).then_inc(prepared, 1)
                nc.gpsimd.tensor_scalar(a2[:, :], a2[:, :], 1.0, None, ALU.add).then_inc(prepared, 1)
                pool.wait_ge(prepared, KC + 3 * s + 2)
                nc.gpsimd.tensor_tensor(a2[:, :], a2[:, :], S["gpre"][:, :], ALU.mult).then_inc(prepared, 1)

        @block.tensor
        def _(pe):
            pe.sem_inc(t_done, LEAD)
            pe.sem_inc(pv_done, LEAD)
            with pe.Fori(0, PAIRS // 2) as i:
                for b in range(2):
                    n0 = seqs(i, b)
                    pe.wait_ge(full[b], i * (16 * NLOAD) + 16 * NLOAD)

                    def score(m):
                        u = units[m]
                        pe.wait_ge(e_done, n0 + (LEAD + m - NZ + 1))
                        z = ps_z[m % NZ]
                        if u["h"] == 2:
                            lhsT, rhs = kTs[b][:, u["kb"] * P:(u["kb"] + 1) * P], qzs[b][:, :]
                        else:
                            q0 = u["bank"] * 512 + u["c0"]
                            lhsT = kT[b][:, u["kb"] * P:(u["kb"] + 1) * P]
                            rhs = qz[b][:, u["h"], q0:(u["bank"] + 1) * 512]
                        nc.tensor.matmul(z[:, u["c0"]:u["c1"]], lhsT, rhs, start=True, stop=True,
                                         skip_group_check=True).then_inc(z_done, 1)

                    def after(m):
                        u = units[m]
                        z, c0, c1 = ps_z[m % NZ], u["c0"], u["c1"]
                        pe.wait_ge(sp_done, n0 + (LEAD + m + 1))
                        last = nc.tensor.matmul(z[:, c0:c1], ntri, spt[m % NS][:, c0:c1], start=False, stop=True,
                                                skip_group_check=True)
                        if not u["first"]:
                            lo = c0 + P if u["diag"] and u["h"] < 2 else c0
                            last = nc.tensor.matmul(z[:, lo:c1], nones, R[u["h"]][(u["par"] - 1) % NR][:, lo:c1],
                                                    start=False, stop=True, skip_group_check=True)
                        last.then_inc(t_done, 1)

                    def values(m):
                        u = units[m]
                        pe.wait_ge(e_done, n0 + (LEAD + m + 1))
                        if u["diag"]:
                            pe.wait_ge(w_done, i * (2 * ND) + (b * ND + u["nd"] + 1))
                        if u["opens"]:
                            pe.wait_ge(o_read, i * 6 + (3 * b + u["bank"] + 1))
                        o, c0, c1, w = ps_o[u["bank"]], u["c0"], u["c1"], wt[m % NS]
                        if u["h"] == 2:
                            for h in range(2):
                                last = nc.tensor.matmul(o[:, 0:DEC], vzs[b][:, h, u["kb"], :],
                                                        w[:, h * DEC:(h + 1) * DEC], start=u["opens"] and h == 0,
                                                        stop=u["closes"] and h == 1, skip_group_check=True)
                        else:
                            last = nc.tensor.matmul(o[:, c0:c1], vz[b][:, u["h"], u["kb"], :], w[:, c0:c1],
                                                    start=u["opens"], stop=u["closes"], skip_group_check=True)
                        last.then_inc(pv_done, 1)

                    for m in range(AHEAD):
                        score(m)
                    for m in range(NU):
                        if m + AHEAD < NU:
                            score(m + AHEAD)
                        after(m)
                        if m >= AHEAD:
                            values(m - AHEAD)
                    for m in range(NU - AHEAD, NU):
                        values(m)

        @block.scalar
        def _(act):
            own = Chain(act, act_own)
            PER = 2 * 2 * NU
            act.preload_act_table_set(LOG_EXP)
            act.sem_inc(e_done, LEAD)
            with act.Fori(0, PAIRS // 2) as i:
                own.base, own.n = i * PER, 0
                for b in range(2):
                    n0 = seqs(i, b)

                    def logs(m):
                        u = units[m]
                        c = slice(u["c0"], u["c1"])
                        act.wait_ge(z_done, n0 + (m + 1))
                        act.wait_ge(sp_done, n0 + (LEAD + m - NS + 1))
                        own.link(nc.scalar.activation(lt[m % NS][:, c], ps_z[m % NZ][:, c], ACT.Abs))
                        own.link(nc.scalar.activation(lt[m % NS][:, c], lt[m % NS][:, c], ACT.Exp, scale=-1.0))
                        nc.scalar.activation(lt[m % NS][:, c], lt[m % NS][:, c], ACT.Ln, bias=1.0).then_inc(l_done, 1)

                    def weights(m):
                        u = units[m]
                        c = slice(u["c0"], u["c1"])
                        act.wait_ge(t_done, n0 + (LEAD + m + 1))
                        act.wait_ge(pv_done, n0 + (LEAD + m - NS + 1))
                        nc.scalar.activation(wt[m % NS][:, c], ps_z[m % NZ][:, c], ACT.Exp).then_inc(e_done, 1)

                    for m in range(AHEAD):
                        logs(m)
                    for m in range(NU):
                        if m + AHEAD < NU:
                            logs(m + AHEAD)
                        weights(m)
                assert own.n == PER

        @block.vector
        def _(dve):
            own = Chain(dve, dve_own)
            dve.sem_inc(o_read, 3)
            dve.sem_inc(sp_done, LEAD)
            PER = 2 * sum(1 + u["diag"] for u in units)
            with dve.Fori(0, PAIRS // 2) as i:
                own.base, own.n = i * PER, 0
                for b in range(2):
                    n0 = seqs(i, b)

                    def masked(tile, u):
                        if u["h"] == 2:
                            at = tile[:, 0:P].rearrange("p (h q) -> p h q", h=2)
                            by = mask[:, None, 0:DEC].broadcast_to([P, 2, DEC])
                        else:
                            at, by = tile[:, u["c0"]:u["c0"] + P], mask
                        return nc.vector.tensor_tensor(at, at, by, ALU.mult)

                    def softplus(m):
                        u = units[m]
                        c = slice(u["c0"], u["c1"])
                        dve.wait_ge(l_done, n0 + (m + 1))
                        dve.wait_ge(t_done, n0 + (LEAD + m - NS + 1))
                        op = nc.vector.scalar_tensor_tensor(out=spt[m % NS][:, c], in0=ps_z[m % NZ][:, c], scalar=0.0,
                                                            in1=lt[m % NS][:, c], op0=ALU.max, op1=ALU.add)
                        own.link(op)
                        if u["diag"]:
                            own.link(masked(spt[m % NS], u))
                        if u["h"] == 2 and not u["last"]:
                            dve.wait_ge(t_done, n0 + (LEAD + m - 1))
                        if not u["last"]:
                            new, old = R[u["h"]][u["par"]], R[u["h"]][(u["par"] - 1) % NR]
                            lo = u["c0"] + P if u["diag"] and u["h"] < 2 else u["c0"]
                            if u["first"]:
                                nc.vector.tensor_copy(new[:, c], spt[m % NS][:, c]).then_inc(r_done, 1)
                            else:
                                if lo > u["c0"]:
                                    nc.vector.tensor_copy(new[:, u["c0"]:lo], spt[m % NS][:, u["c0"]:lo])
                                nc.vector.tensor_tensor(new[:, lo:u["c1"]], old[:, lo:u["c1"]],
                                                        spt[m % NS][:, lo:u["c1"]], ALU.add).then_inc(r_done, 1)
                        else:
                            dve.sem_inc(r_done, 1)
                        dve.wait_ge(r_done, n0 + (m + 1))
                        dve.sem_inc(sp_done, 1)

                    def finish(m):
                        u = units[m]
                        if not u["diag"]:
                            return
                        dve.wait_ge(e_done, n0 + (LEAD + m + 1))
                        masked(wt[m % NS], u).then_inc(w_done, 1)

                    def read(m):
                        u = units[m]
                        if u["closes"]:
                            dve.wait_ge(pv_done, n0 + (LEAD + m + 1))
                            c0, n = RANGES[u["bank"]]
                            nc.vector.tensor_copy(oT[:, bass.ds(i * 2 + b, 1), c0:c0 + n],
                                                  ps_o[u["bank"]][:, None, 0:n]).then_inc(o_read, 1)

                    for m in range(AHEAD):
                        softplus(m)
                    for m in range(NU):
                        if m + AHEAD < NU:
                            softplus(m + AHEAD)
                        finish(m)
                        if m >= 4:
                            read(m - 4)
                    for m in range(NU - 4, NU):
                        read(m)
                assert own.n == PER, (own.n, PER)


def is_sample(n):
    return isinstance(n, int) and n == 0


def width(n):
    return TOPK // 2 if is_sample(n) else TOPK


def slots(n, h):
    if is_sample(n):
        return width(0) * h
    return n * SLOTS + (TOPK * h - SLOTS // 2 if h >= 0 else -SLOTS // 2 - width(n - 1))


def known(n, h):
    return 2 * (h + 1) if is_sample(n) else n * PH + (PH + h + 1)


class Find:

    PASS = 28

    def __init__(self, nc, S, stack):
        sb = lambda n, s, d=F32: stack.enter_context(nc.sbuf_tensor(n, s, d))
        aux, const = S["aux"], S["const"]
        view = lambda c0, c1, **kw: aux[:, c0:c1].rearrange("p (a b) -> p a b", **kw)
        self.nc, self.w_q, self.keys = nc, S["w_q"], S["keys"]
        self.iota = const[:, C_IOTA:C_IOTA + TOPK]
        self.h2T = view(0, D, a=KC)
        self.onehot = view(D, D + 512, a=2 * TOPK)
        self.cand = view(D + 512, D + 768, a=TOPK)
        self.crep = view(D + 768, 2 * D, a=TOPK)
        self.srep = view(2 * D, 2 * D + 256, a=2)
        self.qTs = view(2 * D + 256, 2 * D + 512, a=2)
        self.v16 = sb("v16", [P, 2, TOPK])
        self.i16 = sb("i16", [P, 2, TOPK], U32)
        self.i16f = sb("i16f", [P, 2, TOPK])
        self.best = sb("best", [P, TOPK])
        self.sel = sb("sel", [P, TOPK], U32)
        self.selij = sb("selij", [P, 2, TOPK], U32)
        self.selijf = sb("selijf", [P, 2, TOPK])
        self.picked = sb("picked", [P, 2, TOPK])
        self.idxf = sb("idxf", [P, TOPK])
        self.gexp = sb("gexp", [P, TOPK])
        self.gsum = sb("gsum", [P, 1])
        self.idx = sb("idx", [P, SLOTS], U32)
        self.gate = sb("gate", [P, SLOTS])
        self.idx0 = sb("idx0", [P, SLOTS // 2], U32)
        self.gate0 = sb("gate0", [P, SLOTS // 2])
        sem = S["sem"]
        (self.h2_tr, self.h2T_done, self.q_done, self.q_ready, self.s_done, self.s_read, self.gate_ask,
         self.gate_exp, self.idx_ready, self.v_used) = (
             sem(n) for n in ("h2_tr", "h2T_done", "q_done", "q_ready", "s_done", "s_read", "gate_ask", "gate_exp",
                              "idx_ready", "v_used"))

    def banks(self, ps_t, ps_q, ps_s):
        self.ps_t, self.ps_q, self.ps_s = ps_t, ps_q, ps_s

    def queries(self, pe, n, h):
        nc = self.nc
        if not (is_sample(n) and h == 0):
            pe.wait_ge(self.q_ready, n * PH + h)
        for side in range(2):
            c = 2 * h + side
            for k in range(KC):
                last = nc.tensor.matmul(self.ps_q[:, side * P:(side + 1) * P], self.w_q[:, k, c * P:(c + 1) * P],
                                        self.h2T[:, k, :], start=(k == 0), stop=(k == KC - 1), skip_group_check=True)
        last.then_inc(self.q_done, 1)

    def scores(self, pe, n, h):
        nc = self.nc
        pe.wait_ge(self.q_ready, n * PH + (h + 1))
        if not (is_sample(n) and h < 2):
            pe.wait_ge(self.s_read, n * PH + (h - 1))
        for side in range(2):
            last = nc.tensor.matmul(self.ps_s[h % 2][:, side * P:(side + 1) * P], self.qTs[:, side, :],
                                    self.keys[:, 2 * h + side, :], start=True, stop=True, skip_group_check=True)
        last.then_inc(self.s_done, 1)

    def take_q(self, act, n, h):
        nc = self.nc
        act.wait_ge(self.q_done, n * PH + (h + 1))
        if not (is_sample(n) and h == 0):
            act.wait_ge(self.s_done, n * PH + h)
        nc.scalar.activation(self.qTs[:, :, :], self.ps_q[:, 0:2 * P].rearrange("p (k t) -> p k t", k=2), ACT.Copy)\
            .then_inc(self.q_ready, 1)

    def exp_gate(self, act, n, h):
        act.wait_ge(self.gate_ask, n * PH + (h + 1))
        self.nc.scalar.activation(self.gexp[:, :], self.gexp[:, :], ACT.Exp).then_inc(self.gate_exp, 1)

    def top16(self, own, passed, chains):
        nc = self.nc

        def step(ops):
            for op in ops[:-1]:
                own.add(op())
            own.link_apart(ops[-1](), passed)

        step([lambda v=v, src=src: nc.vector.max(v[:, 0:8], src) for v, src, _, _ in chains])
        for v, src, rep, index in chains:
            own.add(nc.vector.max_index(index[:, 0:8], v[:, 0:8], src))
            own.add(nc.vector.match_replace(rep, v[:, 0:8], src, LOWEST))
        own.pass_apart(passed)
        step([lambda v=v, rep=rep: nc.vector.max(v[:, 8:16], rep) for v, _, rep, _ in chains])
        step([lambda v=v, rep=rep, index=index: nc.vector.max_index(index[:, 8:16], v[:, 8:16], rep)
              for v, _, rep, index in chains])

    def search(self, own, dve, passed, n, h):
        nc = self.nc
        s = self.ps_s[h % 2]
        dve.wait_ge(self.s_done, n * PH + (h + 1))
        dve.sem_inc(passed, 1)
        self.top16(own, passed, [(self.v16[:, side, :], s[:, side * P:(side + 1) * P], self.srep[:, side, :],
                                  self.i16[:, side, :]) for side in range(2)])
        dve.sem_inc(self.s_read, 1)
        own.add(nc.vector.tensor_copy(self.i16f[:, :, :], self.i16[:, :, :]))
        own.link_apart(nc.vector.tensor_tensor(self.cand[:, :, :], self.v16[:, 0, :, None].broadcast_to([P, TOPK, TOPK]),
                                               self.v16[:, 1, None, :].broadcast_to([P, TOPK, TOPK]), ALU.add),
                       passed)
        flat = self.cand[:, :, :].rearrange("p a b -> p (a b)")
        self.top16(own, passed, [(self.best[:, :], flat, self.crep[:, :, :].rearrange("p a b -> p (a b)"),
                                  self.sel[:, :])])
        nc.vector.tensor_scalar(self.gexp[:, :], self.best[:, :], self.best[:, 0:1], None, ALU.subtract)\
            .then_inc(self.gate_ask, 1)
        own.add(nc.vector.tensor_scalar(self.selij[:, 0, :], self.sel[:, :], 4, None, ALU.logical_shift_right))
        own.link(nc.vector.tensor_scalar(self.selij[:, 1, :], self.sel[:, :], TOPK - 1, None, ALU.bitwise_and))
        own.link(nc.vector.tensor_copy(self.selijf[:, :, :], self.selij[:, :, :]))
        own.link(nc.vector.tensor_tensor(
            self.onehot[:, :, :], self.selijf[:, :, :].rearrange("p s k -> p (s k)")[:, :, None]
            .broadcast_to([P, 2 * TOPK, TOPK]),
            self.iota[:, None, :].broadcast_to([P, 2 * TOPK, TOPK]), ALU.is_equal))
        for side in range(2):
            at = self.onehot[:, side * TOPK:(side + 1) * TOPK, :]
            own.add(nc.vector.tensor_tensor(at, at, self.i16f[:, side, None, :].broadcast_to([P, TOPK, TOPK]),
                                            ALU.mult))
        own.wait()
        own.link(nc.vector.tensor_reduce(self.picked[:, :, :].rearrange("p s k -> p (s k)"), self.onehot[:, :, :],
                                         AX_X, ALU.add))
        own.link(nc.vector.scalar_tensor_tensor(out=self.idxf[:, :], in0=self.picked[:, 0, :], scalar=float(NKEY),
                                                in1=self.picked[:, 1, :], op0=ALU.mult, op1=ALU.add))
        if is_sample(n):
            for half in range(2):
                p, c = slice(DEC * half, DEC * (half + 1)), slice(width(0) * h, width(0) * (h + 1))
                nc.vector.tensor_copy(self.idx0[p, c], self.idxf[p, :].rearrange("p (k s) -> p k s", s=2)[:, :, half])\
                    .then_inc(self.idx_ready, 1)
        else:
            if not isinstance(n, int) or n > 1:
                dve.wait_ge(self.v_used, slots(n - 1, 0) + TOPK * (h + 1))
            nc.vector.tensor_copy(self.idx[:, TOPK * h:TOPK * (h + 1)], self.idxf[:, :]).then_inc(self.idx_ready, 1)
        dve.wait_ge(self.gate_exp, n * PH + (h + 1))
        own.link(nc.vector.tensor_reduce(self.gsum[:, :], self.gexp[:, :], AX_X, ALU.add))
        own.link(nc.vector.reciprocal(self.gsum[:, :], self.gsum[:, :]))
        if is_sample(n):
            for half in range(2):
                p, c = slice(DEC * half, DEC * (half + 1)), slice(width(0) * h, width(0) * (h + 1))
                own.add(nc.vector.tensor_scalar(
                    self.gate0[p, c], self.gexp[p, :].rearrange("p (k s) -> p k s", s=2)[:, :, half], self.gsum[p, 0:1],
                    None, ALU.mult))
            own.wait()
        else:
            own.link(nc.vector.tensor_scalar(self.gate[:, TOPK * h:TOPK * (h + 1)], self.gexp[:, :], self.gsum[:, 0:1],
                                             None, ALU.mult))


def output(nc, A, S):
    sem = S["sem"]
    const = S["const"]
    eps, ident = const[:, C_EPS:C_EPS + 1], const[:, C_ID:C_ID + P]
    oT, w_out, g1, a2, b2, find = (S[n] for n in ("oT", "w_out", "g1", "a2", "b2", "find"))
    tiles = TILES[-1:] + TILES[:-1]
    NTILE = len(tiles)
    NX = 3
    seq = lambda t: 1 if t == 0 else 0
    heads = {2: [0], 3: [1, 2], 4: [3], 5: [4], 6: [5], 7: [6], 8: [7]}
    with ExitStack() as st:
        sb = lambda n, s, d=F32: st.enter_context(nc.sbuf_tensor(n, s, d))
        xt = [sb(f"xo{i}", [P, D]) for i in range(NX)]
        ot = [sb(f"ot{i}", [P, D]) for i in range(2)]
        junk = sb("junk3", [P, D])
        h2 = [sb(f"h2o{i}", [P, D]) for i in range(2)]
        sq = sb("sq3", [P, KC, P])
        msq = sb("msq3", [P, NTILE, 4])
        rs = sb("rs3", [P, NTILE, 4])
        tmp = sb("tmp3", [P, 2])
        ones = sb("ones3", [P, 1])
        ps_a = [st.enter_context(nc.psum_tensor(f"ps_a{i}", [P, 512], F32)) for i in range(2)]
        ps_b = [st.enter_context(nc.psum_tensor(f"ps_b{i}", [P, 512], F32)) for i in range(2)]
        ps_n = st.enter_context(nc.psum_tensor("ps_n", [P, 512], F32))
        ps_tq = st.enter_context(nc.psum_tensor("ps_tq", [P, 512], F32))
        find.banks(ps_tq, ps_tq, [st.enter_context(nc.psum_tensor(f"ps_s3{i}", [P, 512], F32)) for i in range(2)])
        x_full = [sem(f"xo_full{i}") for i in range(NX)]
        ones_set, sq_done, n_done, ab_done, part_done, ab_read = (
            sem(n) for n in ("ones_set", "sq_done3", "n_done", "ab_done", "part_done", "ab_read"))
        ab_root, ab_rs, o_root, x1_root, act_own, dve_own, dve_passed = (
            sem(n) for n in ("ab_root", "ab_rs", "o_root", "x1_root", "act_own3", "dve_own3", "dve_passed3"))
        o_scaled, x1_done, x1_scaled, h2_done = (sem(n) for n in ("o_scaled", "x1_done", "x1_scaled", "h2_done"))
        x1_out = [sem(f"x1_out{i}") for i in range(NX)]
        h2_out = [sem(f"h2_out{i}") for i in range(2)]
        block = st.enter_context(nc.Block())

        def load(eng, t):
            t0, rows = tiles[t]
            src = A["x_p"][t0:t0 + rows, :] if t else A["x_s"][:, :]
            eng.dma_start(xt[t % NX][0:rows, :], src).then_inc(x_full[t % NX], 16)

        @block.sync
        def _(sp):
            for t in range(NX):
                load(sp, t)
            w_v = A["w_query"].rearrange("(k p) n -> p k n", p=P)
            for k in range(KC):
                sp.dma_start(S["w_q"][:, k, :], w_v[:, k, :]).then_inc(S["w_q_full"], 16)
            sp.dma_start(S["keys"][:, :, :], A["keysT"][:, :, :]).then_inc(S["w_q_full"], 16)
            for t, (t0, rows) in enumerate(tiles):
                sp.wait_ge(h2_done, t + 1)
                sp.dma_start(S["x1_d"][t0:t0 + rows, :], xt[t % NX][0:rows, :]).then_inc(x1_out[t % NX], 16)
                sp.dma_start(S["h2_d"][t0:t0 + rows, :], h2[t % 2][0:rows, :]).then_inc(h2_out[t % 2], 16)
                if t + NX < NTILE:
                    sp.wait_ge(x1_out[t % NX], 16 * (t // NX + 1))
                    load(sp, t + NX)
            for b in range(NX):
                sp.wait_ge(x1_out[b], 16 * (NTILE // NX))
            sp.wait_ge(h2_out[0], 16 * 5)
            sp.wait_ge(h2_out[1], 16 * 4)

        @block.scalar
        def _(act):
            act.preload_act_table_set(LOG_EXP)
            own = Chain(act, act_own)

            def squares(t):
                t0, rows = tiles[t]
                if t:
                    act.wait_ge(n_done, t)
                nc.scalar.activation(sq[:, :, 0:rows], oT[:, :, t0:t0 + rows], ACT.Square).then_inc(sq_done, 1)

            def roots(rows, t, cols, src, n, done):
                own.link(nc.scalar.activation(rs[0:rows, t, cols], src, ACT.Ln, scale=1.0 / n, bias=eps[0:rows, :]))
                nc.scalar.activation(rs[0:rows, t, cols], rs[0:rows, t, cols], ACT.Exp, scale=-0.5).then_inc(done, 1)

            def branch_roots(t):
                rows = tiles[t][1]
                act.wait_ge(n_done, t + 1)
                roots(rows, t, slice(0, 2), ps_n[0:rows, 2 * t:2 * t + 2], DA, ab_root)

            def row_root(rows, t, col, src, done):
                cols = slice(col, col + 1)
                own.link(nc.scalar.activation(junk[0:rows, :], src, ACT.Square, accum_out=msq[0:rows, t, cols]))
                roots(rows, t, cols, msq[0:rows, t, cols], D, done)

            squares(0)
            branch_roots(0)
            squares(1)
            for t in range(NTILE + 1):
                if t < NTILE:
                    rows = tiles[t][1]
                    act.wait_ge(ab_rs, t + 1)
                    if t >= 2:
                        act.wait_ge(x1_done, t - 1)
                    for half in range(2):
                        j = 2 * t + half
                        act.wait_ge(ab_done, j + 1)
                        nc.scalar.activation(ot[t % 2][0:rows, 512 * half:512 * (half + 1)], ps_a[j % 2][0:rows, :],
                                             ACT.Copy, scale=rs[0:rows, t, 0:1]).then_inc(part_done, 1)
                    act.wait_ge(ab_read, 2 * (t + 1))
                    row_root(rows, t, 2, ot[t % 2][0:rows, :], o_root)
                late = t if t == 0 else t - 1
                if t != 1:
                    rows = tiles[late][1]
                    act.wait_ge(x1_done, late + 1)
                    row_root(rows, late, 3, xt[late % NX][0:rows, :], x1_root)
                for h in heads.get(t, [])[1:]:
                    find.take_q(act, 0, h)
                if t == 1:
                    for half in range(2):
                        act.wait_ge(find.h2_tr, half + 1)
                        nc.scalar.activation(
                            find.h2T[:, 4 * half:4 * half + 4, :].rearrange("p k (r t) -> p k r t", r=2),
                            ps_tq[:, :].rearrange("p (k t) -> p k t", k=4)[:, :, None, 0:DEC]
                            .broadcast_to([P, 4, 2, DEC]), ACT.Copy).then_inc(find.h2T_done, 1)
                if t + 1 < NTILE:
                    branch_roots(t + 1)
                for h in heads.get(t + 1, [])[:1]:
                    find.take_q(act, 0, h)
                if t + 2 < NTILE:
                    squares(t + 2)
                for h in heads.get(t, []):
                    find.exp_gate(act, 0, h)

        @block.vector
        def _(dve):
            own = Chain(dve, dve_own)
            nc.vector.memset(ones[:, :], 1.0).then_inc(ones_set, 1)

            def branch_norms(t):
                rows = tiles[t][1]
                r, y = msq[0:rows, t, 0:2], rs[0:rows, t, 0:2]
                x = tmp[0:rows, 0:2]
                dve.wait_ge(ab_root, t + 1)
                own.add(nc.vector.tensor_scalar(r, ps_n[0:rows, 2 * t:2 * t + 2], 1.0 / DA, EPS, ALU.mult, ALU.add))
                own.link(nc.vector.tensor_tensor(x, y, y, ALU.mult))
                own.link(nc.vector.tensor_tensor(x, x, r, ALU.mult))
                own.link(nc.vector.tensor_scalar(x, x, -0.5, 1.5, ALU.mult, ALU.add))
                nc.vector.tensor_tensor(y, y, x, ALU.mult).then_inc(ab_rs, 1)
                dve.wait_ge(ab_rs, t + 1)

            def norm(rows, t, col):
                cols = slice(col, col + 1)
                r = msq[0:rows, t, cols]
                own.link(nc.vector.tensor_scalar(r, r, 1.0 / D, EPS, ALU.mult, ALU.add))
                newton(own, nc, r, rs[0:rows, t, cols], tmp[0:rows, 0:1])

            def product(t):
                rows = tiles[t][1]
                for half in range(2):
                    j = 2 * t + half
                    c = slice(512 * half, 512 * (half + 1))
                    dve.wait_ge(part_done, j + 1)
                    nc.vector.scalar_tensor_tensor(out=ot[t % 2][0:rows, c], in0=ps_b[j % 2][0:rows, :],
                                                   scalar=rs[0:rows, t, 1:2], in1=ot[t % 2][0:rows, c],
                                                   op0=ALU.mult, op1=ALU.add).then_inc(ab_read, 1)

            def residual(t):
                rows = tiles[t][1]
                dve.wait_ge(o_root, t + 1)
                norm(rows, t, 2)
                o = ot[t % 2][0:rows, :]
                nc.vector.scalar_tensor_tensor(out=o, in0=o, scalar=rs[0:rows, t, 2:3],
                                               in1=g1[seq(t)][0:rows, :], op0=ALU.mult, op1=ALU.mult)\
                    .then_inc(o_scaled, 1)

            def second(t):
                rows = tiles[t][1]
                dve.wait_ge(x1_root, t + 1)
                norm(rows, t, 3)
                if t >= 2:
                    dve.wait_ge(h2_out[t % 2], 16 * (t // 2))
                    dve.wait_ge(find.h2_tr, 2)
                nc.vector.scalar_tensor_tensor(out=h2[t % 2][0:rows, :], in0=xt[t % NX][0:rows, :],
                                               scalar=rs[0:rows, t, 3:4], in1=a2[seq(t)][0:rows, :],
                                               op0=ALU.mult, op1=ALU.mult).then_inc(x1_scaled, 1)

            dve.wait_ge(S["prepared"], KC + 6)
            branch_norms(0)
            for t in range(NTILE + 1):
                if t < NTILE:
                    product(t)
                if t != 1:
                    residual(max(t - 1, 0))
                if t == 0 or t >= 3:
                    second(max(t - 2, 0))
                if t + 1 < NTILE:
                    branch_norms(t + 1)
                for h in heads.get(t, []):
                    find.search(own, dve, dve_passed, 0, h)
            second(NTILE - 1)

        @block.gpsimd
        def _(pool):
            def residual(t):
                x, rows = xt[t % NX], tiles[t][1]
                pool.wait_ge(x_full[t % NX], 16 * (t // NX + 1))
                pool.wait_ge(o_scaled, t + 1)
                nc.gpsimd.tensor_tensor(x[0:rows, :], x[0:rows, :], ot[t % 2][0:rows, :], ALU.add).then_inc(x1_done, 1)

            def second(t):
                h, rows = h2[t % 2], tiles[t][1]
                pool.wait_ge(x1_scaled, t + 1)
                nc.gpsimd.tensor_tensor(h[0:rows, :], h[0:rows, :], b2[seq(t)][0:rows, :], ALU.add).then_inc(h2_done, 1)

            for t in range(NTILE + 1):
                if t != 1:
                    residual(max(t - 1, 0))
                if t == 0 or t >= 3:
                    second(max(t - 2, 0))
            second(NTILE - 1)

        @block.tensor
        def _(pe):
            pe.wait_ge(S["prepared"], KC + 6)
            pe.wait_ge(ones_set, 1)
            for t, (t0, rows) in enumerate(tiles):
                if t == 2:
                    pe.wait_ge(h2_done, 1)
                    for half in range(2):
                        if half:
                            pe.wait_ge(find.h2T_done, 1)
                        for q in range(4):
                            k = 4 * half + q
                            last = nc.tensor.transpose(ps_tq[:, q * P:q * P + DEC], h2[0][0:DEC, k * P:(k + 1) * P],
                                                       ident[0:DEC, 0:DEC])
                        last.then_inc(find.h2_tr, 1)
                    pe.wait_ge(find.h2T_done, 2)
                    pe.wait_ge(S["w_q_full"], 16 * (KC + 1))
                for h in heads.get(t, [])[:1]:
                    find.queries(pe, 0, h)
                pe.wait_ge(sq_done, t + 1)
                if t:
                    pe.wait_ge(ab_rs, t)
                for m in range(2):
                    for f in range(FA):
                        last = nc.tensor.matmul(ps_n[0:rows, 2 * t + m:2 * t + m + 1], sq[:, FA * m + f, 0:rows],
                                                ones[:, :], start=(f == 0), stop=(f == FA - 1), skip_group_check=True)
                last.then_inc(n_done, 1)
                for half in range(2):
                    j = 2 * t + half
                    if j >= 2:
                        pe.wait_ge(ab_read, j - 1)
                    for m, bank in enumerate((ps_a[j % 2], ps_b[j % 2])):
                        for f in range(FA):
                            last = nc.tensor.matmul(bank[0:rows, :], oT[:, FA * m + f, t0:t0 + rows],
                                                    w_out[:, FA * m + f, 512 * half:512 * (half + 1)],
                                                    start=(f == 0), stop=(f == FA - 1))
                    last.then_inc(ab_done, 1)
                    if half == 0:
                        for h in heads.get(t, [])[:1]:
                            find.scores(pe, 0, h)
                for h in heads.get(t, [])[1:]:
                    find.queries(pe, 0, h)
                    find.scores(pe, 0, h)


def experts(nc, A, S):
    sem = S["sem"]
    const = S["const"]
    ident = const[:, C_ID:C_ID + P]
    fold, eps = const[:, C_FOLD:C_FOLD + DEC], const[:, C_EPS:C_EPS + 1]
    find = S["find"]
    h2T, idx, idx0, gate, gate0 = find.h2T, find.idx, find.idx0, find.gate, find.gate0
    h2_tr, h2T_done, q_done, idx_ready, v_used = find.h2_tr, find.h2T_done, find.q_done, find.idx_ready, find.v_used
    with ExitStack() as st:
        sb = lambda n, s, d=F32: st.enter_context(nc.sbuf_tensor(n, s, d))
        ps = lambda n, w=512: st.enter_context(nc.psum_tensor(n, [P, w], F32))
        urow = [sb(f"urow{i}", [P, D]) for i in range(RING)]
        vrow = [sb(f"vrow{i}", [P, D]) for i in range(RING)]
        diag = [sb(f"diag{i}", [P, P]) for i in range(DIAGS)]
        h2n = sb("h2n", [P, D])
        x1 = sb("x1e", [P, D])
        ysum = sb("ysum", [P, D])
        y = sb("ye", [P, D])
        gpost = sb("gpost4", [P, D])
        g2 = [sb(f"g2_{i}", [P, D]) for i in range(2)]
        dots = [sb(f"dots{i}", [P, TOPK]) for i in range(2)]
        gelu = [sb(f"gelu{i}", [P, TOPK]) for i in range(2)]
        wgt = [sb(f"wgt{i}", [P, TOPK]) for i in range(2)]
        msq = sb("msq4", [P, 1])
        rs = sb("rs4", [P, 1])
        tmp = sb("tmp4", [P, 1])
        ps_y = st.enter_context(nc.psum_tensor("ps_y", [P, D], F32))
        ps_h = st.enter_context(nc.psum_tensor("ps_h", [P, D], F32))
        ps_t = ps("ps_tr4")
        find.banks(ps_t, ps("ps_q"), [ps(f"ps_s4{i}") for i in range(2)])

        u_full = [sem(f"u_full{i}") for i in range(RING)]
        v_full = [sem(f"v_full{i}") for i in range(RING)]
        (u_used, h2_in, x1_in, g2_in, h2_copied, dots_done, gelu_done, w_ready, diag_ready, y_root, y_free, y_done,
         y_out) = (sem(n) for n in (
             "u_used", "h2_in", "x1_in", "g2_in", "h2_copied", "dots_done", "gelu_done", "w_ready", "diag_ready",
             "y_root", "y_free", "y_done", "y_out"))
        act_own, dve_own = sem("act_own4"), sem("dve_own4")
        pool_passed, dve_passed = sem("pool_passed"), sem("dve_passed")
        block = st.enter_context(nc.Block())

        def filled(n, h, k):
            s = width(n) * h + k
            if is_sample(n):
                return 16 * (s // RING + 1)
            return n * (16 * SLOTS // RING) + 16 * (s // RING + 1 - SLOTS // 2 // RING)

        def run(eng, start, body, end):
            start()
            body(0, True)
            body(1, True)
            with eng.Fori(0, NT - 2) as i:
                body(i + 2, True)
            body(NT, False)
            end()

        @block.sync
        def _(sp):
            def start():
                for half in range(2):
                    sp.dma_start(h2n[DEC * half:DEC * (half + 1), :], S["h2_d"][SEQ:TOK, :]).then_inc(h2_in, 16)
                for i in range(2):
                    sp.dma_start(g2[i][:, :], S["mod_d"][i:i + 1, 5 * D:6 * D].broadcast_to([P, D]))\
                        .then_inc(g2_in, 16)
                sp.dma_start(gpost[:, :], A["rows"][2:3, :].broadcast_to([P, D])).then_inc(g2_in, 16)

            def store(n):
                sp.wait_ge(y_done, n + 1)
                if is_sample(n):
                    sp.dma_start(A["y_s"][:, :], y[0:DEC, :]).then_inc(y_out, 16)
                else:
                    sp.dma_start(A["y_p"][bass.ds(n * P - P, P), :], y[:, :]).then_inc(y_out, 16)

            def body(n, more):
                if more:
                    sp.wait_ge(h2_copied, n * 2 + 2)
                    sp.wait_ge(h2_tr, n * 2 + 2)
                    sp.dma_start(h2n[:, :], S["h2_d"][bass.ds(n * P, P), :]).then_inc(h2_in, 16)
                if is_sample(n):
                    sp.dma_start(x1[0:DEC, :], S["x1_d"][SEQ:TOK, :]).then_inc(x1_in, 16)
                else:
                    store(n - 1)
                    sp.dma_start(x1[:, :], S["x1_d"][bass.ds(n * P - P, P), :]).then_inc(x1_in, 16)

            run(sp, start, body, lambda: store(NT))
            sp.wait_ge(y_out, 16 * (NT + 1))

        @block.gpsimd
        def _(pool):
            def gather(table, ring, full, n, h, k):
                col = width(n) * h + k
                places = idx0 if is_sample(n) else idx
                nc.gpsimd.indirect_dma_start(
                    ring[k % RING][:, :], None, A[table][:, :],
                    bass.IndirectOffsetOnAxis(ap=places[:, col:col + 1], axis=0)).then_inc(full[k % RING], 16)

            def start():
                pool.wait_ge(idx_ready, known(0, 0))
                for k in range(width(0)):
                    gather("u_tab", urow, u_full, 0, 0, k)

            def body(n, more):
                for h in range(PH):
                    un, uh = (n, h + 1) if h < PH - 1 else (n + 1, 0)
                    ahead = h < PH - 1 or more
                    if ahead:
                        pool.wait_ge(idx_ready, known(un, uh))
                    for k in range(TOPK):
                        if ahead and k < width(un):
                            pool.wait_ge(u_used, slots(un, uh) + (k - RING + 1))
                            pool.sem_inc(pool_passed, 1)
                            gather("u_tab", urow, u_full, un, uh, k)
                        if k < width(n):
                            if not (is_sample(n) and h == 0):
                                pool.wait_ge(v_used, slots(n, h) + (k - RING + 1))
                                pool.sem_inc(pool_passed, 1)
                            gather("v_tab", vrow, v_full, n, h, k)

            run(pool, start, body, lambda: None)

        @block.scalar
        def _(act):
            own = Chain(act, act_own)

            def take_h2T(n):
                for half in range(2):
                    act.wait_ge(h2_tr, n * 2 + (half + 1))
                    if half == 0:
                        act.wait_ge(q_done, n * PH)
                    nc.scalar.activation(h2T[:, 4 * half:4 * half + 4, :],
                                         ps_t[:, :].rearrange("p (k t) -> p k t", k=4), ACT.Copy).then_inc(h2T_done, 1)

            def copy_h2(n):
                if not is_sample(n):
                    act.wait_ge(u_used, slots(n, 0))
                act.wait_ge(h2_in, n * 16 + 32)
                for half in range(2):
                    c = slice(512 * half, 512 * (half + 1))
                    nc.scalar.activation(ps_h[:, c], h2n[:, c], ACT.Copy).then_inc(h2_copied, 1)

            def do_gelu(n, h):
                act.wait_ge(dots_done, n * PH + (h + 1))
                w = width(n)
                nc.scalar.activation(gelu[h % 2][:, 0:w], dots[h % 2][:, 0:w], ACT.Gelu).then_inc(gelu_done, 1)

            def copy_sum(n):
                rows = DEC if is_sample(n) else P
                act.wait_ge(v_used, slots(n, 0) + width(n) * PH)
                if not is_sample(n):
                    act.wait_ge(y_done, n)
                nc.scalar.activation(ysum[0:rows, :], ps_y[0:rows, :], ACT.Copy).then_inc(y_free, 1)

            def norm(n):
                rows = DEC if is_sample(n) else P
                act.preload_act_table_set(LOG_EXP)
                act.wait_ge(y_free, n + 1)
                if not is_sample(n):
                    act.wait_ge(y_out, n * 16)
                own.base, own.n = n * 2, 0
                own.link(nc.scalar.activation(y[0:rows, :], ysum[0:rows, :], ACT.Square, accum_out=msq[0:rows, :]))
                own.link(nc.scalar.activation(rs[0:rows, :], msq[0:rows, :], ACT.Ln, scale=1.0 / D,
                                              bias=eps[0:rows, :]))
                nc.scalar.activation(rs[0:rows, :], rs[0:rows, :], ACT.Exp, scale=-0.5).then_inc(y_root, 1)

            def start():
                copy_h2(0)
                do_gelu(0, 0)

            def body(n, more):
                for h in range(PH):
                    if h == 0 and more:
                        take_h2T(n + 1)
                    if h == PH - 1 and more:
                        copy_h2(n + 1)
                    act.wait_ge(w_ready, n * PH + (h + 1))
                    for k in range(width(n)):
                        s = width(n) * h + k
                        if not (is_sample(n) and s < DIAGS):
                            act.wait_ge(v_used, slots(n, h) + (k - DIAGS + 1))
                        weight = wgt[h % 2][:, k:k + 1]
                        if is_sample(n):
                            nc.scalar.activation(diag[s % DIAGS][:, 0:DEC], fold, ACT.Copy, scale=weight)\
                                .then_inc(diag_ready, 1)
                        else:
                            nc.scalar.activation(diag[s % DIAGS][:, :], ident, ACT.Copy, scale=weight)\
                                .then_inc(diag_ready, 1)
                        if k == 3 and more:
                            find.take_q(act, n + 1, h)
                        if h == 0 and k == 9:
                            norm(n - 1)
                    if h == 0:
                        if not is_sample(n):
                            find.exp_gate(act, n, PH - 1)
                    elif more:
                        find.exp_gate(act, n + 1, h - 1)
                    if h < PH - 1:
                        do_gelu(n, h + 1)
                    elif more:
                        do_gelu(n + 1, 0)
                copy_sum(n)

            run(act, start, body, lambda: norm(NT))

        @block.vector
        def _(dve):
            own = Chain(dve, dve_own)
            def products(n, h):
                if h == 0:
                    dve.wait_ge(h2_copied, n * 2 + 2)
                if not (is_sample(n) and h < 2):
                    dve.wait_ge(gelu_done, n * PH + (h - 1))
                for k in range(width(n)):
                    dve.wait_ge(u_full[k % RING], filled(n, h, k))
                    nc.vector.tensor_tensor_reduce(out=urow[k % RING][:, :], in0=urow[k % RING][:, :], in1=ps_h[:, :],
                                                   scale=1.0, scalar=0.0, op0=ALU.mult, op1=ALU.add,
                                                   accum_out=dots[h % 2][:, k:k + 1]).then_inc(u_used, 1)
                dve.wait_ge(u_used, slots(n, h) + width(n))
                dve.sem_inc(dots_done, 1)

            def weights(n, h):
                w = width(n)
                dve.wait_ge(gelu_done, n * PH + (h + 1))
                if not (is_sample(n) and h < 2):
                    dve.wait_ge(diag_ready, slots(n, h - 1))
                nc.vector.tensor_tensor(wgt[h % 2][:, 0:w], (gate0 if is_sample(n) else gate)[:, w * h:w * (h + 1)],
                                        gelu[h % 2][:, 0:w], ALU.mult).then_inc(w_ready, 1)

            def finish(n):
                r = slice(0, DEC if is_sample(n) else P)
                dve.wait_ge(y_root, n + 1)
                own.link(nc.vector.tensor_scalar(msq[r, :], msq[r, :], 1.0 / D, EPS, ALU.mult, ALU.add))
                newton(own, nc, msq[r, :], rs[r, :], tmp[r, :])
                own.link(nc.vector.scalar_tensor_tensor(out=y[r, :], in0=ysum[r, :], scalar=rs[r, 0:1],
                                                        in1=g2[1 if is_sample(n) else 0][r, :], op0=ALU.mult,
                                                        op1=ALU.mult))
                dve.wait_ge(x1_in, n * 16 + 16)
                nc.vector.tensor_tensor(y[r, :], y[r, :], x1[r, :], ALU.add).then_inc(y_done, 1)

            FINISH = 5
            AHEAD = 2
            PER = PH * find.PASS + FINISH

            def start():
                products(0, 0)
                weights(0, 0)
                dve.wait_ge(g2_in, 48)
                for i in range(2):
                    own.link(nc.vector.tensor_tensor(g2[i][:, :], g2[i][:, :], gpost[:, :], ALU.mult))
                assert own.n == AHEAD, own.n

            def body(n, more):
                own.base, own.n = (AHEAD if is_sample(n) else n * PER + (AHEAD - find.PASS - FINISH)), 0
                for h in range(PH):
                    un, uh = (n, h + 1) if h < PH - 1 else (n + 1, 0)
                    if h < PH - 1 or more:
                        products(un, uh)
                    if h == 0:
                        if not is_sample(n):
                            finish(n - 1)
                            find.search(own, dve, dve_passed, n, PH - 1)
                    elif more:
                        find.search(own, dve, dve_passed, n + 1, h - 1)
                    if h < PH - 1 or more:
                        weights(un, uh)
                if more:
                    assert own.n == (PER - find.PASS - FINISH if is_sample(n) else PER), own.n

            run(dve, start, body, lambda: finish(NT))

        @block.tensor
        def _(pe):
            def transposes(n):
                pe.wait_ge(h2_in, n * 16 + 32)
                for half in range(2):
                    pe.wait_ge(h2T_done, n * 2 + half)
                    for q in range(4):
                        k = 4 * half + q
                        last = nc.tensor.transpose(ps_t[:, q * P:(q + 1) * P], h2n[:, k * P:(k + 1) * P], ident)
                    last.then_inc(h2_tr, 1)
                pe.wait_ge(h2T_done, n * 2 + 2)

            def add_row(n, h, k):
                rows = DEC if is_sample(n) else P
                s = width(n) * h + k
                pe.wait_ge(v_full[k % RING], filled(n, h, k))
                pe.wait_ge(diag_ready, slots(n, h) + (k + 1))
                for half in range(2):
                    c = slice(512 * half, 512 * (half + 1))
                    last = nc.tensor.matmul(ps_y[0:rows, c], diag[s % DIAGS][:, 0:rows], vrow[k % RING][:, c],
                                            start=(s == 0), stop=(s == PH * width(n) - 1))
                last.then_inc(v_used, 1)

            def body(n, more):
                for h in range(PH):
                    if more:
                        if h == 0:
                            transposes(n + 1)
                        find.queries(pe, n + 1, h)
                    if h == 0 and not is_sample(n):
                        pe.wait_ge(y_free, n)
                    for k in range(width(n)):
                        add_row(n, h, k)
                        if k == width(n) // 2 - 1 and more:
                            find.scores(pe, n + 1, h)

            run(pe, lambda: None, body, lambda: None)


def constants():
    import numpy as np

    c = np.zeros((P, C_END), np.float32)
    i = np.arange(P)
    c[:, C_ID:C_ID + P] = np.eye(P)
    c[:, C_NTRI:C_NTRI + P] = -(i[:, None] >= i[None, :]).astype(np.float32)
    c[:, C_NONES:C_NONES + P] = -1.0
    c[:, C_MASK:C_MASK + P] = i[:, None] < i[None, :]
    c[:, C_IOTA:C_IOTA + TOPK] = np.arange(TOPK)
    c[:, C_FOLD:C_FOLD + DEC] = i[:, None] % DEC == np.arange(DEC)[None, :]
    c[:, C_EPS] = EPS
    for g, w in enumerate(WINDOWS):
        c[:, C_INVC + 16 * g:C_INVC + 16 * (g + 1)] = 1.0 / np.minimum(np.arange(16) + 1, w)
    return c


_OUTS = [("y_p", (SEQ, D)), ("y_s", (DEC, D)), ("k_p", (SEQ, DA)), ("v_p", (SEQ, DA)), ("pool_p", (HIST, DPOOL)),
         ("k_s", (DEC, DA)), ("v_s", (DEC, DA)), ("pool_s", (HIST, DPOOL))]


def kernel(x_prompt, x_sample, cache_k, cache_v, state_pool, c_prompt, c_sample, w_ada, b_ada, g_pre1, g_post1,
           g_pre2, g_post2, w_in, g_out_a, g_out_b, w_pool, pool_scale, w_out, w_query, sub_keys, u_experts, v_experts):
    import numpy as np
    import concourse.bacc as bacc
    from concourse.bass_utils import run_bass_kernel_spmd

    a = lambda v: np.ascontiguousarray(np.asarray(v))
    col = lambda v: np.asarray(v).reshape(-1, P).T
    ins = {
        "x_p": a(x_prompt)[0], "x_s": a(x_sample)[0],
        "cT": a(np.stack([np.asarray(c_prompt)[0], np.asarray(c_sample)[0]]).reshape(2, KC, P).transpose(2, 1, 0)
                .reshape(P, 2 * KC)),
        "w_ada": a(w_ada)[0], "b_ada": a(b_ada),
        "gains": a(np.concatenate([col(g_pre1), col(g_out_a), col(g_out_b), col(pool_scale)], axis=1)),
        "rows": a(np.concatenate([np.asarray(g_post1), np.asarray(g_pre2), np.asarray(g_post2)])),
        "w_in": a(w_in)[0], "w_pool": a(w_pool)[0], "w_out": a(w_out)[0], "w_query": a(w_query)[0],
        "keysT": a(np.asarray(sub_keys)[0].transpose(3, 1, 0, 2).reshape(P, 2 * PH, NKEY)),
        "kpastT": a(np.asarray(cache_k)[0, 0].reshape(PAST, DA).T), "vpast": a(cache_v)[0, 0].reshape(PAST, DA),
        "histT": a(np.asarray(state_pool)[0, 0].reshape(HIST, FA, P).transpose(2, 1, 0)),
        "u_tab": a(u_experts)[0], "v_tab": a(v_experts)[0],
        "const": constants(),
    }
    nc = bacc.Bacc("TRN2", target_bir_lowering=False, num_devices=1)
    A, arrays = {}, {}
    for name, v in ins.items():
        arrays[f"in_{name}"] = np.ascontiguousarray(v)
        A[name] = nc.dram_tensor(f"in_{name}", v.shape, mybir.dt.from_np(v.dtype), kind="ExternalInput").ap()
    for name, shape in _OUTS:
        A[name] = nc.dram_tensor(f"out_{name}", shape, F32, kind="ExternalOutput").ap()
    build(nc, A)
    r = run_bass_kernel_spmd(nc, [arrays], core_ids=[0]).results[0]
    y_p, y_s, k_p, v_p, pool_p, k_s, v_s, pool_s = (r[f"out_{name}"] for name, _ in _OUTS)
    kv = lambda t, n: t.reshape(1, 1, n, DA // HD, HD)
    return (y_p[None], y_s[None], kv(k_p, SEQ), kv(v_p, SEQ), pool_p[None, None], kv(k_s, DEC), kv(v_s, DEC),
            pool_s[None, None])
```
